# Optimizing a Trainium2 kernel written in Bass

```python
import math
import jax, jax.numpy as jnp
from jax import lax
import numpy as np

D_MODEL = 1024
BATCH = 1
SEQ = 512
DEPTH = 1

CHUNK = 64
MIX_WIDTH = D_MODEL
ATTN_WIDTH = MIX_WIDTH // 2
ATTN_HEAD_DIM = 64
ATTN_HEADS = ATTN_WIDTH // ATTN_HEAD_DIM
ATTN_KV_HEADS = max(1, ATTN_HEADS // 4)
ATTN_GROUP = ATTN_HEADS // ATTN_KV_HEADS
WINDOW = 128
WIN_CHUNKS = WINDOW // CHUNK
DN_WIDTH = MIX_WIDTH - ATTN_WIDTH
DN_HEAD_DIM = 128
DN_HEADS = DN_WIDTH // DN_HEAD_DIM
DN_CONV_WIDTH = 4
N_EXPERTS = 32
TOP_K = 4
D_FF = D_MODEL
SWIGLU_LIMIT = 7.0
SWIGLU_ALPHA = 1.702
MOE_BLOCK = 128
NORM_EPS = 1e-6

IN_SIZES = (ATTN_HEADS * ATTN_HEAD_DIM, ATTN_KV_HEADS * ATTN_HEAD_DIM, ATTN_KV_HEADS * ATTN_HEAD_DIM,
            DN_WIDTH, DN_WIDTH, DN_WIDTH, DN_WIDTH, DN_HEADS, DN_HEADS)
IN_WIDTH = sum(IN_SIZES)
IN_SPLITS = tuple(int(s) for s in np.cumsum(IN_SIZES)[:-1])

kernel_name = "hybrid_swa_sink_gdn_moe_block"

def rms_norm(x, w):
    xf = x.astype(jnp.float32)
    y = xf * lax.rsqrt(jnp.mean(xf * xf, axis=-1, keepdims=True) + NORM_EPS)
    return (y * w.astype(jnp.float32)).astype(x.dtype)

def l2_norm(x):
    return x * lax.rsqrt(jnp.sum(x * x, axis=-1, keepdims=True) + NORM_EPS)

def swa_sink_attention(q, k, v, sinks):
    Bsz, S = q.shape[0], q.shape[1]
    nc = S // CHUNK
    qc = q.reshape(Bsz, nc, CHUNK, ATTN_KV_HEADS, ATTN_GROUP, ATTN_HEAD_DIM)
    kc = k.reshape(Bsz, nc, CHUNK, ATTN_KV_HEADS, ATTN_HEAD_DIM)
    vc = v.reshape(Bsz, nc, CHUNK, ATTN_KV_HEADS, ATTN_HEAD_DIM)

    def band(t):
        parts = [jnp.pad(t, ((0, 0), (j, 0), (0, 0), (0, 0), (0, 0)))[:, :nc]
                 for j in range(WIN_CHUNKS - 1, -1, -1)]
        return jnp.concatenate(parts, axis=2)

    kb, vb = band(kc), band(vc)
    shift = jnp.repeat(jnp.arange(WIN_CHUNKS - 1, -1, -1), CHUNK)
    valid = jnp.arange(nc)[:, None] >= shift[None, :]
    s = jnp.einsum('bnqhgd,bnkhd->bnhgqk', qc, kb).astype(jnp.float32) * (ATTN_HEAD_DIM ** -0.5)
    s = jnp.where(valid[None, :, None, None, None, :], s, -jnp.inf)
    sink = jnp.broadcast_to(
        sinks.astype(jnp.float32).reshape(ATTN_KV_HEADS, ATTN_GROUP)[None, None, :, :, None, None],
        s.shape[:-1] + (1,))
    p = jax.nn.softmax(jnp.concatenate([s, sink], axis=-1), axis=-1)[..., :-1]
    o = jnp.einsum('bnhgqk,bnkhd->bnqhgd', p.astype(v.dtype), vb)
    return o.reshape(Bsz, S, ATTN_HEADS * ATTN_HEAD_DIM)

def causal_depthwise_conv(x, w):
    return lax.conv_general_dilated(
        x, w[:, None, :].astype(x.dtype), window_strides=(1,),
        padding=[(DN_CONV_WIDTH - 1, 0)], dimension_numbers=('NWC', 'WIO', 'NWC'),
        feature_group_count=x.shape[-1])

def chunked_gated_delta_rule(q, k, v, g, beta):
    Bsz, S, H, Dk = q.shape
    Dv = v.shape[-1]
    nc = S // CHUNK

    def chunks(t):
        return jnp.moveaxis(t.reshape((Bsz, nc, CHUNK, H) + t.shape[3:]), 3, 1)

    q = chunks(q) * (Dk ** -0.5)
    k = chunks(k)
    v = chunks(v)
    beta = chunks(beta)
    g = jnp.cumsum(chunks(g), axis=-1)
    tri = jnp.tril(jnp.ones((CHUNK, CHUNK), dtype=bool))
    tri_strict = jnp.tril(jnp.ones((CHUNK, CHUNK), dtype=bool), -1)
    decay = jnp.exp(jnp.where(tri, g[..., :, None] - g[..., None, :], -jnp.inf))
    k_beta = k * beta[..., None]
    lower = jnp.where(tri_strict, jnp.einsum('bhncd,bhnsd->bhncs', k_beta, k) * decay, 0.0)
    eye = jnp.eye(CHUNK, dtype=jnp.float32)
    rhs = jnp.concatenate([v * beta[..., None], k_beta * jnp.exp(g)[..., None]], axis=-1)
    sol = lax.linalg.triangular_solve(lower + eye, rhs, left_side=True, lower=True,
                                      unit_diagonal=True)
    u, w = sol[..., :Dv], sol[..., Dv:]
    intra = jnp.where(tri, jnp.einsum('bhncd,bhnsd->bhncs', q, k) * decay, 0.0)
    q_decayed = q * jnp.exp(g)[..., None]
    g_last = g[..., -1]
    k_to_end = k * jnp.exp(g_last[..., None] - g)[..., None]

    def step(state, xs):
        q_c, k_c, u_c, w_c, intra_c, gl_c = xs
        v_new = u_c - jnp.einsum('bhck,bhkv->bhcv', w_c, state)
        o_c = (jnp.einsum('bhck,bhkv->bhcv', q_c, state)
               + jnp.einsum('bhcs,bhsv->bhcv', intra_c, v_new))
        state = state * jnp.exp(gl_c)[..., None, None] + jnp.einsum('bhck,bhcv->bhkv', k_c, v_new)
        return state, o_c

    xs = tuple(jnp.moveaxis(t, 2, 0) for t in (q_decayed, k_to_end, u, w, intra, g_last))
    state0 = jnp.zeros((Bsz, H, Dk, Dv), jnp.float32)
    _, o = lax.scan(step, state0, xs)
    return jnp.transpose(o, (1, 0, 3, 2, 4)).reshape(Bsz, S, H, Dv)

def gated_deltanet(dq, dk, dv, dz, db, da, conv_w, a_log, dt_bias, out_norm_w):
    Bsz, S = dq.shape[0], dq.shape[1]
    qkv = jax.nn.silu(causal_depthwise_conv(jnp.concatenate([dq, dk, dv], axis=-1), conv_w))
    q, k, v = jnp.split(qkv.astype(jnp.float32), 3, axis=-1)
    hs = (Bsz, S, DN_HEADS, DN_HEAD_DIM)
    q = l2_norm(q.reshape(hs))
    k = l2_norm(k.reshape(hs))
    v = v.reshape(hs)
    beta = jax.nn.sigmoid(db.astype(jnp.float32))
    g = -jnp.exp(a_log.astype(jnp.float32)) * jax.nn.softplus(
        da.astype(jnp.float32) + dt_bias.astype(jnp.float32))
    o = chunked_gated_delta_rule(q, k, v, g, beta)
    o = rms_norm(o, out_norm_w) * jax.nn.silu(dz.astype(jnp.float32).reshape(hs))
    return o.reshape(Bsz, S, DN_WIDTH).astype(dq.dtype)

def clamped_swiglu_expert(xb, w_gu, b_gu, w_down, b_down):
    gu = xb @ w_gu + b_gu
    gate = jnp.minimum(gu[:, :D_FF], SWIGLU_LIMIT)
    up = jnp.clip(gu[:, D_FF:], -SWIGLU_LIMIT, SWIGLU_LIMIT)
    act = (up + 1.0) * (gate * jax.nn.sigmoid(gate * SWIGLU_ALPHA))
    return act @ w_down + b_down

def moe_ffn(h, router_w, router_b, w_gu, b_gu, w_down, b_down):
    Bsz, S, D = h.shape
    T = Bsz * S
    P = T * TOP_K
    ht = h.reshape(T, D)
    logits = (ht @ router_w).astype(jnp.float32) + router_b.astype(jnp.float32)
    top_val, top_idx = lax.top_k(logits, TOP_K)
    gates = jax.nn.softmax(top_val, axis=-1)
    pair_expert = top_idx.reshape(P).astype(jnp.int32)
    pair_token = jnp.arange(P, dtype=jnp.int32) // TOP_K
    pair_gate = gates.reshape(P)
    order = jnp.argsort(pair_expert)
    sorted_expert = pair_expert[order]
    counts = jnp.bincount(pair_expert, length=N_EXPERTS)
    padded = (counts + MOE_BLOCK - 1) // MOE_BLOCK * MOE_BLOCK
    start = jnp.cumsum(counts) - counts
    pstart = jnp.cumsum(padded) - padded
    dest = pstart[sorted_expert] + jnp.arange(P, dtype=jnp.int32) - start[sorted_expert]
    n_rows = P + N_EXPERTS * MOE_BLOCK
    n_blocks = n_rows // MOE_BLOCK
    row_token = jnp.zeros((n_rows,), jnp.int32).at[dest].set(pair_token[order])
    row_gate = jnp.zeros((n_rows,), jnp.float32).at[dest].set(pair_gate[order])
    block_expert = jnp.minimum(
        jnp.searchsorted(jnp.cumsum(padded), jnp.arange(n_blocks) * MOE_BLOCK, side='right'),
        N_EXPERTS - 1).astype(jnp.int32)
    xb = ht[row_token].reshape(n_blocks, MOE_BLOCK, D)

    def run_block(args):
        xb_i, e = args
        return clamped_swiglu_expert(xb_i, w_gu[e], b_gu[e], w_down[e], b_down[e])

    yb = lax.map(run_block, (xb, block_expert)).reshape(n_rows, D)
    y = jnp.zeros((T, D), jnp.float32).at[row_token].add(yb.astype(jnp.float32) * row_gate[:, None])
    return y.reshape(Bsz, S, D).astype(h.dtype)

def setup_inputs(seed: int = 0) -> dict:
    key = jax.random.key(seed)
    ks = jax.random.split(key, 18)
    f32 = jnp.float32
    L = DEPTH
    nrm = lambda k, s: jax.random.normal(k, s, f32)
    x = nrm(ks[0], (BATCH, SEQ, D_MODEL))
    norm_mix_w = 1.0 + 0.02 * nrm(ks[1], (L, D_MODEL))
    w_in = nrm(ks[2], (L, D_MODEL, IN_WIDTH)) * D_MODEL ** -0.5
    attn_q_norm_w = 1.0 + 0.02 * nrm(ks[3], (L, ATTN_HEAD_DIM))
    attn_k_norm_w = 1.0 + 0.02 * nrm(ks[4], (L, ATTN_HEAD_DIM))
    attn_sinks = 0.5 * nrm(ks[5], (L, ATTN_HEADS))
    dn_conv_w = nrm(ks[6], (L, DN_CONV_WIDTH, 3 * DN_WIDTH)) * DN_CONV_WIDTH ** -0.5
    dn_a_log = jnp.log(jax.random.uniform(ks[7], (L, DN_HEADS), f32, 1.0, 16.0))
    dt = jnp.exp(jax.random.uniform(ks[8], (L, DN_HEADS), f32, math.log(1e-3), math.log(1e-1)))
    dn_dt_bias = dt + jnp.log(-jnp.expm1(-dt))
    dn_out_norm_w = 1.0 + 0.02 * nrm(ks[9], (L, DN_HEAD_DIM))
    w_out = nrm(ks[10], (L, MIX_WIDTH, D_MODEL)) * MIX_WIDTH ** -0.5
    norm_ffn_w = 1.0 + 0.02 * nrm(ks[11], (L, D_MODEL))
    router_w = nrm(ks[12], (L, D_MODEL, N_EXPERTS)) * D_MODEL ** -0.5
    router_b = 0.01 * nrm(ks[13], (L, N_EXPERTS))
    expert_w_gate_up = nrm(ks[14], (L, N_EXPERTS, D_MODEL, 2 * D_FF)) * D_MODEL ** -0.5
    expert_b_gate_up = 0.01 * nrm(ks[15], (L, N_EXPERTS, 2 * D_FF))
    expert_w_down = nrm(ks[16], (L, N_EXPERTS, D_FF, D_MODEL)) * D_FF ** -0.5
    expert_b_down = 0.01 * nrm(ks[17], (L, N_EXPERTS, D_MODEL))
    return {"x": x, "norm_mix_w": norm_mix_w, "w_in": w_in, "attn_q_norm_w": attn_q_norm_w,
            "attn_k_norm_w": attn_k_norm_w, "attn_sinks": attn_sinks, "dn_conv_w": dn_conv_w,
            "dn_a_log": dn_a_log, "dn_dt_bias": dn_dt_bias, "dn_out_norm_w": dn_out_norm_w,
            "w_out": w_out, "norm_ffn_w": norm_ffn_w, "router_w": router_w, "router_b": router_b,
            "expert_w_gate_up": expert_w_gate_up, "expert_b_gate_up": expert_b_gate_up,
            "expert_w_down": expert_w_down, "expert_b_down": expert_b_down}

def reference(x, norm_mix_w, w_in, attn_q_norm_w, attn_k_norm_w, attn_sinks, dn_conv_w,
              dn_a_log, dn_dt_bias, dn_out_norm_w, w_out, norm_ffn_w, router_w, router_b,
              expert_w_gate_up, expert_b_gate_up, expert_w_down, expert_b_down):
    Bsz, S, _ = x.shape
    h = x
    for l in range(DEPTH):
        u = rms_norm(h, norm_mix_w[l])
        proj = u @ w_in[l]
        aq, ak, av, dq, dk, dv, dz, db, da = jnp.split(proj, IN_SPLITS, axis=-1)
        aq = rms_norm(aq.reshape(Bsz, S, ATTN_HEADS, ATTN_HEAD_DIM), attn_q_norm_w[l])
        ak = rms_norm(ak.reshape(Bsz, S, ATTN_KV_HEADS, ATTN_HEAD_DIM), attn_k_norm_w[l])
        av = av.reshape(Bsz, S, ATTN_KV_HEADS, ATTN_HEAD_DIM)
        attn_out = swa_sink_attention(aq, ak, av, attn_sinks[l])
        dn_out = gated_deltanet(dq, dk, dv, dz, db, da, dn_conv_w[l], dn_a_log[l],
                                dn_dt_bias[l], dn_out_norm_w[l])
        h = h + jnp.concatenate([attn_out, dn_out], axis=-1) @ w_out[l]
        h = h + moe_ffn(rms_norm(h, norm_ffn_w[l]), router_w[l], router_b[l],
                        expert_w_gate_up[l], expert_b_gate_up[l],
                        expert_w_down[l], expert_b_down[l])
    return h


_drawn_inputs = setup_inputs


def setup_inputs(seed=0):
    import zlib

    import numpy as np

    out = dict(_drawn_inputs(seed))
    spreads = {}
    factors = {'attn_q_norm_w': 5.147,
     'attn_k_norm_w': 6.252,
     'attn_sinks': 8.0,
     'expert_b_gate_up': 8.0,
     'expert_b_down': 8.0,
     'dn_out_norm_w': 2.697,
     'router_b': 3.101}
    for name, (base, spread) in spreads.items():
        noise = np.random.default_rng([zlib.crc32(name.encode()), seed]).standard_normal(out[name].shape)
        drawn = base * np.exp(spread * noise) if base else spread * noise
        out[name] = __import__('jax').numpy.asarray(drawn.astype(out[name].dtype))
    for name, factor in factors.items():
        out[name] = (out[name] * factor).astype(out[name].dtype)
    return out
```

```python
from contextlib import ExitStack

import numpy as np

import concourse.bass as bass
from concourse import mybir
from concourse.alu_op_type import AluOpType as ALU

ACT = mybir.ActivationFunctionType
AX = mybir.AxisListType
F32 = mybir.dt.float32
I32 = mybir.dt.int32
U32 = mybir.dt.uint32

P = 128
D = 1024
S = 512
NT = S // P
KD = D // P
HA, DH, KV = 8, 64, 2
HP = HA // KV
CH = 64
NCH = S // CH
HD = 4
NE, TOPK = 32, 4
FF = 1024
EPS = 1e-6
BT = 32
MAXB = S * TOPK // BT + NE
QW = 256
LIMIT, ALPHA = 7.0, 1.702

SLABS = [(0, 256), (256, 256), (512, 256), (2304, 260), (2564, 260)] + [(768 + 256 * i, 256) for i in range(6)]
SLABW = 260
NSL = 3
TOKU = 5 * NT
CHU = 12
LEVELS = [2, 4, 8, 16, 32, 64]


def hybrid_block(nc, x, norm_mix_w, w_in, qn_w, kn_w, sinks, conv_w, a_log, dt_bias, out_norm_w, w_out,
                 norm_ffn_w, router_w, router_b, w_gu, b_gu, w_dn, b_dn, out):
    ctx = ExitStack()
    with ctx:
        def sb(name, cols, dt=F32):
            return ctx.enter_context(nc.sbuf_tensor(name, [P, cols], dt))

        sems = {}

        def S_(name):
            if name not in sems:
                sems[name] = ctx.enter_context(nc.semaphore(name))
            return sems[name]

        h_d = nc.dram_tensor("h_scratch", (S, D), F32).ap()
        hn_d = nc.dram_tensor("hn_scratch", (S * 4, QW), F32).ap()
        y_d = nc.dram_tensor("y_scratch", (MAXB * BT, D), F32).ap()

        WE = [sb("W0", 24576), sb("W1", 24576)]
        W0, W1 = WE
        GUW = [w[:, 0:16384].rearrange("p (k n) -> p k n", k=KD) for w in WE]
        DNW = [w[:, 16384:24576].rearrange("p (k n) -> p k n", k=KD) for w in WE]

        ident = sb("ident", P)
        XG = sb("XG", QW)
        XT = sb("XT", 2 * P)
        GU = sb("GU", 2 * QW)
        SIG = sb("SIG", QW)
        AT = sb("AT", 2 * P)
        Y = sb("Y", QW)
        BGU = [sb("BGU0", 2 * QW), sb("BGU1", 2 * QW)]
        BDN = [sb("BDN0", QW), sb("BDN1", QW)]
        IDX = sb("IDX", MAXB + 1, U32)
        IDXC = sb("IDXC", 2, U32)
        LASTB = sb("LASTB", NE, I32)
        SLOT = sb("SLOT", 4 * TOPK, U32)
        GATE = sb("GATE", 4 * TOPK)
        SM = sb("SM", 420)

        def small(at, n):
            return SM[:, at:at + n]

        SSX, RSX = small(0, 4), small(4, 4)
        SSA, RNA = small(8, 40), small(48, 40)
        MXS, MNEG, ESK, DEN, RDEN = [small(88 + 4 * i, 4) for i in range(5)]
        SKT = small(108, 4)
        KWT = small(112, 64)
        AL, DTB = small(176, 4), small(180, 4)
        GV, SPT, SPM = small(184, 16), small(200, 16), small(216, 16)
        BETA = small(232, 16)
        GC, GLC = small(248, 16), small(264, 16)
        EG, EGD, EGL = small(280, 16), small(296, 16), small(312, 16)
        SSQ, RSQ = small(328, 32), small(360, 32)
        SSO, RSO = small(392, 16), small(392, 16)
        SSH, RSH = small(408, 4), small(412, 4)

        X = W0[:, 0:4096].rearrange("p (t n) -> p t n", t=NT)
        CV = [W0[:, 512 * i:512 * i + 512] for i in range(2)]
        SG = [W0[:, 1024 + 512 * i:1536 + 512 * i] for i in range(2)]
        ST = [W0[:, 2048 + 512 * i:2560 + 512 * i] for i in range(2)]
        SGZ = W0[:, 3072:3584]
        UT = W0[:, 4096:8192].rearrange("p (k n) -> p k n", k=KD)
        SL = [W0[:, 8192 + i * 2080:8192 + i * 2080 + 2080].rearrange("p (k n) -> p k n", k=KD) for i in range(NSL)]
        AQ = W0[:, 14432:17504].rearrange("p (t n) -> p t n", t=NT)
        QNT = W0[:, 17504:19552].rearrange("p (c h q) -> p c h q", c=NCH, h=HP)
        KNT = W0[:, 19552:20064]
        AVS = W0[:, 20064:20448].rearrange("p (i n) -> p i n", i=3)
        MSK = [W0[:, 20480 + P * i:20608 + P * i] for i in range(7)]
        TRIU = W0[:, 21376:21504]
        ONES = W0[:, 21504:21632]
        NEGM = W0[:, 21632:21760]
        STATE = W0[:, 21760:22272]
        WO1 = W0[:, 16384:20480].rearrange("p (k n) -> p k n", k=4)
        QTM, KTM, VTM = [W1[:, 2048 * i:2048 * i + 2048].rearrange("p (t h n) -> p t h n", t=NT, h=HD)
                         for i in range(3)]
        OB = W1[:, 0:2048].rearrange("p (t n) -> p t n", t=NT)
        WO0 = W1[:, 2048:6144].rearrange("p (k n) -> p k n", k=4)
        DZ = W1[:, 6144:8224].rearrange("p (t n) -> p t n", t=NT)
        CAT = W1[:, 20480:24576].rearrange("p (k n) -> p k n", k=KD)

        def slot(i):
            return W1[:, 8224 + 512 * i:8736 + 512 * i] if i < 23 else W0[:, 22272 + 512 * (i - 23):22784 + 512 * (i - 23)]

        names = ["KH", "KB", "QN", "QE", "KBEG", "KTE", "VB", "KHT", "KBT", "QET", "QNT", "DEC", "LT"]
        B = [{n: slot(2 * i + c) for i, n in enumerate(names)} for c in range(2)]
        for b in B:
            b.update(INT=b["KH"], CT=b["KB"], P1=b["QN"], USOL=b["QE"], U=b["KHT"], T=b["KBT"], WT=b["QNT"], VN=b["DEC"])
        QNB = [W1[:, 8224 + 640 * i:8864 + 640 * i] for i in range(2)]
        PB = [W1[:, 9504 + 512 * i:10016 + 512 * i] for i in range(2)]
        PT = W1[:, 10528:11040]
        SQA = W1[:, 11040:11680]
        NW = W1[:, 11680:12704]
        CWR = W1[0:48, 12704:12832]
        CW = W0[:, 23808:23856]
        ZNW = W0[:, 23856:23984]
        SQD = W0[:, 3584:4096]
        H = W1[:, 6144:10240].rearrange("p (t n) -> p t n", t=NT)
        HN = W1[:, 10240:14336].rearrange("p (t n) -> p t n", t=NT)
        HNT = W1[:, 14336:18432].rearrange("p (k n) -> p k n", k=KD)
        FW = W1[:, 18432:19456]
        RW = W1[:, 19456:19712].rearrange("p (k n) -> p k n", k=KD)
        RB = W1[:, 19712:19744]
        LG = W1[:, 19744:19872].rearrange("p (t n) -> p t n", t=NT)
        MX8 = W1[:, 19872:19904].rearrange("p (t n) -> p t n", t=NT)
        MI8 = W1[:, 19904:19936].bitcast(U32).rearrange("p (t n) -> p t n", t=NT)
        MIF = W1[:, 19936:19968].rearrange("p (t n) -> p t n", t=NT)
        RT = W1[:, 0:6144]
        OH = RT[:, 0:512].rearrange("p (t k e) -> p t k e", t=NT, k=TOPK)
        OHR = RT[:, 512:1024].rearrange("p (t k e) -> p t k e", t=NT, k=TOPK)
        MASK = RT[:, 1024:1152].rearrange("p (t e) -> p t e", t=NT)
        NBF = RT[:, 1152:1184]
        NBI = RT[:, 1184:1216].bitcast(I32)
        BEF = RT[:, 1216:1248]
        BSF = RT[:, 1248:1280]
        ONE32 = RT[:, 1280:1312]
        RK = RT[:, 1312:1328]
        RKI = RT[:, 1328:1344].bitcast(I32)
        RKB = RT[:, 1344:1360]
        BSK = RT[:, 1360:1376]
        TPOS = RT[:, 1376:1392]
        BLK = RT[:, 1392:1408]
        GSUM = RT[:, 1408:1412]
        GREC = RT[:, 1412:1416]
        PJ = RT[:, 1416:1417]
        PJI = RT[:, 1417:1418].bitcast(I32)
        TOK4 = RT[:, 1420:1424]
        IO32 = RT[:, 1424:1456]
        IOM = RT[:, 1456:1584]
        IOB = RT[:, 1584:1584 + MAXB + 1]
        RANK = RT[:, 1696:1824].rearrange("p (t e) -> p t e", t=NT)
        STRU = RT[:, 1824:1952]
        ONER = RT[:, 1952:2080]
        T1 = [RT[:, 2080 + P * i:2208 + P * i] for i in range(2)]
        B1 = [RT[:, 2336 + P * i:2336 + P * i + MAXB + 1] for i in range(2)]
        HF = W0[:, 0:4096].rearrange("p (t n) -> p t n", t=NT)
        YG = W0[:, 4096:20480].rearrange("p (i n) -> p i n", i=4 * TOPK)

        PS = [ctx.enter_context(nc.psum_tensor(f"PS{i}", [P, 512], F32))[:, :] for i in range(4)]
        PSC = ctx.enter_context(nc.psum_tensor("PSC", [P, 2, 512], F32))
        PS += [PSC[:, 0, :], PSC[:, 1, :]]
        PS += [ctx.enter_context(nc.psum_tensor(f"PS{i}", [P, 512], F32))[:, :] for i in (6, 7)]
        PA = PS[0:2]
        TA, TB, AO, XP = PS[2], PS[3], PS[6], PS[7]

        GPS, DPS, XPS, ATPS, RPS = PS[0], PS[1][:, 0:QW], PS[2][:, 0:QW], PS[3][:, 0:QW], PS[6][:, 0:P]

        def bc(v, n):
            a = v.shape[1]
            return v.rearrange("p (a o) -> p a o", o=1).to_broadcast([P, a, n])

        def bm(v, a):
            return v.rearrange("p (o n) -> p o n", o=1).to_broadcast([P, a, v.shape[1]])

        def h4(v):
            return v.rearrange("p (h n) -> p h n", h=HD)

        block = ctx.enter_context(nc.Block())

        def rep(v, n=P):
            return v.partition_broadcast(n)

        ATT_N, ATT_LAST = NCH, NCH + 2

        @block.sync
        def _(sp):
            for t in range(NT):
                sp.dma_start(X[:, t, :], x[t * P:(t + 1) * P, :]).then_inc(S_(f"x_in{t}"), 16)
                if t == 0:
                    sp.dma_start(NW, rep(norm_mix_w)).then_inc(S_("nw_in"), 16)
            for n, (c0, w) in enumerate(SLABS):
                if n >= NSL:
                    sp.wait_ge(S_("slab_used"), n - NSL + 1)
                sp.dma_start(SL[n % NSL][:, :, 0:w],
                             w_in.rearrange("(k p) n -> p k n", p=P)[:, :, c0:c0 + w]).then_inc(S_(f"slab_in{n % NSL}"), 16)
                if n == 3:
                    sp.wait_ge(S_("tok_evac"), 3 * NT)
                    for i in range(3):
                        sp.dma_start(AVS[0:64, i, :], AQ[64:P, i, 640:768]).then_inc(S_("avs_in"), 16)
                        sp.dma_start(AVS[64:P, i, :], AQ[0:64, i + 1, 640:768]).then_inc(S_("avs_in"), 16)
            sp.wait_ge(S_("tm_evac"), CHU)
            sp.wait_ge(S_("z_done"), NT)
            sp.wait_ge(S_("ssq"), 8)
            sp.wait_ge(S_("att_out"), NCH)
            for q in range(4):
                sp.dma_start(GUW[0][:, 2 * q:2 * q + 2, :],
                             w_gu[0].rearrange("(k p) n -> p k n", p=P)[:, 2 * q:2 * q + 2, :]).then_inc(S_(f"gu_in0{q}"), 16)
            wo_v = w_out[512:1024, :].rearrange("(k p) n -> p k n", p=P)
            sp.dma_start(WO1, wo_v).then_inc(S_("wo_in"), 16)
            sp.wait_ge(S_("kq_scaled"), 3 * (4) - 2)
            sp.wait_ge(S_("scaled_pool"), 4)
            for kv in range(KV):
                sp.dma_start(WO0[kv * 64:kv * 64 + 64, :, :],
                             w_out[kv * 256:kv * 256 + 256, :].rearrange("(h d) n -> d h n", h=HP)).then_inc(S_("wo_in"), 16)
            sp.wait_ge(S_("dn_out"), NT)
            for t in range(NT):
                sp.dma_start(H[:, t, :], x[t * P:(t + 1) * P, :]).then_inc(S_("res_in"), 16)
            sp.dma_start(FW, rep(norm_ffn_w)).then_inc(S_("res_in"), 16)
            sp.dma_start(RW, router_w.rearrange("(k p) n -> p k n", p=P)).then_inc(S_("res_in"), 16)
            sp.dma_start(RB, rep(router_b)).then_inc(S_("res_in"), 16)
            for t in range(NT):
                sp.wait_ge(S_("h_add"), 2 * t + 2)
                sp.dma_start(h_d[t * P:(t + 1) * P, :], H[:, t, :]).then_inc(S_("h_out"), 16)
                sp.wait_ge(S_("hn_ready"), t + 1)
                sp.dma_start(hn_d[t * 512:(t + 1) * 512, :].rearrange("(p j) n -> p (j n)", j=4), HN[:, t, :]).then_inc(S_("hn_out"), 16)
            def biases(e, p):
                sp.dma_start(BGU[p][0:P:32, :].rearrange("p (g n) -> p g n", g=2),
                             b_gu[e].rearrange("(g j n) -> j g n", g=2, j=4)).then_inc(S_(f"bias_in{p}"), 16)
                sp.dma_start(BDN[p][0:P:32, :], b_dn[e].rearrange("(j n) -> j n", j=4)).then_inc(S_(f"bias_in{p}"), 16)

            def gu_part(e, p, through=None):
                for q in range(4):
                    if through is not None:
                        sp.wait_ge(S_(f"gu_read{q}" if q < 3 else "gu_ps"), through)
                    sp.dma_start(GUW[p][:, 2 * q:2 * q + 2, :],
                                 w_gu[e].rearrange("(k p) n -> p k n", p=P)[:, 2 * q:2 * q + 2, :]).then_inc(S_(f"gu_in{p}{q}"), 16)

            def dn_part(e, p, through=None):
                for q in range(2):
                    if through is not None:
                        sp.wait_ge(S_("dn_read"), through) if q == 0 else sp.wait_ge(S_("d_ps"), through + 1)
                    sp.dma_start(DNW[p][:, 4 * q:4 * q + 4, :],
                                 w_dn[e].rearrange("(k p) n -> p k n", p=P)[:, 4 * q:4 * q + 4, :]).then_inc(S_(f"dn_in{p}{q}"), 16)

            sp.wait_ge(S_("bias_zeros"), 4)
            biases(0, 0)
            sp.wait_ge(S_("outproj"), 2 * NT)
            dn_part(0, 0)
            biases(1, 1)
            sp.wait_ge(S_("hn_out"), 16 * NT)
            sp.wait_ge(S_("h_out"), 16 * NT)
            sp.wait_ge(S_("lists_done"), 1)
            gu_part(1, 1)
            dn_part(1, 1)

            def reload(e, p):
                through = sp.value_load(LASTB[0:1, bass.ds(e - 2, 1)], min_val=0, max_val=MAXB - 1) + 1
                gu_part(e, p, through)
                dn_part(e, p, through)
                sp.wait_ge(S_("y_free"), e - 1)
                biases(e, p)

            with sp.Fori(1, NE // 2) as r:
                reload(2 * r, 0)
                reload(2 * r + 1, 1)
            through = sp.value_load(LASTB[0:1, NE - 2:NE - 1], min_val=0, max_val=MAXB - 1) + 1
            sp.wait_ge(S_("gu_ps"), through)
            for t in range(NT):
                sp.dma_start(HF[:, t, :], h_d[t * P:(t + 1) * P, :]).then_inc(S_("hf_in"), 16)
            for t in range(NT):
                sp.wait_ge(S_("summed"), t + 1)
                sp.dma_start(out[t * P:(t + 1) * P, :], HF[:, t, :]).then_inc(S_("out_done"), 16)
            sp.wait_ge(S_("out_done"), 16 * NT)

        @block.gpsimd
        def _(g):
            g.memset(AT[:, :], 0.0).then_inc(S_("zeros"), 1)
            g.memset(ident[:, :], 0.0).then_inc(S_("p_a"), 1)
            g.memset(ONES, 1.0).then_inc(S_("ones"), 1)
            for b in BGU + BDN:
                g.memset(b[:, :], 0.0).then_inc(S_("bias_zeros"), 1)
            g.memset(TRIU, 1.0).then_inc(S_("p_a"), 1)
            g.memset(NEGM, 0.0).then_inc(S_("p_a"), 1)
            g.wait_ge(S_("p_a"), 3)
            g.affine_select(out=ident[:, :], in_=ident[:, :], compare_op=ALU.not_equal, fill=1.0, base=0,
                            pattern=[[-1, P]], channel_multiplier=1).then_inc(S_("ident"), 1)
            g.affine_select(out=TRIU, in_=TRIU, compare_op=ALU.is_ge, fill=0.0, base=0,
                            pattern=[[1, P]], channel_multiplier=-1).then_inc(S_("tri"), 1)
            g.affine_select(out=NEGM, in_=NEGM, compare_op=ALU.is_ge, fill=-1e30, base=0,
                            pattern=[[1, P]], channel_multiplier=-1).then_inc(S_("tri"), 1)
            for i, s in enumerate([1] + LEVELS):
                g.memset(MSK[i], 0.0).then_inc(S_("p_b"), 1)
                g.wait_ge(S_("p_b"), 4 * i + 1)
                odd = MSK[i].rearrange("p (b two s) -> p b two s", two=2, s=s)[:, :, 1, :]
                g.memset(odd, 1.0).then_inc(S_("p_b"), 1)
                g.wait_ge(S_("p_b"), 4 * i + 2)
                g.affine_select(out=odd, in_=odd, compare_op=ALU.is_ge, fill=0.0, base=0,
                                pattern=[[-2 * s, P // (2 * s)], [0, s]], channel_multiplier=1).then_inc(S_("p_b"), 1)
                g.wait_ge(S_("p_b"), 4 * i + 3)
                g.affine_select(out=odd, in_=odd, compare_op=ALU.is_ge, fill=0.0, base=s - 1,
                                pattern=[[2 * s, P // (2 * s)], [0, s]], channel_multiplier=-1).then_inc(S_("p_b"), 1)
            for c in range(NT):
                b = B[c % 2]
                hs = slice(4 * c, 4 * c + 4)
                if c == 0:
                    g.wait_ge(S_("att_out"), NCH)
                    g.wait_ge(S_("dn_act"), 7)
                    g.wait_ge(S_("tm_evac"), CHU)
                    g.wait_ge(S_("dn_act"), 1)
                    g.wait_ge(S_("dn_vec"), 5)
                if c >= 2:
                    g.wait_ge(S_("kv_ps"), 2)
                    g.wait_ge(S_("o_ps"), 2)
                g.wait_ge(S_("kq_scaled"), 3 * (c + 1) - 2)
                g.tensor_tensor(h4(b["KTE"]), h4(b["KH"]), bc(EGD[:, hs], P), ALU.mult).then_inc(S_("p_c"), 1)
                g.tensor_tensor(h4(b["VB"]), VTM[:, c, :, :], bc(BETA[:, hs], P), ALU.mult).then_inc(S_("p_c"), 1)
                g.wait_ge(S_("kq_scaled"), 3 * (c + 1) - 1)
                g.tensor_tensor(h4(b["KBEG"]), h4(b["KB"]), bc(EG[:, hs], P), ALU.mult).then_inc(S_("p_c"), 1)
                g.wait_ge(S_("p_c"), 3 * c + 3)
                g.wait_ge(S_("kq_scaled"), 3 * (c + 1) - 0)
                g.tensor_tensor(h4(b["QE"]), h4(b["QN"]), bc(EG[:, hs], P), ALU.mult).then_inc(S_("scaled_pool"), 1)
            g.wait_ge(S_("outproj"), 2 * NT)
            g.iota(PJI, pattern=[[0, 1]], base=0, channel_multiplier=1).then_inc(S_("consts"), 1)
            g.iota(TOK4, pattern=[[512, 4]], base=0, channel_multiplier=4, allow_small_or_imprecise_dtypes=True).then_inc(S_("consts"), 1)
            g.iota(IO32, pattern=[[1, 32]], base=0, channel_multiplier=0, allow_small_or_imprecise_dtypes=True).then_inc(S_("consts"), 1)
            g.iota(IOM.rearrange("p (a b) -> p a b", a=4), pattern=[[0, 4], [1, 32]], base=0, channel_multiplier=0, allow_small_or_imprecise_dtypes=True).then_inc(S_("consts"), 1)
            g.iota(IOB, pattern=[[1, MAXB + 1]], base=0, channel_multiplier=0, allow_small_or_imprecise_dtypes=True).then_inc(S_("consts"), 1)
            g.memset(ONE32, 1.0).then_inc(S_("consts"), 1)
            g.memset(ONER, 1.0).then_inc(S_("consts"), 1)
            g.memset(STRU, 1.0).then_inc(S_("consts"), 1)
            g.wait_ge(S_("consts"), 8)
            g.affine_select(out=STRU, in_=STRU, compare_op=ALU.is_gt, fill=0.0, base=0,
                            pattern=[[1, P]], channel_multiplier=-1).then_inc(S_("consts"), 1)
            g.wait_ge(S_("lists_done"), 1)
            g.wait_ge(S_("hn_out"), 16 * NT)
            nb = g.value_load(LASTB[0:1, NE - 1:NE], min_val=NE - 1, max_val=MAXB - 1) + 1

            def gather(i):
                g.tensor_copy(IDXC[:, 0:1], IDX[:, bass.ds(i, 1)]).then_inc(S_("idx_cur"), 1)
                g.wait_ge(S_("idx_cur"), i + 1)
                g.sem_inc(S_("pool_passed"), 1)
                g.indirect_dma_start(out=XG[:, :], out_offset=None, in_=hn_d,
                                     in_offset=bass.IndirectOffsetOnAxis(ap=IDXC[:, 0:1], axis=0)).then_inc(S_("gathered"), 16)

            gather(0)
            with g.Fori(1, nb + 1) as i:
                g.wait_ge(S_("xt_ps"), i)
                g.wait_ge(S_("gathered"), i * 16)
                gather(i)
            g.wait_ge(S_("y_out"), (nb + 1) * 16)
            g.sem_inc(S_("pool_passed"), 1)
            for i in range(4 * TOPK):
                g.indirect_dma_start(out=YG[:, i, :], out_offset=None, in_=y_d,
                                     in_offset=bass.IndirectOffsetOnAxis(ap=SLOT[:, i:i + 1], axis=0)).then_inc(S_(f"yg_in{i % 4}"), 16)

        @block.scalar
        def _(a):
            a.dma_start(KWT, rep(kn_w)).then_inc(S_("par_in"), 16)
            a.dma_start(SIG[:, 0:64], rep(qn_w)).then_inc(S_("par_in"), 16)
            for half in range(2):
                a.dma_start(SKT[64 * half:64 * half + 64, :],
                            sinks.rearrange("(g two) -> two g", two=2)[half].partition_broadcast(64),
                            allow_slow_non_contiguous=True).then_inc(S_("par_in"), 16)
            a.dma_start(AL, rep(a_log)).then_inc(S_("par_in"), 16)
            a.dma_start(DTB, rep(dt_bias)).then_inc(S_("par_in"), 16)
            a.dma_start(ZNW, rep(out_norm_w)).then_inc(S_("par_in"), 16)
            a.dma_start(CWR, conv_w.rearrange("j (t c) -> (j t) c", c=P)).then_inc(S_("par_in"), 16)
            rest = (MAXB - NE) * BT // P
            a.wait_ge(S_("zeros"), 1)
            a.dma_start(y_d[NE * BT:, :].rearrange("(p r) n -> p (r n)", p=P).rearrange("p (a n) -> p a n", n=2 * P),
                        AT[:, :].rearrange("p (o n) -> p o n", o=1).to_broadcast([P, rest * D // (2 * P), 2 * P])).then_inc(S_("y_out"), 16)
            for t in range(NT):
                a.wait_ge(S_(f"x_in{t}"), 16)
                if t:
                    a.wait_ge(S_("ssx"), t)
                a.activation(W1[:, 0:D], X[:, t, :], ACT.Square, accum_out=SSX[:, t:t + 1]).then_inc(S_("ssx"), 1)
            a.wait_ge(S_("meansq"), 1)
            a.activation(RSX, SSX, ACT.Sqrt).then_inc(S_("sqrt"), 1)
            for n in range(2 * NT):
                t, half = n // 2, n % 2
                a.wait_ge(S_("ut_ps"), n + 1)
                a.activation(UT[:, 4 * half:4 * half + 4, t * P:(t + 1) * P], h4(PS[n % 2]), ACT.Copy).then_inc(S_("ut_ready"), 1)
            def tok_unit(n):
                s, t = n // NT, n % NT
                w = SLABS[s][1]
                dst = AQ[:, t, 256 * s:256 * s + 256] if s < 3 else DZ[:, t, 260 * (s - 3):260 * (s - 3) + 260]
                a.wait_ge(S_("proj_ps"), n + 1)
                a.activation(dst, PA[n % 2][:, 0:w], ACT.Copy).then_inc(S_("tok_evac"), 1)
            for n in range(12):
                tok_unit(n)
            a.wait_ge(S_("meansq"), 2)
            a.activation(RNA, SSA, ACT.Sqrt).then_inc(S_("sqrt"), 1)
            for n in range(12, TOKU):
                tok_unit(n)
            for t in range(NT):
                a.wait_ge(S_("qk_ps"), t + 1)
                a.activation(QNT[:, 2 * t:2 * t + 2, :, :].rearrange("p c h q -> p h c q"),
                             TA.rearrange("p (h c q) -> p h c q", h=4, c=2), ACT.Copy)
                a.activation(KNT[:, t * P:(t + 1) * P], TB[:, 0:P], ACT.Copy).then_inc(S_("kt_ready"), 1)
            a.activation(BETA.rearrange("p (t h) -> p t h", t=NT), DZ[:, :, 512:516], ACT.Sigmoid).then_inc(S_("dn_act"), 1)
            for t in range(NT):
                if t:
                    a.wait_ge(S_("z_done"), t)
                a.activation(SGZ, DZ[:, t, 0:512], ACT.Sigmoid).then_inc(S_("z_sig"), 1)
            for i in range(CHU + 2):
                if i < CHU:
                    a.wait_ge(S_("conv"), 4 * i + 4)
                    if i >= 2:
                        a.wait_ge(S_("silu"), i - 1)
                    a.activation(SG[i % 2], CV[i % 2], ACT.Sigmoid).then_inc(S_("sig"), 1)
                if i < NCH:
                    a.wait_ge(S_("shifted"), i + 1)
                    w = P if i else CH
                    pv = PB[i % 2].rearrange("p (g n) -> p g n", g=4)[:, :, 0:w]
                    a.activation(pv, pv, ACT.Exp).then_inc(S_("exps_done"), 1)
                    a.activation(ESK, MNEG, ACT.Exp).then_inc(S_("exps_done"), 1)
                if 1 <= i <= NCH:
                    n = i - 1
                    k = P if n else CH
                    a.wait_ge(S_("pt_ps"), n + 1)
                    if n:
                        a.wait_ge(S_("pv_ps"), n)
                    a.activation(PT[0:k, :], TA[0:k, :], ACT.Copy).then_inc(S_("pt_ready"), 1)
                if 2 <= i:
                    u = i - 2
                    sub, hd = u // 4, u % 4
                    a.wait_ge(S_("st_ps"), u + 1)
                    dst = [QTM, KTM, VTM][sub][:, :, hd, :]
                    a.activation(dst, h4(XP), ACT.Copy).then_inc(S_("tm_evac"), 1)
                if 2 <= i < NCH + 2:
                    n = i - 2
                    a.wait_ge(S_("pv_ps"), n + 1)
                    a.activation(CAT[:, 0:4, n * CH:(n + 1) * CH], AO[:, 0:256].rearrange("p (h q) -> p h q", h=4), ACT.Copy).then_inc(S_("att_out"), 1)
            for n in range(8):
                c, sub = n // 2, n % 2
                a.wait_ge(S_("tm_evac"), CHU)
                if n:
                    a.wait_ge(S_("ssq"), n)
                a.activation(h4(SQD), [QTM, KTM][sub][:, c, :, :], ACT.Square).then_inc(S_("sq_done"), 1)
            a.wait_ge(S_("meansq"), 3)
            a.activation(RSQ, SSQ, ACT.Sqrt).then_inc(S_("sqrt"), 1)
            a.wait_ge(S_("dn_vec"), 1)
            a.activation(SPM, SPM, ACT.Exp).then_inc(S_("dn_act"), 1)
            a.activation(AL, AL, ACT.Exp).then_inc(S_("dn_act"), 1)
            a.wait_ge(S_("dn_vec"), 2)
            a.activation(SPM, SPM, ACT.Ln).then_inc(S_("dn_act"), 1)
            a.wait_ge(S_("dn_vec"), 5)
            a.activation(EG, GC, ACT.Exp).then_inc(S_("dn_act"), 1)
            a.activation(EGD, EGD, ACT.Exp).then_inc(S_("dn_act"), 1)
            a.activation(EGL, GLC, ACT.Exp).then_inc(S_("dn_act"), 1)
            for pair in range(2):
                for c in (2 * pair, 2 * pair + 1):
                    b = B[c % 2]
                    a.wait_ge(S_("dsub"), c + 1)
                    a.activation(b["DEC"], b["DEC"], ACT.Exp).then_inc(S_("decay"), 1)
                    for i, n in enumerate(("KHT", "KBT", "QNT", "QET")):
                        a.wait_ge(S_("dt_ps"), 4 * c + i + 1)
                        a.activation(b[n], PS[2 + (4 * c + i) % 2], ACT.Copy).then_inc(S_("dt_ready"), 1)
                for c in (2 * pair, 2 * pair + 1):
                    a.wait_ge(S_("t0_ps"), c + 1)
                    a.activation(B[c % 2]["T"], PS[4 + c % 2], ACT.Copy).then_inc(S_("t_ready"), 1)
                for lv in range(len(LEVELS)):
                    for c in (2 * pair, 2 * pair + 1):
                        n = (pair * len(LEVELS) + lv) * 2 + c % 2
                        a.wait_ge(S_("p1_ps"), n + 1)
                        a.activation(B[c % 2]["P1"], PS[4 + c % 2], ACT.Copy).then_inc(S_("p1_ready"), 1)
                for c in (2 * pair, 2 * pair + 1):
                    a.wait_ge(S_("uw_ps"), 2 * c + 1)
                    a.activation(B[c % 2]["USOL"], PS[2], ACT.Copy).then_inc(S_("uw"), 1)
                    a.wait_ge(S_("uw_ps"), 2 * c + 2)
                    a.activation(B[c % 2]["WT"], PS[3], ACT.Copy).then_inc(S_("uw"), 1)
                    a.wait_ge(S_("o_ps"), c + 1)
                    a.activation(OB[:, c, :], PS[6], ACT.Copy).then_inc(S_("o_evac"), 1)
            for c in range(NT):
                a.wait_ge(S_("o_evac"), NT)
                if c:
                    a.wait_ge(S_("ssq"), 8 + c)
                a.activation(B[0]["LT"], OB[:, c, :], ACT.Square).then_inc(S_("sq_done"), 1)
            a.wait_ge(S_("meansq"), 4)
            a.activation(RSO, SSO, ACT.Sqrt).then_inc(S_("sqrt"), 1)
            for c in range(NT):
                a.wait_ge(S_("dcat_ps"), c + 1)
                a.activation(CAT[:, 4:8, c * P:(c + 1) * P], h4(PS[c % 2]), ACT.Copy).then_inc(S_("dcat"), 1)
            for t in range(NT):
                a.wait_ge(S_("h_add"), 2 * t + 2)
                a.activation(HN[:, t, :], H[:, t, :], ACT.Square, accum_out=SSH[:, t:t + 1]).then_inc(S_("ssh"), 1)
                a.wait_ge(S_("meansq"), 5 + t)
                a.activation(RSH[:, t:t + 1], SSH[:, t:t + 1], ACT.Sqrt).then_inc(S_("sqrt"), 1)
                for half in range(2):
                    a.wait_ge(S_("hnt_ps"), 2 * t + half + 1)
                    a.activation(HNT[:, 4 * half:4 * half + 4, t * P:(t + 1) * P], h4(PS[2 + half]), ACT.Copy).then_inc(S_("hnt_ready"), 1)
            a.wait_ge(S_("v_gate"), NT)
            a.activation(GATE[:, :], GATE[:, :], ACT.Exp).then_inc(S_("gexp"), 1)
            a.wait_ge(S_("rank_ps"), 1)
            a.activation(RANK, PS[2][:, 0:P].rearrange("p (t e) -> p t e", t=NT), ACT.Copy).then_inc(S_("rank"), 1)
            a.wait_ge(S_("lists_done"), 1)
            last = a.value_load(LASTB[0:1, NE - 1:NE], min_val=NE - 1, max_val=MAXB - 1)
            nb = last + 1

            def xt_copy(i):
                a.activation(XT[:, :], XPS, ACT.Copy).then_inc(S_("xt_ready"), 1)

            def sigmoid(i):
                a.wait_ge(S_("gate_ready"), i + 1)
                a.wait_ge(S_("act_ready"), i) if not isinstance(i, int) or i else None
                a.activation(SIG[:, :], GU[:, 0:QW], ACT.Sigmoid, scale=ALPHA).then_inc(S_("sig_ready"), 1)

            def at_copy(i):
                a.wait_ge(S_("at_ps"), i + 1)
                a.wait_ge(S_("d_ps"), i + 1)
                a.activation(AT[:, :], ATPS, ACT.Copy).then_inc(S_("at_ready"), 1)

            def y_store(i):
                a.wait_ge(S_("y_ready"), i + 2)
                a.dma_start(y_d[bass.ds(i * BT, BT), :].rearrange("t (j n) -> j t n", j=4), Y[:, :]).then_inc(S_("y_out"), 16)

            a.wait_ge(S_("xt_ps"), 1)
            xt_copy(0)
            a.wait_ge(S_("xt_ps"), 2)
            a.wait_ge(S_("gu_ps"), 1)
            xt_copy(1)
            sigmoid(0)
            a.wait_ge(S_("y_out"), 16)
            with a.Fori(1, nb) as i:
                at_copy(i - 1)
                a.wait_ge(S_("xt_ps"), i + 2)
                a.wait_ge(S_("gu_ps"), i + 1)
                xt_copy(i + 1)
                sigmoid(i)
                y_store(i - 1)
            at_copy(last)
            y_store(last)

        @block.tensor
        def _(pe):
            def mm(o, l, r, st, sp_):
                return pe.matmul(o, l, r, start=st, stop=sp_)

            pe.wait_ge(S_("ident"), 1)
            for n in range(2 * NT):
                t, half = n // 2, n % 2
                if half == 0:
                    pe.wait_ge(S_("u_ready"), t + 1)
                if n >= 2:
                    pe.wait_ge(S_("ut_ready"), n - 1)
                for j in range(4):
                    k = 4 * half + j
                    last = pe.transpose(PS[n % 2][:, j * P:(j + 1) * P], X[:, t, k * P:(k + 1) * P], ident[:, :])
                last.then_inc(S_("ut_ps"), 1)
            pe.wait_ge(S_("par_in"), 16 * 8)
            pe.transpose(XP[:, 0:48], CWR, ident[0:48, 0:48]).then_inc(S_("cw_ps"), 1)
            pe.wait_ge(S_("ut_ready"), 2 * NT)

            def bank_free(n):
                m = n - 2
                if m < 0:
                    return
                if m < TOKU:
                    pe.wait_ge(S_("tok_evac"), m + 1)
                else:
                    pe.wait_ge(S_("conv"), 4 * (m - TOKU) + 4)

            def tok_unit(n):
                s, t = n // NT, n % NT
                w = SLABS[s][1]
                if t == 0:
                    pe.wait_ge(S_(f"slab_in{s % NSL}"), 16 * (s // NSL + 1))
                bank_free(n)
                for k in range(KD):
                    last = mm(PA[n % 2][:, 0:w], UT[:, k, t * P:(t + 1) * P], SL[s % NSL][:, k, 0:w], k == 0, k == KD - 1)
                last.then_inc(S_("proj_ps"), 1)
                if t == NT - 1:
                    pe.wait_ge(S_("cw_evac"), 1)
                    pe.transpose(XP[:, 0:48], CWR, ident[0:48, 0:48]).then_inc(S_("slab_used"), 1)

            for n in range(TOKU):
                tok_unit(n)
            for t in range(NT):
                pe.wait_ge(S_("qkn"), 3 * t + 3)
                if t:
                    pe.wait_ge(S_("kt_ready"), t)
                q = QNB[t % 2]
                for h in range(4):
                    pe.transpose(TA[:, h * P:(h + 1) * P], q[:, h * P:(h + 1) * P], ident[:, :])
                pe.transpose(TB[:, 0:P], q[:, 512:640], ident[:, :]).then_inc(S_("qk_ps"), 1)
            pe.wait_ge(S_("kt_ready"), NT)
            pe.wait_ge(S_("avs_in"), 16 * 6)
            for i in range(CHU + 2):
                if i < CHU:
                    n, s = TOKU + i, 5 + i // 2
                    if i % 2 == 0:
                        pe.wait_ge(S_(f"slab_in{s % NSL}"), 16 * (s // NSL + 1))
                    bank_free(n)
                    for k in range(KD):
                        last = mm(PA[n % 2], SL[s % NSL][:, k, (i % 2) * P:(i % 2) * P + P], UT[:, k, :], k == 0, k == KD - 1)
                    last.then_inc(S_("proj_ps"), 1)
                    if i % 2:
                        pe.transpose(TB[:, 0:P], ident[:, :], ident[:, :]).then_inc(S_("slab_used"), 1)
                if i < NCH:
                    if i:
                        pe.wait_ge(S_("shifted"), i)
                    k0, k1 = (i - 1) * CH if i else 0, (i + 1) * CH
                    for kv in range(KV):
                        rows = slice(64 * kv, 64 * kv + 64)
                        for hp in range(2):
                            last = mm(PSC[:, kv, hp * P:hp * P + k1 - k0],
                                      QNT[rows, i, 2 * hp:2 * hp + 2, :].rearrange("p h q -> p (h q)"), KNT[rows, k0:k1], True, True)
                    last.then_inc(S_("sc_ps"), 1)
                if 1 <= i <= NCH:
                    n = i - 1
                    pe.wait_ge(S_("pnorm"), n + 1)
                    if n:
                        pe.wait_ge(S_("pt_ready"), n)
                    k = P if n else CH
                    for g in range(4):
                        last = pe.transpose(TA[0:k, g * P:(g + 1) * P], PB[n % 2][:, g * P:g * P + k], ident[:, :])
                    last.then_inc(S_("pt_ps"), 1)
                if 2 <= i:
                    u = i - 2
                    pe.wait_ge(S_("silu"), u + 1)
                    if u:
                        pe.wait_ge(S_("tm_evac"), u)
                    else:
                        pe.wait_ge(S_("cw_evac"), 1)
                    for t in range(NT):
                        last = pe.transpose(XP[:, t * P:(t + 1) * P], ST[u % 2][:, t * P:(t + 1) * P], ident[:, :])
                    last.then_inc(S_("st_ps"), 1)
                if 1 <= i <= NCH:
                    n = i - 1
                    pe.wait_ge(S_("pt_ready"), n + 1)
                    if n:
                        pe.wait_ge(S_("att_out"), n)
                    k = P if n else CH
                    v = AQ[0:k, (n - 1) // 2 if n else 0, 640:768] if n % 2 or n == 0 else AVS[:, n // 2 - 1, :]
                    for kv in range(KV):
                        last = mm(AO[64 * kv:64 * kv + 64, 0:256], v[:, 64 * kv:64 * kv + 64], PT[0:k, 256 * kv:256 * kv + 256], True, True)
                    last.then_inc(S_("pv_ps"), 1)
            pe.wait_ge(S_("tri"), 2)
            pe.wait_ge(S_("ones"), 1)
            pe.wait_ge(S_("dn_vec"), 3)
            pe.wait_ge(S_("att_out"), NCH)
            mm(AO[:, 0:16], TRIU, GV, True, True)
            mm(AO[:, 16:32], ONES, GV, True, True).then_inc(S_("g_ps"), 1)
            pe.wait_ge(S_("dn_vec"), 5)
            for pair in range(2):
                cs = (2 * pair, 2 * pair + 1)
                for c in cs:
                    b = B[c % 2]
                    if c:
                        pe.wait_ge(S_("dsub"), c)
                    if c == 2:
                        pe.wait_ge(S_("state"), 2)
                        pe.wait_ge(S_("o_evac"), 2)
                    for h in range(HD):
                        last = mm(XP[:, h * P:(h + 1) * P], GV[:, 4 * c + h:4 * c + h + 1].to_broadcast([P, P]), TRIU, True, True)
                    last.then_inc(S_("grow_ps"), 1)
                    for i, (n, ready, cnt) in enumerate((("KH", "kq_scaled", 3 * c + 1), ("KB", "kq_scaled", 3 * c + 2), ("QN", "kq_scaled", 3 * c + 3), ("QE", "scaled_pool", c + 1))):
                        m = 4 * c + i
                        pe.wait_ge(S_(ready), cnt)
                        if m >= 2:
                            pe.wait_ge(S_("dt_ready"), m - 1)
                        if i < 2 and c == 2:
                            pe.wait_ge(S_("uw"), 2 * (2) - 0)
                        for h in range(HD):
                            last = pe.transpose(PS[2 + m % 2][:, h * P:(h + 1) * P], b[n][:, h * P:(h + 1) * P], ident[:, :])
                        last.then_inc(S_("dt_ps"), 1)
                    pe.wait_ge(S_("dt_ready"), 4 * c + 3)
                    if c >= 1:
                        pe.wait_ge(S_("li"), 2 * (c) - 0)
                    for h in range(HD):
                        hs = slice(h * P, (h + 1) * P)
                        last = mm(PS[0][:, hs], b["KHT"][:, hs], b["KBT"][:, hs], True, True)
                    last.then_inc(S_("li_ps"), 1)
                    for h in range(HD):
                        hs = slice(h * P, (h + 1) * P)
                        last = mm(PS[1][:, hs], b["KHT"][:, hs], b["QNT"][:, hs], True, True)
                    last.then_inc(S_("li_ps"), 1)
                for c in cs:
                    b = B[c % 2]
                    pe.wait_ge(S_("u_init"), c + 1)
                    for h in range(HD):
                        hs = slice(h * P, (h + 1) * P)
                        last = pe.transpose(PS[4 + c % 2][:, hs], b["U"][:, hs], ident[:, :])
                    last.then_inc(S_("t0_ps"), 1)
                for lv in range(len(LEVELS)):
                    for c in cs:
                        b, n = B[c % 2], (pair * len(LEVELS) + lv) * 2 + c % 2
                        pe.wait_ge(S_("ct"), n + 1)
                        if lv == 0:
                            pe.wait_ge(S_("t_ready"), c + 1)
                        else:
                            pe.wait_ge(S_("t_upd"), (pair * 5 + lv - 1) * 2 + c % 2 + 1)
                        for h in range(HD):
                            hs = slice(h * P, (h + 1) * P)
                            last = mm(PS[4 + c % 2][:, hs], b["CT"][:, hs], b["T"][:, hs], True, True)
                        last.then_inc(S_("p1_ps"), 1)
                    for c in cs:
                        b, n = B[c % 2], (pair * len(LEVELS) + lv) * 2 + c % 2
                        pe.wait_ge(S_("p1_ready"), n + 1)
                        if n:
                            pe.wait_ge(S_("u_upd"), n)
                        if lv < len(LEVELS) - 1:
                            for h in range(HD):
                                hs = slice(h * P, (h + 1) * P)
                                last = mm(PS[6][:, hs], b["U"][:, hs], b["P1"][:, hs], True, True)
                            last.then_inc(S_("p2_ps"), 1)
                        for h in range(HD):
                            hs = slice(h * P, (h + 1) * P)
                            last = mm(PS[7][:, hs], b["P1"][:, hs], b["U"][:, hs], True, True)
                        last.then_inc(S_("p2t_ps"), 1)
                for c in cs:
                    b = B[c % 2]
                    pe.wait_ge(S_("u_upd"), (pair + 1) * 12)
                    pe.wait_ge(S_("scaled_pool"), c + 1)
                    if c:
                        pe.wait_ge(S_("uw"), 2 * (c) - 0)
                    pe.wait_ge(S_("dt_ready"), 4 * c + 4)
                    for h in range(HD):
                        hs = slice(h * P, (h + 1) * P)
                        last = mm(PS[2][:, hs], b["U"][:, hs], b["VB"][:, hs], True, True)
                    last.then_inc(S_("uw_ps"), 1)
                    for h in range(HD):
                        hs = slice(h * P, (h + 1) * P)
                        last = mm(PS[3][:, hs], b["KBEG"][:, hs], b["U"][:, hs], True, True)
                    last.then_inc(S_("uw_ps"), 1)
                    if c:
                        pe.wait_ge(S_("uw"), 2 * (c + 1) - 0)
                        pe.wait_ge(S_("state"), c)
                        for h in range(HD):
                            hs = slice(h * P, (h + 1) * P)
                            last = mm(PS[7][:, hs], b["WT"][:, hs], STATE[:, hs], True, True)
                        last.then_inc(S_("ws_ps"), 1)
                    pe.wait_ge(S_("vnew"), c + 1)
                    if c:
                        pe.wait_ge(S_("o_evac"), c)
                    for h in range(HD):
                        hs = slice(h * P, (h + 1) * P)
                        if c:
                            mm(PS[6][:, hs], b["QET"][:, hs], STATE[:, hs], True, False)
                        last = mm(PS[6][:, hs], b["INT"][:, hs], b["VN"][:, hs], c == 0, True)
                    last.then_inc(S_("o_ps"), 1)
                    for h in range(HD):
                        hs = slice(h * P, (h + 1) * P)
                        last = mm(PS[5][:, hs], b["KTE"][:, hs], b["VN"][:, hs], True, True)
                    last.then_inc(S_("kv_ps"), 1)
            for c in range(NT):
                pe.wait_ge(S_("dn_out"), c + 1)
                if c >= 2:
                    pe.wait_ge(S_("dcat"), c - 1)
                for h in range(HD):
                    last = pe.transpose(PS[c % 2][:, h * P:(h + 1) * P], OB[:, c, h * P:(h + 1) * P], ident[:, :])
                last.then_inc(S_("dcat_ps"), 1)
            pe.wait_ge(S_("wo_in"), 16 * 3)
            pe.wait_ge(S_("dcat"), NT)

            def hn_transposes(t):
                pe.wait_ge(S_("hn_ready"), t + 1)
                for half in range(2):
                    if t:
                        pe.wait_ge(S_("hnt_ready"), 2 * t - 1 + half)
                    for j in range(4):
                        k = 4 * half + j
                        last = pe.transpose(PS[2 + half][:, j * P:(j + 1) * P], HN[:, t, k * P:(k + 1) * P], ident[:, :])
                    last.then_inc(S_("hnt_ps"), 1)

            def logits(t):
                pe.wait_ge(S_("hnt_ready"), 2 * t + 2)
                if t:
                    pe.wait_ge(S_("logits"), t)
                for k in range(KD):
                    last = mm(PS[5][:, 0:NE], HNT[:, k, t * P:(t + 1) * P], RW[:, k, :], k == 0, k == KD - 1)
                last.then_inc(S_("lg_ps"), 1)

            for n in range(2 * NT):
                t, half = n // 2, n % 2
                if n >= 2:
                    pe.wait_ge(S_("h_add"), n - 1)
                for k in range(KD):
                    w = WO0[:, k, :] if k < 4 else WO1[:, k - 4, :]
                    last = mm(PS[n % 2], CAT[:, k, t * P:(t + 1) * P], w[:, half * 512:half * 512 + 512], k == 0, k == KD - 1)
                last.then_inc(S_("outproj"), 1)
                if half and t:
                    hn_transposes(t - 1)
                if half == 0 and t > 1:
                    if t == 2:
                        pe.wait_ge(S_("res_in"), 16 * (NT + 3))
                    logits(t - 2)
            logits(2)
            hn_transposes(3)
            logits(3)
            pe.wait_ge(S_("mask"), NT)
            pe.wait_ge(S_("consts"), 9)
            pe.wait_ge(S_("hnt_ready"), 2 * NT)
            for t in range(NT):
                for s in range(t):
                    mm(PS[2][:, t * NE:(t + 1) * NE], ONER, MASK[:, s, :], s == 0, False)
                mm(PS[2][:, t * NE:(t + 1) * NE], STRU, MASK[:, t, :], t == 0, True)
            for s in range(NT):
                last = mm(PS[3][:, 0:NE], ONER, MASK[:, s, :], s == 0, s == NT - 1)
            last.then_inc(S_("rank_ps"), 1)
            for i in range(4 * TOPK):
                pe.wait_ge(S_("onehots"), 2 * i + 2)
                last = mm(PS[4][:, 0:MAXB + 1], T1[i % 2], B1[i % 2], i == 0, i == 4 * TOPK - 1)
                last.then_inc(S_("list_ps"), 1)
            pe.wait_ge(S_("gathered"), 16)

            def x_transposes(i):
                for half in range(2):
                    last = pe.transpose(XPS[:, half * P:(half + 1) * P], XG[:, half * P:(half + 1) * P], ident[:, :])
                last.then_inc(S_("xt_ps"), 1)

            def gate_up(i, p, rnd, first_of_expert, first):
                pe.wait_ge(S_("xt_ready"), i + 1)
                if not first:
                    pe.wait_ge(S_("gu_evac"), i)
                for k in range(KD):
                    if first_of_expert and k % 2 == 0:
                        pe.wait_ge(S_(f"gu_in{p}{k // 2}"), rnd)
                    if k == 5:
                        pe.wait_ge(S_("gathered"), (i + 2) * 16)
                        x_transposes(i + 1)
                        if not first:
                            pe.wait_ge(S_("act_ready"), i)
                            act_transposes()
                    for j in range(4):
                        rhs = GUW[p][:, k, :].rearrange("p (g n) -> p g n", g=2)[:, :, j * QW:(j + 1) * QW]
                        last = pe.matmul(GPS[32 * j:32 * j + 32, :].rearrange("p (g n) -> p g n", g=2),
                                         XT[:, (k % 2) * P + (k // 2) * 32:(k % 2) * P + (k // 2) * 32 + 32], rhs,
                                         start=(k == 0), stop=(k == KD - 1), tile_position=(0, 32 * j), skip_group_check=True)
                    if k % 2:
                        last.then_inc(S_(f"gu_read{k // 2}" if k < KD - 1 else "gu_ps"), 1)

            def act_transposes():
                for half in range(2):
                    last = pe.transpose(ATPS[:, half * P:(half + 1) * P], GU[:, half * P:(half + 1) * P], ident[:, :])
                last.then_inc(S_("at_ps"), 1)

            def down(i, p, rnd):
                pe.wait_ge(S_("at_ready"), i + 1)
                pe.wait_ge(S_("y_ready"), i + 1)
                if rnd is not None:
                    pe.wait_ge(S_(f"dn_in{p}0"), rnd)
                    pe.wait_ge(S_(f"dn_in{p}1"), rnd)
                for k in range(KD):
                    for j in range(4):
                        last = pe.matmul(DPS[32 * j:32 * j + 32, :],
                                         AT[:, (k % 2) * P + (k // 2) * 32:(k % 2) * P + (k // 2) * 32 + 32],
                                         DNW[p][:, k, j * QW:(j + 1) * QW],
                                         start=(k == 0), stop=(k == KD - 1), tile_position=(0, 32 * j), skip_group_check=True)
                    if k == KD // 2 - 1:
                        last.then_inc(S_("dn_read"), 1)
                last.then_inc(S_("d_ps"), 1)

            def more_blocks(e, p, before, rnd):
                last = pe.value_load(LASTB[0:1, bass.ds(e, 1)], min_val=0, max_val=MAXB - 1)
                with pe.If(last > before + 1):
                    with pe.Fori(before + 2, last + 1) as i:
                        gate_up(i, p, rnd, False, False)
                        down(i - 1, p, rnd)
                return last

            def expert(e, p, before, rnd, prnd):
                gate_up(before + 1, p, rnd, True, False)
                down(before, 1 - p, prnd)
                return more_blocks(e, p, before, rnd)

            pe.transpose(RPS, ident[:, :], ident[:, :]).then_inc(S_("d_ps"), 1)
            x_transposes(0)
            gate_up(0, 0, 16, True, True)
            last = pe.value_load(LASTB[0:1, 0:1], min_val=0, max_val=MAXB - 1)
            with pe.If(last > 0):
                gate_up(1, 0, 16, False, False)
                down(0, 0, 16)
            with pe.If(last > 1):
                with pe.Fori(2, last + 1) as i:
                    gate_up(i, 0, 16, False, False)
                    down(i - 1, 0, 16)

            with pe.Fori(0, NE // 2 - 1) as r:
                last = pe.value_load(LASTB[0:1, bass.ds(2 * r, 1)], min_val=0, max_val=MAXB - 1)
                last = expert(2 * r + 1, 1, last, (r + 1) * 16, (r + 1) * 16)
                expert(2 * r + 2, 0, last, (r + 2) * 16, (r + 1) * 16)
            last = pe.value_load(LASTB[0:1, NE - 2:NE - 1], min_val=0, max_val=MAXB - 1)
            last = expert(NE - 1, 1, last, NE * 8, NE * 8)
            pe.wait_ge(S_("act_ready"), last + 1)
            act_transposes()
            down(last, 1, NE * 8)

        @block.vector
        def _(v):
            stt, tt, ts = v.scalar_tensor_tensor, v.tensor_tensor, v.tensor_scalar
            chain = [0]

            def link(ins):
                chain[0] += 1
                ins.then_inc(S_("v_chain"), 1)
                v.wait_ge(S_("v_chain"), chain[0])

            v.wait_ge(S_("ssx"), NT)
            ts(SSX, SSX, 1.0 / D, EPS, ALU.mult, ALU.add).then_inc(S_("meansq"), 1)
            v.wait_ge(S_("sqrt"), 1)
            link(v.reciprocal(RSX, RSX))
            v.wait_ge(S_("nw_in"), 16)
            for t in range(NT):
                stt(out=X[:, t, :], in0=X[:, t, :], scalar=RSX[:, t:t + 1], in1=NW, op0=ALU.mult, op1=ALU.mult).then_inc(S_("u_ready"), 1)
            v.wait_ge(S_("cw_ps"), 1)
            v.tensor_copy(CW, XP[:, 0:48]).then_inc(S_("cw_evac"), 1)
            v.wait_ge(S_("par_in"), 16 * 8)
            link(stt(out=KWT, in0=KWT, scalar=DH ** -0.5, in1=SIG[:, 0:64], op0=ALU.mult, op1=ALU.mult))
            for t in range(NT):
                v.wait_ge(S_("tok_evac"), 2 * NT + t + 1)
                link(tt(SQA, AQ[:, t, 0:640], AQ[:, t, 0:640], ALU.mult))
                link(v.tensor_reduce(SSA[:, 10 * t:10 * t + 10], SQA.rearrange("p (h n) -> p h n", h=10), AX.X, ALU.add))
            ts(SSA, SSA, 1.0 / DH, EPS, ALU.mult, ALU.add).then_inc(S_("meansq"), 1)
            v.wait_ge(S_("sqrt"), 2)
            link(v.reciprocal(RNA, RNA))
            for t in range(NT):
                if t >= 2:
                    v.wait_ge(S_("qk_ps"), t - 1)
                q = QNB[t % 2]
                tt(q[:, 0:512].rearrange("p (h g d) -> p g h d", h=4, g=2),
                   AQ[:, t, 0:512].rearrange("p (g h d) -> p g h d", g=2, h=4),
                   RNA[:, 10 * t:10 * t + 8].rearrange("p (g h o) -> p g h o", g=2, o=1).to_broadcast([P, 2, 4, 64]), ALU.mult).then_inc(S_("qkn"), 1)
                k = q[:, 512:640].rearrange("p (g d) -> p g d", g=2)
                tt(k, AQ[:, t, 512:640].rearrange("p (g d) -> p g d", g=2), bc(RNA[:, 10 * t + 8:10 * t + 10], 64), ALU.mult).then_inc(S_("qkn"), 1)
                v.wait_ge(S_("qkn"), 3 * t + 2)
                tt(k, k, bm(KWT, 2), ALU.mult).then_inc(S_("qkn"), 1)
            for t in range(NT):
                v.wait_ge(S_("z_sig"), t + 1)
                tt(DZ[:, t, 0:512], DZ[:, t, 0:512], SGZ, ALU.mult).then_inc(S_("z_done"), 1)
            v.wait_ge(S_("z_done"), NT)
            for t in range(NT):
                tt(h4(DZ[:, t, 0:512]), h4(DZ[:, t, 0:512]), bm(ZNW, HD), ALU.mult).then_inc(S_("zw"), 1)

            def taps(i):
                n = TOKU + i
                v.wait_ge(S_("proj_ps"), n + 1)
                if i >= 2:
                    v.wait_ge(S_("sig"), i - 1)
                    v.wait_ge(S_("silu"), i - 1)
                src, cv = PA[n % 2], CV[i % 2]
                ts(cv, src, CW[:, 36 + i:37 + i], None, ALU.mult).then_inc(S_("conv"), 1)
                for j in range(1, 4):
                    v.wait_ge(S_("conv"), 4 * i + j)
                    col = (3 - j) * 12 + i
                    stt(out=cv[:, j:S], in0=src[:, 0:S - j], scalar=CW[:, col:col + 1], in1=cv[:, j:S],
                        op0=ALU.mult, op1=ALU.add).then_inc(S_("conv"), 1)

            def silu(i):
                v.wait_ge(S_("sig"), i + 1)
                if i >= 2:
                    v.wait_ge(S_("st_ps"), i - 1)
                tt(ST[i % 2], CV[i % 2], SG[i % 2], ALU.mult).then_inc(S_("silu"), 1)

            def softmax_a(n):
                w = P if n else CH
                v.wait_ge(S_("sc_ps"), n + 1)
                if n >= 2:
                    v.wait_ge(S_("pt_ps"), n - 1)
                if n:
                    v.wait_ge(S_("shifted"), n)
                sc = PSC[:, :, 0:256].rearrange("p k (h n) -> p k h n", h=2)[:, :, :, 0:w]
                link(v.tensor_reduce(MXS.rearrange("p (k h) -> p k h", k=2), sc, AX.X, ALU.max))
                link(tt(MXS, MXS, SKT, ALU.max))
                link(tt(MNEG, SKT, MXS, ALU.subtract))
                pb = PB[n % 2].rearrange("p (k h n) -> p k h n", k=2, h=2)[:, :, :, 0:w]
                tt(pb, sc, MXS.rearrange("p (k h o) -> p k h o", k=2, o=1).to_broadcast([P, 2, 2, w]), ALU.subtract).then_inc(S_("shifted"), 1)

            def softmax_b(n):
                w = P if n else CH
                pb = PB[n % 2].rearrange("p (g n) -> p g n", g=4)[:, :, 0:w]
                v.wait_ge(S_("exps_done"), 2 * (n + 1) - 1)
                if n:
                    v.wait_ge(S_("pnorm"), n)
                link(v.tensor_reduce(DEN, pb, AX.X, ALU.add))
                v.wait_ge(S_("exps_done"), 2 * (n + 1) - 0)
                link(tt(DEN, DEN, ESK, ALU.add))
                link(v.reciprocal(RDEN, DEN))
                tt(pb, pb, bc(RDEN, w), ALU.mult).then_inc(S_("pnorm"), 1)

            for i in range(CHU + 1):
                if i < CHU:
                    taps(i)
                if i < NCH:
                    softmax_a(i)
                if i >= 1:
                    silu(i - 1)
                if i < NCH:
                    softmax_b(i)
            for n in range(8):
                v.wait_ge(S_("sq_done"), n + 1)
                v.tensor_reduce(SSQ[:, 4 * n:4 * n + 4], h4(SQD), AX.X, ALU.add).then_inc(S_("ssq"), 1)
            v.wait_ge(S_("ssq"), 8)
            ts(SSQ, SSQ, EPS, None, ALU.add).then_inc(S_("meansq"), 1)
            link(tt(SPT.rearrange("p (t h) -> p t h", t=NT), DZ[:, :, 516:520], bm(DTB, NT), ALU.add))
            link(ts(SPM, SPT, -1.0, None, ALU.mult))
            tt(SPM, SPM, SPT, ALU.min).then_inc(S_("dn_vec"), 1)
            v.wait_ge(S_("dn_vec"), 1)
            link(ts(SPT, SPT, 0.0, None, ALU.max))
            v.wait_ge(S_("dn_act"), 2)
            ts(SPM, SPM, 1.0, None, ALU.add).then_inc(S_("dn_vec"), 1)
            v.wait_ge(S_("sqrt"), 3)
            link(v.reciprocal(RSQ, RSQ))
            link(ts(RSQ.rearrange("p (c s h) -> p c s h", c=NT, s=2)[:, :, 0, :], RSQ.rearrange("p (c s h) -> p c s h", c=NT, s=2)[:, :, 0, :],
                    float(P) ** -0.5, None, ALU.mult))
            v.wait_ge(S_("dn_act"), 4)
            link(tt(SPT, SPT, SPM, ALU.add))
            v.wait_ge(S_("dn_act"), 3)
            link(ts(AL, AL, -1.0, None, ALU.mult))
            tt(GV.rearrange("p (t h) -> p t h", t=NT), SPT.rearrange("p (t h) -> p t h", t=NT), bm(AL, NT), ALU.mult).then_inc(S_("dn_vec"), 1)
            v.wait_ge(S_("g_ps"), 1)
            link(v.tensor_copy(GC, AO[:, 0:16]))
            v.tensor_copy(GLC, AO[:, 16:32]).then_inc(S_("dn_vec"), 1)
            v.wait_ge(S_("dn_vec"), 4)
            tt(EGD, GLC, GC, ALU.subtract).then_inc(S_("dn_vec"), 1)
            v.wait_ge(S_("dn_act"), 1)
            v.wait_ge(S_("att_out"), NCH)
            v.wait_ge(S_("tri"), 2)
            v.wait_ge(S_("p_b"), 28)
            for pair in range(2):
                cs = (2 * pair, 2 * pair + 1)
                if pair:
                    v.wait_ge(S_("kv_ps"), 2)
                    v.wait_ge(S_("o_ps"), 2)
                for c in cs:
                    b = B[c % 2]
                    hs = slice(4 * c, 4 * c + 4)
                    tt(h4(b["KH"]), KTM[:, c, :, :], bc(RSQ[:, 8 * c + 4:8 * c + 8], P), ALU.mult).then_inc(S_("kq_scaled"), 1)
                    v.wait_ge(S_("kq_scaled"), 3 * (c + 1) - 2)
                    tt(h4(b["KB"]), h4(b["KH"]), bc(BETA[:, hs], P), ALU.mult).then_inc(S_("kq_scaled"), 1)
                    tt(h4(b["QN"]), QTM[:, c, :, :], bc(RSQ[:, 8 * c:8 * c + 4], P), ALU.mult).then_inc(S_("kq_scaled"), 1)
                    v.wait_ge(S_("grow_ps"), c + 1)
                    link(tt(h4(b["DEC"]), h4(XP), bc(GC[:, hs], P), ALU.subtract))
                    tt(h4(b["DEC"]), h4(b["DEC"]), bm(NEGM, HD), ALU.add).then_inc(S_("dsub"), 1)
                    v.wait_ge(S_("decay"), c + 1)
                    v.wait_ge(S_("li_ps"), 2 * (c + 1) - 1)
                    tt(b["LT"], PS[0], b["DEC"], ALU.mult).then_inc(S_("li"), 1)
                    v.wait_ge(S_("li_ps"), 2 * (c + 1) - 0)
                    v.wait_ge(S_("scaled_pool"), c + 1)
                    tt(b["INT"], PS[1], b["DEC"], ALU.mult).then_inc(S_("li"), 1)
                    if c == 3:
                        v.wait_ge(S_("kq_scaled"), 3 * (4) - 0)
                for c in cs:
                    b = B[c % 2]
                    v.wait_ge(S_("li"), 2 * (c + 1) - 1)
                    v.wait_ge(S_("dt_ready"), 4 * c + 4)
                    link(tt(h4(b["CT"]), h4(b["LT"]), bm(MSK[0], HD), ALU.mult))
                    tt(h4(b["U"]), bm(ident[:, :], HD), h4(b["CT"]), ALU.subtract).then_inc(S_("u_init"), 1)
                    v.wait_ge(S_("u_init"), c + 1)
                    tt(h4(b["CT"]), h4(b["LT"]), bm(MSK[1], HD), ALU.mult).then_inc(S_("ct"), 1)
                for lv in range(len(LEVELS)):
                    for c in cs:
                        b, n = B[c % 2], (pair * len(LEVELS) + lv) * 2 + c % 2
                        if lv < len(LEVELS) - 1:
                            v.wait_ge(S_("p2_ps"), (pair * 5 + lv) * 2 + c % 2 + 1)
                            tt(b["T"], b["T"], PS[6], ALU.subtract).then_inc(S_("t_upd"), 1)
                        v.wait_ge(S_("p2t_ps"), n + 1)
                        tt(b["U"], b["U"], PS[7], ALU.subtract).then_inc(S_("u_upd"), 1)
                        if lv < len(LEVELS) - 1:
                            tt(h4(b["CT"]), h4(b["LT"]), bm(MSK[lv + 2], HD), ALU.mult).then_inc(S_("ct"), 1)
                for c in cs:
                    b = B[c % 2]
                    v.wait_ge(S_("uw"), 2 * (c + 1) - 1)
                    if c:
                        v.wait_ge(S_("ws_ps"), c)
                        tt(b["VN"], b["USOL"], PS[7], ALU.subtract).then_inc(S_("vnew"), 1)
                    else:
                        v.tensor_copy(b["VN"], b["USOL"]).then_inc(S_("vnew"), 1)
                    v.wait_ge(S_("kv_ps"), c + 1)
                    if c:
                        v.wait_ge(S_("o_ps"), c + 1)
                        v.wait_ge(S_("dn_act"), 7)
                        link(tt(h4(STATE), h4(STATE), bc(EGL[:, 4 * c:4 * c + 4], P), ALU.mult))
                        tt(STATE, STATE, PS[5], ALU.add).then_inc(S_("state"), 1)
                    else:
                        v.tensor_copy(STATE, PS[5]).then_inc(S_("state"), 1)
            for c in range(NT):
                v.wait_ge(S_("sq_done"), 8 + c + 1)
                v.tensor_reduce(SSO[:, 4 * c:4 * c + 4], h4(B[0]["LT"]), AX.X, ALU.add).then_inc(S_("ssq"), 1)
            v.wait_ge(S_("ssq"), 8 + NT)
            ts(SSO, SSO, 1.0 / P, EPS, ALU.mult, ALU.add).then_inc(S_("meansq"), 1)
            v.wait_ge(S_("sqrt"), 4)
            link(v.reciprocal(RSO, RSO))
            v.wait_ge(S_("zw"), NT)
            for c in range(NT):
                link(tt(h4(OB[:, c, :]), h4(OB[:, c, :]), bc(RSO[:, 4 * c:4 * c + 4], P), ALU.mult))
                tt(OB[:, c, :], OB[:, c, :], DZ[:, c, 0:512], ALU.mult).then_inc(S_("dn_out"), 1)
            v.wait_ge(S_("res_in"), 16 * (NT + 3))
            v.wait_ge(S_("res_in"), 16 * (NT + 3))

            def top4(t):
                v.wait_ge(S_("lg_ps"), t + 1)
                tt(LG[:, t, :], PS[5][:, 0:NE], RB, ALU.add).then_inc(S_("logits"), 1)
                v.wait_ge(S_("logits"), t + 1)
                link(v.max(MX8[:, t, :], LG[:, t, :]))
                link(v.max_index(MI8[:, t, :], MX8[:, t, :], LG[:, t, :]))
                link(v.tensor_copy(MIF[:, t, :], MI8[:, t, :]))

            for t in range(NT):
                for half in range(2):
                    v.wait_ge(S_("outproj"), 2 * t + half + 1)
                    hh = H[:, t, half * 512:half * 512 + 512]
                    tt(hh, hh, PS[half], ALU.add).then_inc(S_("h_add"), 1)
                v.wait_ge(S_("h_add"), 2 * t + 2)
                v.wait_ge(S_("ssh"), t + 1)
                ts(SSH[:, t:t + 1], SSH[:, t:t + 1], 1.0 / D, EPS, ALU.mult, ALU.add).then_inc(S_("meansq"), 1)
                v.wait_ge(S_("sqrt"), 5 + t)
                link(v.reciprocal(RSH[:, t:t + 1], RSH[:, t:t + 1]))
                stt(out=HN[:, t, :], in0=H[:, t, :], scalar=RSH[:, t:t + 1], in1=FW, op0=ALU.mult, op1=ALU.mult).then_inc(S_("hn_ready"), 1)
                if t >= 2:
                    top4(t - 2)
            for t in (2, 3):
                top4(t)
            for t in range(NT):
                ts(GATE[:, 4 * t:4 * t + 4], MX8[:, t, 0:4], MX8[:, t, 0:1], None, ALU.subtract).then_inc(S_("v_gate"), 1)
            v.wait_ge(S_("v_gate"), NT)
            v.wait_ge(S_("consts"), 9)
            for t in range(NT):
                for k in range(TOPK):
                    ts(OH[:, t, k, :], IO32, MIF[:, t, k:k + 1], None, ALU.is_equal).then_inc(S_("v_oh"), 1)
                v.wait_ge(S_("v_oh"), 4 * t + 4)
                v.tensor_reduce(MASK[:, t, :], OH[:, t, :, :].rearrange("p k e -> p e k"), AX.X, ALU.add).then_inc(S_("mask"), 1)
            v.wait_ge(S_("gexp"), 1)
            link(v.tensor_reduce(GSUM, GATE[:, :].rearrange("p (t k) -> p t k", t=NT), AX.X, ALU.add))
            link(v.reciprocal(GREC, GSUM))
            link(tt(GATE[:, :].rearrange("p (t k) -> p t k", t=NT), GATE[:, :].rearrange("p (t k) -> p t k", t=NT), bc(GREC, TOPK), ALU.mult))
            v.wait_ge(S_("rank_ps"), 1)
            link(ts(NBI, PS[3][:, 0:NE], float(BT - 1), None, ALU.add))
            link(ts(NBI, NBI, 5, None, ALU.logical_shift_right))
            link(ts(NBF, NBI, 1.0, None, ALU.max))
            link(v.tensor_tensor_scan(BEF, ONE32, NBF, 0.0, ALU.mult, ALU.add))
            link(ts(LASTB[:, :], BEF, -1.0, None, ALU.add))
            link(tt(BSF, BEF, NBF, ALU.subtract))
            v.wait_ge(S_("rank"), 1)
            for t in range(NT):
                link(tt(OHR[:, t, :, :], OH[:, t, :, :], bm(RANK[:, t, :], TOPK), ALU.mult))
            link(v.tensor_reduce(RK.rearrange("p (t k) -> p t k", t=NT), OHR, AX.X, ALU.add))
            for t in range(NT):
                link(tt(OHR[:, t, :, :], OH[:, t, :, :], bm(BSF, TOPK), ALU.mult))
            link(v.tensor_reduce(BSK.rearrange("p (t k) -> p t k", t=NT), OHR, AX.X, ALU.add))
            link(v.tensor_copy(RKI, RK))
            link(ts(RKI, RKI, 5, None, ALU.logical_shift_right))
            link(v.tensor_copy(RKB, RKI))
            link(stt(out=TPOS, in0=RKB, scalar=-float(BT), in1=RK, op0=ALU.mult, op1=ALU.add))
            link(tt(BLK, BSK, RKB, ALU.add))
            link(stt(out=SLOT[:, :], in0=BSK, scalar=float(BT), in1=RK, op0=ALU.mult, op1=ALU.add))
            for i in range(4 * TOPK):
                if i >= 2:
                    v.wait_ge(S_("list_ps"), i - 1)
                t = i // TOPK
                ts(T1[i % 2], IOM, TPOS[:, i:i + 1], TOK4[:, t:t + 1], ALU.is_equal, ALU.mult).then_inc(S_("onehots"), 1)
                ts(B1[i % 2], IOB, BLK[:, i:i + 1], None, ALU.is_equal).then_inc(S_("onehots"), 1)
            link(ts(PJI, PJI, 5, None, ALU.logical_shift_right))
            link(v.tensor_copy(PJ, PJI))
            v.wait_ge(S_("list_ps"), 4 * TOPK)
            ts(IDX[:, :], PS[4][:, 0:MAXB + 1], PJ, None, ALU.add).then_inc(S_("lists_done"), 1)
            v.wait_ge(S_("lists_done"), 1)

            def activate(i, p, first):
                v.wait_ge(S_("gu_ps"), i + 1)
                if not first:
                    v.wait_ge(S_("at_ps"), i)
                tt(GU[:, :], GPS, BGU[p][:, :], ALU.add).then_inc(S_("gu_evac"), 1)
                v.wait_ge(S_("gu_evac"), i + 1)
                ts(GU[:, 0:QW], GU[:, 0:QW], LIMIT, None, ALU.min).then_inc(S_("gate_ready"), 1)
                ts(GU[:, QW:2 * QW], GU[:, QW:2 * QW], LIMIT, -LIMIT, ALU.min, ALU.max)
                v.wait_ge(S_("sig_ready"), i + 1)
                tt(SIG[:, :], SIG[:, :], GU[:, 0:QW], ALU.mult).then_inc(S_("glu"), 1)
                v.wait_ge(S_("glu"), i + 1)
                stt(out=GU[:, 0:QW], in0=GU[:, QW:2 * QW], scalar=1.0, in1=SIG[:, :], op0=ALU.add, op1=ALU.mult).then_inc(S_("act_ready"), 1)

            def spread_biases(e, p, rnd):
                v.wait_ge(S_(f"bias_in{p}"), rnd)
                v.sem_inc(S_("bias_passed"), 1)
                v.stream_shuffle(BGU[p][:, :], BGU[p][:, :], [0] * 32).then_inc(S_("bias_spread"), 1)
                v.stream_shuffle(BDN[p][:, :], BDN[p][:, :], [0] * 32).then_inc(S_("bias_spread"), 1)
                v.wait_ge(S_("bias_spread"), 2 * (e + 1))

            def y_evac(i, p):
                v.wait_ge(S_("d_ps"), i + 2)
                v.wait_ge(S_("y_out"), (i + 1) * 16)
                tt(Y[:, :], DPS, BDN[p][:, :], ALU.add).then_inc(S_("y_ready"), 1)

            v.memset(IDXC[:, 1:2], 0).then_inc(S_("y_ready"), 1)
            spread_biases(0, 0, 32)
            activate(0, 0, True)
            last = v.value_load(LASTB[0:1, 0:1], min_val=0, max_val=MAXB - 1)
            with v.If(last > 0):
                activate(1, 0, False)
                y_evac(0, 0)
            with v.If(last > 1):
                with v.Fori(2, last + 1) as i:
                    activate(i, 0, False)
                    y_evac(i - 1, 0)

            def expert(e, p, before, brnd):
                spread_biases(e, p, brnd)
                activate(before + 1, p, False)
                y_evac(before, 1 - p)
                v.memset(IDXC[:, 1:2], 0).then_inc(S_("y_free"), 1)
                last = v.value_load(LASTB[0:1, bass.ds(e, 1)], min_val=0, max_val=MAXB - 1)
                with v.If(last > before + 1):
                    with v.Fori(before + 2, last + 1) as i:
                        activate(i, p, False)
                        y_evac(i - 1, p)
                return last

            with v.Fori(0, NE // 2 - 1) as r:
                last = v.value_load(LASTB[0:1, bass.ds(2 * r, 1)], min_val=0, max_val=MAXB - 1)
                last = expert(2 * r + 1, 1, last, (r + 1) * 32)
                expert(2 * r + 2, 0, last, (r + 2) * 32)
            last = v.value_load(LASTB[0:1, NE - 2:NE - 1], min_val=0, max_val=MAXB - 1)
            last = expert(NE - 1, 1, last, NE * 16)
            y_evac(last, 1)
            v.wait_ge(S_("hf_in"), 16 * NT)
            for k in range(4):
                v.wait_ge(S_(f"yg_in{k}"), 64)
            for t in range(NT):
                for k in range(TOPK):
                    i = TOPK * t + k
                    ins = stt(out=HF[:, t, :], in0=YG[:, i, :], scalar=GATE[:, i:i + 1], in1=HF[:, t, :], op0=ALU.mult, op1=ALU.add)
                    if k == TOPK - 1:
                        ins.then_inc(S_("summed"), 1)
                    else:
                        link(ins)


_INS = ["x", "norm_mix_w", "w_in", "attn_q_norm_w", "attn_k_norm_w", "attn_sinks", "dn_conv_w", "dn_a_log", "dn_dt_bias",
        "dn_out_norm_w", "w_out", "norm_ffn_w", "router_w", "router_b", "expert_w_gate_up", "expert_b_gate_up",
        "expert_w_down", "expert_b_down"]


def kernel(**inputs):
    import numpy as _np
    import concourse.bacc as _bacc
    from concourse import mybir as _mybir
    from concourse.bass_utils import run_bass_kernel_spmd as _run

    nc = _bacc.Bacc("TRN2", target_bir_lowering=False, num_devices=1)
    arrays, args = {}, []
    for name in _INS:
        a = _np.ascontiguousarray(inputs[name])[0]
        arrays[f"in_{name}"] = a
        args.append(nc.dram_tensor(f"in_{name}", a.shape, _mybir.dt.from_np(a.dtype), kind="ExternalInput").ap())
    out = nc.dram_tensor("out_0", (S, D), _mybir.dt.float32, kind="ExternalOutput").ap()
    hybrid_block(nc, *args, out)
    r = _run(nc, [arrays], core_ids=[0])
    return r.results[0]["out_0"].reshape(1, S, D)
```

```python
from contextlib import ExitStack

import numpy as np

import concourse.bass as bass
from concourse import mybir
from concourse.alu_op_type import AluOpType as ALU

ACT = mybir.ActivationFunctionType
AX = mybir.AxisListType
F32 = mybir.dt.float32
I32 = mybir.dt.int32
U32 = mybir.dt.uint32

P = 128
D = 1024
S = 512
NT = S // P
KD = D // P
HA, DH, KV = 8, 64, 2
HP = HA // KV
CH = 64
NCH = S // CH
HD = 4
NE, TOPK = 32, 4
FF = 1024
EPS = 1e-6
BT = 32
MAXB = S * TOPK // BT + NE
QW = 256
LIMIT, ALPHA = 7.0, 1.702

SLABS = [(0, 256), (256, 256), (512, 256), (2304, 260), (2564, 260)] + [(768 + 256 * i, 256) for i in range(6)]
SLABW = 260
NSL = 3
TOKU = 5 * NT
CHU = 12
LEVELS = [2, 4, 8, 16, 32, 64]


def hybrid_block(nc, x, norm_mix_w, w_in, qn_w, kn_w, sinks, conv_w, a_log, dt_bias, out_norm_w, w_out,
                 norm_ffn_w, router_w, router_b, w_gu, b_gu, w_dn, b_dn, out):
    ctx = ExitStack()
    with ctx:
        def sb(name, cols, dt=F32):
            return ctx.enter_context(nc.sbuf_tensor(name, [P, cols], dt))

        sems = {}

        def S_(name):
            if name not in sems:
                sems[name] = ctx.enter_context(nc.semaphore(name))
            return sems[name]

        h_d = nc.dram_tensor("h_scratch", (S, D), F32).ap()
        hn_d = nc.dram_tensor("hn_scratch", (S * 4, QW), F32).ap()
        y_d = nc.dram_tensor("y_scratch", (MAXB * BT, D), F32).ap()

        WE = [sb("W0", 24576), sb("W1", 24576)]
        W0, W1 = WE
        GUW = [w[:, 0:16384].rearrange("p (k n) -> p k n", k=KD) for w in WE]
        DNW = [w[:, 16384:24576].rearrange("p (k n) -> p k n", k=KD) for w in WE]

        ident = sb("ident", P)
        XG = sb("XG", QW)
        XT = sb("XT", 2 * P)
        GU = sb("GU", 2 * QW)
        SIG = sb("SIG", QW)
        AT = sb("AT", 2 * P)
        Y = sb("Y", QW)
        BGU = [sb("BGU0", 2 * QW), sb("BGU1", 2 * QW)]
        BDN = [sb("BDN0", QW), sb("BDN1", QW)]
        IDX = sb("IDX", MAXB + 1, U32)
        IDXC = sb("IDXC", 2, U32)
        LASTB = sb("LASTB", NE, I32)
        SLOT = sb("SLOT", 4 * TOPK, U32)
        GATE = sb("GATE", 4 * TOPK)
        SM = sb("SM", 420)

        def small(at, n):
            return SM[:, at:at + n]

        SSX, RSX = small(0, 4), small(4, 4)
        SSA, RNA = small(8, 40), small(48, 40)
        MXS, MNEG, ESK, DEN, RDEN = [small(88 + 4 * i, 4) for i in range(5)]
        SKT = small(108, 4)
        KWT = small(112, 64)
        AL, DTB = small(176, 4), small(180, 4)
        GV, SPT, SPM = small(184, 16), small(200, 16), small(216, 16)
        BETA = small(232, 16)
        GC, GLC = small(248, 16), small(264, 16)
        EG, EGD, EGL = small(280, 16), small(296, 16), small(312, 16)
        SSQ, RSQ = small(328, 32), small(360, 32)
        SSO, RSO = small(392, 16), small(392, 16)
        SSH, RSH = small(408, 4), small(412, 4)

        X = W0[:, 0:4096].rearrange("p (t n) -> p t n", t=NT)
        CV = [W0[:, 512 * i:512 * i + 512] for i in range(2)]
        SG = [W0[:, 1024 + 512 * i:1536 + 512 * i] for i in range(2)]
        ST = [W0[:, 2048 + 512 * i:2560 + 512 * i] for i in range(2)]
        SGZ = W0[:, 3072:3584]
        UT = W0[:, 4096:8192].rearrange("p (k n) -> p k n", k=KD)
        SL = [W0[:, 8192 + i * 2080:8192 + i * 2080 + 2080].rearrange("p (k n) -> p k n", k=KD) for i in range(NSL)]
        AQ = W0[:, 14432:17504].rearrange("p (t n) -> p t n", t=NT)
        QNT = W0[:, 17504:19552].rearrange("p (c h q) -> p c h q", c=NCH, h=HP)
        KNT = W0[:, 19552:20064]
        AVS = W0[:, 20064:20448].rearrange("p (i n) -> p i n", i=3)
        MSK = [W0[:, 20480 + P * i:20608 + P * i] for i in range(7)]
        TRIU = W0[:, 21376:21504]
        ONES = W0[:, 21504:21632]
        NEGM = W0[:, 21632:21760]
        STATE = W0[:, 21760:22272]
        WO1 = W0[:, 16384:20480].rearrange("p (k n) -> p k n", k=4)
        QTM, KTM, VTM = [W1[:, 2048 * i:2048 * i + 2048].rearrange("p (t h n) -> p t h n", t=NT, h=HD)
                         for i in range(3)]
        OB = W1[:, 0:2048].rearrange("p (t n) -> p t n", t=NT)
        WO0 = W1[:, 2048:6144].rearrange("p (k n) -> p k n", k=4)
        DZ = W1[:, 6144:8224].rearrange("p (t n) -> p t n", t=NT)
        CAT = W1[:, 20480:24576].rearrange("p (k n) -> p k n", k=KD)

        def slot(i, c):
            if c >= 2:
                at = 512 * (2 * i + c - 2)
                return W0[:, at:at + 512]
            n = 2 * i + c
            return W1[:, 8224 + 512 * n:8736 + 512 * n] if n < 23 else W0[:, 22272 + 512 * (n - 23):22784 + 512 * (n - 23)]

        names = ["KH", "KB", "QN", "QE", "KBEG", "KTE", "VB", "KHT", "KBT", "QET", "QNT", "DEC", "LT"]
        B = [{n: slot(i, c) for i, n in enumerate(names)} for c in range(NT)]
        for b in B:
            b.update(INT=b["KH"], CT=b["KB"], P1=b["QN"], USOL=b["QE"], U=b["KHT"], T=b["KBT"], WT=b["QNT"], VN=b["DEC"])
        STATES = [STATE, B[0]["T"]]
        QNB = [W1[:, 8224 + 640 * i:8864 + 640 * i] for i in range(2)]
        PB = [W1[:, 9504 + 512 * i:10016 + 512 * i] for i in range(2)]
        PT = W1[:, 10528:11040]
        SQA = W1[:, 11040:11680]
        NW = W1[:, 11680:12704]
        CWR = W1[0:48, 12704:12832]
        CW = W0[:, 23808:23856]
        ZNW = W0[:, 23856:23984]
        SQD = [W0[:, 3584:4096], SGZ]
        H = W1[:, 6144:10240].rearrange("p (t n) -> p t n", t=NT)
        HN = W1[:, 10240:14336].rearrange("p (t n) -> p t n", t=NT)
        HNT = W1[:, 16384:20480].rearrange("p (k n) -> p k n", k=KD)
        FW = W0[:, 22272:23296]
        RW = W0[:, 23296:23552].rearrange("p (k n) -> p k n", k=KD)
        RB = W0[:, 23552:23584]
        LG = W0[:, 23584:23712].rearrange("p (t n) -> p t n", t=NT)
        MX8 = W0[:, 23712:23744].rearrange("p (t n) -> p t n", t=NT)
        MI8 = W0[:, 23744:23776].bitcast(U32).rearrange("p (t n) -> p t n", t=NT)
        MIF = W0[:, 23776:23808].rearrange("p (t n) -> p t n", t=NT)
        RT = W1[:, 20480:24576]
        OH = RT[:, 0:512].rearrange("p (t k e) -> p t k e", t=NT, k=TOPK)
        OHR = RT[:, 512:1024].rearrange("p (t k e) -> p t k e", t=NT, k=TOPK)
        MASK = RT[:, 1024:1152].rearrange("p (t e) -> p t e", t=NT)
        NBF = RT[:, 1152:1184]
        NBI = RT[:, 1184:1216].bitcast(I32)
        BEF = RT[:, 1216:1248]
        BSF = RT[:, 1248:1280]
        ONE32 = RT[:, 1280:1312]
        RK = RT[:, 1312:1328]
        RKI = RT[:, 1328:1344].bitcast(I32)
        RKB = RT[:, 1344:1360]
        BSK = RT[:, 1360:1376]
        TPOS = RT[:, 1376:1392]
        BLK = RT[:, 1392:1408]
        GSUM = RT[:, 1408:1412]
        GREC = RT[:, 1412:1416]
        PJ = RT[:, 1416:1417]
        PJI = RT[:, 1417:1418].bitcast(I32)
        TOK4 = RT[:, 1420:1424]
        IO32 = RT[:, 1424:1456]
        IOM = RT[:, 1456:1584]
        IOB = RT[:, 1584:1584 + MAXB + 1]
        RANK = RT[:, 1696:1824].rearrange("p (t e) -> p t e", t=NT)
        STRU = RT[:, 1824:1952]
        ONER = RT[:, 1952:2080]
        T1 = [RT[:, 2080 + P * i:2208 + P * i] for i in range(2)]
        B1 = [RT[:, 2336 + P * i:2336 + P * i + MAXB + 1] for i in range(2)]
        HF = W0[:, 0:4096].rearrange("p (t n) -> p t n", t=NT)
        YG = W0[:, 4096:20480].rearrange("p (i n) -> p i n", i=4 * TOPK)

        PS = [ctx.enter_context(nc.psum_tensor(f"PS{i}", [P, 512], F32))[:, :] for i in range(4)]
        PSC = ctx.enter_context(nc.psum_tensor("PSC", [P, 2, 512], F32))
        PS += [PSC[:, 0, :], PSC[:, 1, :]]
        PS += [ctx.enter_context(nc.psum_tensor(f"PS{i}", [P, 512], F32))[:, :] for i in (6, 7)]
        PA = PS[0:2]
        TA, TB, AO, XP = PS[2], PS[3], PS[6], PS[7]

        GPS, DPS, XPS, ATPS, RPS = PS[0], PS[1][:, 0:QW], PS[2][:, 0:QW], PS[3][:, 0:QW], PS[6][:, 0:P]

        def bc(v, n):
            a = v.shape[1]
            return v.rearrange("p (a o) -> p a o", o=1).to_broadcast([P, a, n])

        def bm(v, a):
            return v.rearrange("p (o n) -> p o n", o=1).to_broadcast([P, a, v.shape[1]])

        def h4(v):
            return v.rearrange("p (h n) -> p h n", h=HD)

        block = ctx.enter_context(nc.Block())

        def rep(v, n=P):
            return v.partition_broadcast(n)

        NORM_AT = {6: (0,), 7: (1,), 8: (2,), 9: (3,), 10: (4, 5), 11: (6, 7)}

        @block.sync
        def _(sp):
            for t in range(NT):
                sp.dma_start(X[:, t, :], x[t * P:(t + 1) * P, :]).then_inc(S_(f"x_in{t}"), 16)
                if t == 0:
                    sp.dma_start(NW, rep(norm_mix_w)).then_inc(S_("nw_in"), 16)
            for n, (c0, w) in enumerate(SLABS):
                if n >= NSL:
                    sp.wait_ge(S_("slab_used"), n - NSL + 1)
                sp.dma_start(SL[n % NSL][:, :, 0:w],
                             w_in.rearrange("(k p) n -> p k n", p=P)[:, :, c0:c0 + w]).then_inc(S_(f"slab_in{n % NSL}"), 16)
                if n == 3:
                    sp.wait_ge(S_("tok_evac"), 3 * NT)
                    for i in range(3):
                        sp.dma_start(AVS[0:64, i, :], AQ[64:P, i, 640:768]).then_inc(S_("avs_in"), 16)
                        sp.dma_start(AVS[64:P, i, :], AQ[0:64, i + 1, 640:768]).then_inc(S_("avs_in"), 16)
            sp.wait_ge(S_("att_out"), NCH)
            wo_v = w_out[512:1024, :].rearrange("(k p) n -> p k n", p=P)
            sp.dma_start(WO1, wo_v).then_inc(S_("wo_in"), 16)
            sp.wait_ge(S_("kq_scaled"), 3 * NT)
            sp.wait_ge(S_("scaled_pool"), NT)
            for kv in range(KV):
                sp.dma_start(WO0[kv * 64:kv * 64 + 64, :, :],
                             w_out[kv * 256:kv * 256 + 256, :].rearrange("(h d) n -> d h n", h=HP)).then_inc(S_("wo_in"), 16)
            sp.wait_ge(S_("dn_out"), NT)
            for t in range(NT):
                sp.dma_start(H[:, t, :], x[t * P:(t + 1) * P, :]).then_inc(S_("res_in"), 16)
            sp.dma_start(FW, rep(norm_ffn_w)).then_inc(S_("res_in"), 16)
            sp.dma_start(RW, router_w.rearrange("(k p) n -> p k n", p=P)).then_inc(S_("res_in"), 16)
            sp.dma_start(RB, rep(router_b)).then_inc(S_("res_in"), 16)
            for q in range(4):
                sp.dma_start(GUW[0][:, 2 * q:2 * q + 2, :],
                             w_gu[0].rearrange("(k p) n -> p k n", p=P)[:, 2 * q:2 * q + 2, :]).then_inc(S_(f"gu_in0{q}"), 16)
            for t in range(NT):
                sp.wait_ge(S_("h_add"), 2 * t + 2)
                sp.dma_start(h_d[t * P:(t + 1) * P, :], H[:, t, :]).then_inc(S_("h_out"), 16)
                sp.wait_ge(S_("hn_ready"), t + 1)
                sp.dma_start(hn_d[t * 512:(t + 1) * 512, :].rearrange("(p j) n -> p (j n)", j=4), HN[:, t, :]).then_inc(S_("hn_out"), 16)
            def biases(e, p):
                sp.dma_start(BGU[p][0:P:32, :].rearrange("p (g n) -> p g n", g=2),
                             b_gu[e].rearrange("(g j n) -> j g n", g=2, j=4)).then_inc(S_(f"bias_in{p}"), 16)
                sp.dma_start(BDN[p][0:P:32, :], b_dn[e].rearrange("(j n) -> j n", j=4)).then_inc(S_(f"bias_in{p}"), 16)

            def gu_part(e, p, parts, through=None):
                for q in parts:
                    if through is not None:
                        sp.wait_ge(S_(f"gu_read{q}" if q < 3 else "gu_ps"), through)
                    sp.dma_start(GUW[p][:, 2 * q:2 * q + 2, :],
                                 w_gu[e].rearrange("(k p) n -> p k n", p=P)[:, 2 * q:2 * q + 2, :]).then_inc(S_(f"gu_in{p}{q}"), 16)

            def dn_part(e, p, parts, through=None):
                for q in parts:
                    if through is not None:
                        sp.wait_ge(S_("dn_read"), through) if q == 0 else sp.wait_ge(S_("d_ps"), through + 1)
                    sp.dma_start(DNW[p][:, 4 * q:4 * q + 4, :],
                                 w_dn[e].rearrange("(k p) n -> p k n", p=P)[:, 4 * q:4 * q + 4, :]).then_inc(S_(f"dn_in{p}{q}"), 16)

            sp.wait_ge(S_("bias_zeros"), 4)
            biases(0, 0)
            sp.wait_ge(S_("outproj"), 2 * NT)
            dn_part(0, 0, [0])
            gu_part(1, 1, [0])
            sp.wait_ge(S_("hn_out"), 16 * NT)
            sp.wait_ge(S_("h_out"), 16 * NT)
            sp.wait_ge(S_("hnt_ps"), 2 * NT)
            gu_part(1, 1, [1, 2, 3])
            sp.wait_ge(S_("lists_done"), 1)
            sp.wait_ge(S_("gathered"), 16)
            dn_part(0, 0, [1])
            biases(1, 1)
            dn_part(1, 1, [0, 1])

            def reload(e, p):
                through = sp.value_load(LASTB[0:1, bass.ds(e - 2, 1)], min_val=0, max_val=MAXB - 1) + 1
                gu_part(e, p, range(4), through)
                dn_part(e, p, range(2), through)
                sp.wait_ge(S_("y_free"), e - 1)
                biases(e, p)

            with sp.Fori(1, NE // 2) as r:
                reload(2 * r, 0)
                reload(2 * r + 1, 1)
            through = sp.value_load(LASTB[0:1, NE - 2:NE - 1], min_val=0, max_val=MAXB - 1) + 1
            sp.wait_ge(S_("gu_ps"), through)
            for t in range(NT):
                sp.dma_start(HF[:, t, :], h_d[t * P:(t + 1) * P, :]).then_inc(S_("hf_in"), 16)
            for t in range(NT):
                sp.wait_ge(S_("summed"), t + 1)
                sp.dma_start(out[t * P:(t + 1) * P, :], HF[:, t, :]).then_inc(S_("out_done"), 16)
            sp.wait_ge(S_("out_done"), 16 * NT)

        @block.gpsimd
        def _(g):
            g.memset(AT[:, :], 0.0).then_inc(S_("zeros"), 1)
            g.memset(ident[:, :], 0.0).then_inc(S_("p_a"), 1)
            g.memset(ONES, 1.0).then_inc(S_("ones"), 1)
            for b in BGU + BDN:
                g.memset(b[:, :], 0.0).then_inc(S_("bias_zeros"), 1)
            g.memset(TRIU, 1.0).then_inc(S_("p_a"), 1)
            g.memset(NEGM, 0.0).then_inc(S_("p_a"), 1)
            g.wait_ge(S_("p_a"), 3)
            g.affine_select(out=ident[:, :], in_=ident[:, :], compare_op=ALU.not_equal, fill=1.0, base=0,
                            pattern=[[-1, P]], channel_multiplier=1).then_inc(S_("ident"), 1)
            g.affine_select(out=TRIU, in_=TRIU, compare_op=ALU.is_ge, fill=0.0, base=0,
                            pattern=[[1, P]], channel_multiplier=-1).then_inc(S_("tri"), 1)
            g.affine_select(out=NEGM, in_=NEGM, compare_op=ALU.is_ge, fill=-1e30, base=0,
                            pattern=[[1, P]], channel_multiplier=-1).then_inc(S_("tri"), 1)
            for i, s in enumerate([1] + LEVELS):
                g.memset(MSK[i], 0.0).then_inc(S_("p_b"), 1)
                g.wait_ge(S_("p_b"), 4 * i + 1)
                odd = MSK[i].rearrange("p (b two s) -> p b two s", two=2, s=s)[:, :, 1, :]
                g.memset(odd, 1.0).then_inc(S_("p_b"), 1)
                g.wait_ge(S_("p_b"), 4 * i + 2)
                g.affine_select(out=odd, in_=odd, compare_op=ALU.is_ge, fill=0.0, base=0,
                                pattern=[[-2 * s, P // (2 * s)], [0, s]], channel_multiplier=1).then_inc(S_("p_b"), 1)
                g.wait_ge(S_("p_b"), 4 * i + 3)
                g.affine_select(out=odd, in_=odd, compare_op=ALU.is_ge, fill=0.0, base=s - 1,
                                pattern=[[2 * s, P // (2 * s)], [0, s]], channel_multiplier=-1).then_inc(S_("p_b"), 1)
            g.wait_ge(S_("att_out"), NCH)
            g.wait_ge(S_("dn_act"), 7)
            g.wait_ge(S_("tm_evac"), CHU)
            g.wait_ge(S_("dn_vec"), 5)
            for c in range(NT):
                b = B[c]
                hs = slice(4 * c, 4 * c + 4)
                g.wait_ge(S_("kq_scaled"), 3 * (c + 1) - 2)
                g.tensor_tensor(h4(b["KTE"]), h4(b["KH"]), bc(EGD[:, hs], P), ALU.mult).then_inc(S_("p_c"), 1)
                g.tensor_tensor(h4(b["VB"]), VTM[:, c, :, :], bc(BETA[:, hs], P), ALU.mult).then_inc(S_("p_c"), 1)
                g.wait_ge(S_("kq_scaled"), 3 * (c + 1) - 1)
                g.tensor_tensor(h4(b["KBEG"]), h4(b["KB"]), bc(EG[:, hs], P), ALU.mult).then_inc(S_("p_c"), 1)
                g.wait_ge(S_("p_c"), 3 * c + 3)
                g.wait_ge(S_("kq_scaled"), 3 * (c + 1))
                g.tensor_tensor(h4(b["QE"]), h4(b["QN"]), bc(EG[:, hs], P), ALU.mult).then_inc(S_("scaled_pool"), 1)
            g.wait_ge(S_("outproj"), 2 * NT)
            g.iota(PJI, pattern=[[0, 1]], base=0, channel_multiplier=1).then_inc(S_("consts"), 1)
            g.iota(TOK4, pattern=[[512, 4]], base=0, channel_multiplier=4, allow_small_or_imprecise_dtypes=True).then_inc(S_("consts"), 1)
            g.iota(IO32, pattern=[[1, 32]], base=0, channel_multiplier=0, allow_small_or_imprecise_dtypes=True).then_inc(S_("consts"), 1)
            g.iota(IOM.rearrange("p (a b) -> p a b", a=4), pattern=[[0, 4], [1, 32]], base=0, channel_multiplier=0, allow_small_or_imprecise_dtypes=True).then_inc(S_("consts"), 1)
            g.iota(IOB, pattern=[[1, MAXB + 1]], base=0, channel_multiplier=0, allow_small_or_imprecise_dtypes=True).then_inc(S_("consts"), 1)
            g.memset(ONE32, 1.0).then_inc(S_("consts"), 1)
            g.memset(ONER, 1.0).then_inc(S_("consts"), 1)
            g.memset(STRU, 1.0).then_inc(S_("consts"), 1)
            g.wait_ge(S_("consts"), 8)
            g.affine_select(out=STRU, in_=STRU, compare_op=ALU.is_gt, fill=0.0, base=0,
                            pattern=[[1, P]], channel_multiplier=-1).then_inc(S_("consts"), 1)
            g.wait_ge(S_("lists_done"), 1)
            g.wait_ge(S_("hn_out"), 16 * NT)
            nb = g.value_load(LASTB[0:1, NE - 1:NE], min_val=NE - 1, max_val=MAXB - 1) + 1

            def gather(i):
                g.tensor_copy(IDXC[:, 0:1], IDX[:, bass.ds(i, 1)]).then_inc(S_("idx_cur"), 1)
                g.wait_ge(S_("idx_cur"), i + 1)
                g.sem_inc(S_("pool_passed"), 1)
                g.indirect_dma_start(out=XG[:, :], out_offset=None, in_=hn_d,
                                     in_offset=bass.IndirectOffsetOnAxis(ap=IDXC[:, 0:1], axis=0)).then_inc(S_("gathered"), 16)

            gather(0)
            with g.Fori(1, nb + 1) as i:
                g.wait_ge(S_("xt_ps"), i)
                g.wait_ge(S_("gathered"), i * 16)
                gather(i)
            g.wait_ge(S_("y_out"), (nb + 1) * 16)
            g.sem_inc(S_("pool_passed"), 1)
            for i in range(4 * TOPK):
                g.indirect_dma_start(out=YG[:, i, :], out_offset=None, in_=y_d,
                                     in_offset=bass.IndirectOffsetOnAxis(ap=SLOT[:, i:i + 1], axis=0)).then_inc(S_(f"yg_in{i % 4}"), 16)

        @block.scalar
        def _(a):
            a.dma_start(KWT, rep(kn_w)).then_inc(S_("par_in"), 16)
            a.dma_start(SIG[:, 0:64], rep(qn_w)).then_inc(S_("par_in"), 16)
            for half in range(2):
                a.dma_start(SKT[64 * half:64 * half + 64, :],
                            sinks.rearrange("(g two) -> two g", two=2)[half].partition_broadcast(64),
                            allow_slow_non_contiguous=True).then_inc(S_("par_in"), 16)
            a.dma_start(AL, rep(a_log)).then_inc(S_("par_in"), 16)
            a.dma_start(DTB, rep(dt_bias)).then_inc(S_("par_in"), 16)
            a.dma_start(ZNW, rep(out_norm_w)).then_inc(S_("par_in"), 16)
            a.dma_start(CWR, conv_w.rearrange("j (t c) -> (j t) c", c=P)).then_inc(S_("par_in"), 16)
            rest = (MAXB - NE) * BT // P
            a.wait_ge(S_("zeros"), 1)
            a.dma_start(y_d[NE * BT:, :].rearrange("(p r) n -> p (r n)", p=P).rearrange("p (a n) -> p a n", n=2 * P),
                        AT[:, :].rearrange("p (o n) -> p o n", o=1).to_broadcast([P, rest * D // (2 * P), 2 * P])).then_inc(S_("y_out"), 16)
            for t in range(NT):
                a.wait_ge(S_(f"x_in{t}"), 16)
                if t:
                    a.wait_ge(S_("ssx"), t)
                a.activation(W1[:, 0:D], X[:, t, :], ACT.Square, accum_out=SSX[:, t:t + 1]).then_inc(S_("ssx"), 1)
            a.wait_ge(S_("meansq"), 1)
            a.activation(RSX, SSX, ACT.Sqrt).then_inc(S_("sqrt"), 1)
            for n in range(2 * NT):
                t, half = n // 2, n % 2
                a.wait_ge(S_("ut_ps"), n + 1)
                a.activation(UT[:, 4 * half:4 * half + 4, t * P:(t + 1) * P], h4(PS[n % 2]), ACT.Copy).then_inc(S_("ut_ready"), 1)
            def tok_unit(n):
                s, t = n // NT, n % NT
                w = SLABS[s][1]
                dst = AQ[:, t, 256 * s:256 * s + 256] if s < 3 else DZ[:, t, 260 * (s - 3):260 * (s - 3) + 260]
                a.wait_ge(S_("proj_ps"), n + 1)
                a.activation(dst, PA[n % 2][:, 0:w], ACT.Copy).then_inc(S_("tok_evac"), 1)
            for n in range(12):
                tok_unit(n)
            a.wait_ge(S_("meansq"), 2)
            a.activation(RNA, SSA, ACT.Sqrt).then_inc(S_("sqrt"), 1)
            for n in range(12, TOKU):
                tok_unit(n)
            for t in range(NT):
                a.wait_ge(S_("qk_ps"), t + 1)
                a.activation(QNT[:, 2 * t:2 * t + 2, :, :].rearrange("p c h q -> p h c q"),
                             TA.rearrange("p (h c q) -> p h c q", h=4, c=2), ACT.Copy)
                a.activation(KNT[:, t * P:(t + 1) * P], TB[:, 0:P], ACT.Copy).then_inc(S_("kt_ready"), 1)
            a.activation(BETA.rearrange("p (t h) -> p t h", t=NT), DZ[:, :, 512:516], ACT.Sigmoid).then_inc(S_("dn_act"), 1)
            for t in range(NT):
                if t:
                    a.wait_ge(S_("z_done"), t)
                a.activation(SGZ, DZ[:, t, 0:512], ACT.Sigmoid).then_inc(S_("z_sig"), 1)
            a.wait_ge(S_("dn_vec"), 1)
            a.activation(SPM, SPM, ACT.Exp).then_inc(S_("dn_act"), 1)
            a.activation(AL, AL, ACT.Exp).then_inc(S_("dn_act"), 1)
            a.wait_ge(S_("dn_vec"), 2)
            a.activation(SPM, SPM, ACT.Ln).then_inc(S_("dn_act"), 1)

            def square(n):
                a.wait_ge(S_("tm_evac"), 4 * (n // NT + 1))
                a.wait_ge(S_("z_done"), NT)
                if n >= 2:
                    a.wait_ge(S_("ssq"), n - 1)
                a.activation(h4(SQD[n % 2]), [QTM, KTM][n // NT][:, n % NT, :, :], ACT.Square).then_inc(S_("sq_done"), 1)

            for i in range(CHU + 2):
                if i == 2:
                    a.wait_ge(S_("dn_vec"), 5)
                    a.activation(EG, GC, ACT.Exp).then_inc(S_("dn_act"), 1)
                    a.activation(EGD, EGD, ACT.Exp).then_inc(S_("dn_act"), 1)
                    a.activation(EGL, GLC, ACT.Exp).then_inc(S_("dn_act"), 1)
                if i == CHU:
                    a.wait_ge(S_("meansq"), 3)
                    a.activation(RSQ, SSQ, ACT.Sqrt).then_inc(S_("sqrt"), 1)
                if i < CHU:
                    a.wait_ge(S_("conv"), 4 * i + 4)
                    if i >= 2:
                        a.wait_ge(S_("silu"), i - 1)
                    a.activation(SG[i % 2], CV[i % 2], ACT.Sigmoid).then_inc(S_("sig"), 1)
                if i < NCH:
                    a.wait_ge(S_("shifted"), i + 1)
                    w = P if i else CH
                    pv = PB[i % 2].rearrange("p (g n) -> p g n", g=4)[:, :, 0:w]
                    a.activation(pv, pv, ACT.Exp).then_inc(S_("exps_done"), 1)
                    a.activation(ESK, MNEG, ACT.Exp).then_inc(S_("exps_done"), 1)
                if 1 <= i <= NCH:
                    n = i - 1
                    k = P if n else CH
                    a.wait_ge(S_("pt_ps"), n + 1)
                    if n:
                        a.wait_ge(S_("pv_ps"), n)
                    a.activation(PT[0:k, :], TA[0:k, :], ACT.Copy).then_inc(S_("pt_ready"), 1)
                if 2 <= i:
                    u = i - 2
                    sub, hd = u // 4, u % 4
                    a.wait_ge(S_("st_ps"), u + 1)
                    dst = [QTM, KTM, VTM][sub][:, :, hd, :]
                    a.activation(dst, h4(XP), ACT.Copy).then_inc(S_("tm_evac"), 1)
                if 2 <= i < NCH + 2:
                    n = i - 2
                    a.wait_ge(S_("pv_ps"), n + 1)
                    a.activation(CAT[:, 0:4, n * CH:(n + 1) * CH], AO[:, 0:256].rearrange("p (h q) -> p h q", h=4), ACT.Copy).then_inc(S_("att_out"), 1)
                for n in NORM_AT.get(i, ()):
                    square(n)
            for c in range(NT):
                b = B[c]
                a.wait_ge(S_("dsub"), c + 1)
                a.activation(b["DEC"], b["DEC"], ACT.Exp).then_inc(S_("decay"), 1)
                for i, n in enumerate(("KHT", "KBT", "QNT", "QET")):
                    a.wait_ge(S_("dt_ps"), 4 * c + i + 1)
                    a.activation(b[n], PS[2 + i % 2], ACT.Copy).then_inc(S_("dt_ready"), 1)
            for c in range(NT):
                a.wait_ge(S_("t0_ps"), c + 1)
                a.activation(B[c]["T"], PS[4 + c % 2], ACT.Copy).then_inc(S_("t_ready"), 1)
            for m in range(len(LEVELS) * NT):
                a.wait_ge(S_("p1_ps"), m + 1)
                a.activation(B[m % NT]["P1"], PS[4 + m % 2], ACT.Copy).then_inc(S_("p1_ready"), 1)

            def uw_copies(c):
                a.wait_ge(S_("uw_ps"), 2 * c + 1)
                a.activation(B[c]["USOL"], PS[2], ACT.Copy).then_inc(S_("uw"), 1)
                a.wait_ge(S_("uw_ps"), 2 * c + 2)
                a.activation(B[c]["WT"], PS[3], ACT.Copy).then_inc(S_("uw"), 1)

            def dcat_copy(c):
                a.wait_ge(S_("dcat_ps"), c + 1)
                a.activation(CAT[:, 4:8, c * P:(c + 1) * P], h4(PS[2 + c % 2]), ACT.Copy).then_inc(S_("dcat"), 1)

            uw_copies(0)
            uw_copies(1)
            for i in range(NT + 1):
                if i + 2 < NT:
                    uw_copies(i + 2)
                if i < NT:
                    a.wait_ge(S_("o_ps"), i + 1)
                    a.activation(OB[:, i, :], PS[6 - 2 * (i % 2)], ACT.Copy).then_inc(S_("o_evac"), 1)
                    a.wait_ge(S_("o_evac"), i + 1)
                    a.activation(B[i]["LT"], OB[:, i, :], ACT.Square).then_inc(S_("sq_done"), 1)
                else:
                    dcat_copy(0)
                if i:
                    cs = slice(4 * (i - 1), 4 * i)
                    a.wait_ge(S_("meansq"), 3 + i)
                    a.activation(RSO[:, cs], SSO[:, cs], ACT.Sqrt).then_inc(S_("sqrt"), 1)
            for c in range(1, NT):
                dcat_copy(c)
            for t in range(NT):
                a.wait_ge(S_("h_add"), 2 * t + 2)
                a.activation(HN[:, t, :], H[:, t, :], ACT.Square, accum_out=SSH[:, t:t + 1]).then_inc(S_("ssh"), 1)
                a.wait_ge(S_("meansq"), 8 + t)
                a.activation(RSH[:, t:t + 1], SSH[:, t:t + 1], ACT.Sqrt).then_inc(S_("sqrt"), 1)
                for half in range(2):
                    a.wait_ge(S_("hnt_ps"), 2 * t + half + 1)
                    a.activation(HNT[:, 4 * half:4 * half + 4, t * P:(t + 1) * P], h4(PS[2 + half]), ACT.Copy).then_inc(S_("hnt_ready"), 1)
            a.wait_ge(S_("v_gate"), NT)
            a.activation(GATE[:, :], GATE[:, :], ACT.Exp).then_inc(S_("gexp"), 1)
            a.wait_ge(S_("rank_ps"), 1)
            a.activation(RANK, PS[2][:, 0:P].rearrange("p (t e) -> p t e", t=NT), ACT.Copy).then_inc(S_("rank"), 1)
            a.wait_ge(S_("lists_done"), 1)
            last = a.value_load(LASTB[0:1, NE - 1:NE], min_val=NE - 1, max_val=MAXB - 1)
            nb = last + 1

            def xt_copy(i):
                a.activation(XT[:, :], XPS, ACT.Copy).then_inc(S_("xt_ready"), 1)

            def sigmoid(i):
                a.wait_ge(S_("gate_ready"), i + 1)
                a.wait_ge(S_("act_ready"), i) if not isinstance(i, int) or i else None
                a.activation(SIG[:, :], GU[:, 0:QW], ACT.Sigmoid, scale=ALPHA).then_inc(S_("sig_ready"), 1)

            def at_copy(i):
                a.wait_ge(S_("at_ps"), i + 1)
                a.wait_ge(S_("d_ps"), i + 1)
                a.activation(AT[:, :], ATPS, ACT.Copy).then_inc(S_("at_ready"), 1)

            def y_store(i):
                a.wait_ge(S_("y_ready"), i + 2)
                a.dma_start(y_d[bass.ds(i * BT, BT), :].rearrange("t (j n) -> j t n", j=4), Y[:, :]).then_inc(S_("y_out"), 16)

            a.wait_ge(S_("xt_ps"), 1)
            xt_copy(0)
            a.wait_ge(S_("xt_ps"), 2)
            a.wait_ge(S_("gu_ps"), 1)
            xt_copy(1)
            sigmoid(0)
            a.wait_ge(S_("y_out"), 16)
            with a.Fori(1, nb) as i:
                at_copy(i - 1)
                a.wait_ge(S_("xt_ps"), i + 2)
                a.wait_ge(S_("gu_ps"), i + 1)
                xt_copy(i + 1)
                sigmoid(i)
                y_store(i - 1)
            at_copy(last)
            y_store(last)

        @block.tensor
        def _(pe):
            def mm(o, l, r, st, sp_):
                return pe.matmul(o, l, r, start=st, stop=sp_)

            pe.wait_ge(S_("ident"), 1)
            for n in range(2 * NT):
                t, half = n // 2, n % 2
                if half == 0:
                    pe.wait_ge(S_("u_ready"), t + 1)
                if n >= 2:
                    pe.wait_ge(S_("ut_ready"), n - 1)
                for j in range(4):
                    k = 4 * half + j
                    last = pe.transpose(PS[n % 2][:, j * P:(j + 1) * P], X[:, t, k * P:(k + 1) * P], ident[:, :])
                last.then_inc(S_("ut_ps"), 1)
            pe.wait_ge(S_("par_in"), 16 * 8)
            pe.transpose(XP[:, 0:48], CWR, ident[0:48, 0:48]).then_inc(S_("cw_ps"), 1)
            pe.wait_ge(S_("ut_ready"), 2 * NT)

            def bank_free(n):
                m = n - 2
                if m < 0:
                    return
                if m < TOKU:
                    pe.wait_ge(S_("tok_evac"), m + 1)
                else:
                    pe.wait_ge(S_("conv"), 4 * (m - TOKU) + 4)

            def tok_unit(n):
                s, t = n // NT, n % NT
                w = SLABS[s][1]
                if t == 0:
                    pe.wait_ge(S_(f"slab_in{s % NSL}"), 16 * (s // NSL + 1))
                bank_free(n)
                for k in range(KD):
                    last = mm(PA[n % 2][:, 0:w], UT[:, k, t * P:(t + 1) * P], SL[s % NSL][:, k, 0:w], k == 0, k == KD - 1)
                last.then_inc(S_("proj_ps"), 1)
                if t == NT - 1:
                    pe.wait_ge(S_("cw_evac"), 1)
                    pe.transpose(XP[:, 0:48], CWR, ident[0:48, 0:48]).then_inc(S_("slab_used"), 1)

            for n in range(TOKU):
                tok_unit(n)

            def conv_unit(i):
                n, s = TOKU + i, 5 + i // 2
                if i % 2 == 0:
                    pe.wait_ge(S_(f"slab_in{s % NSL}"), 16 * (s // NSL + 1))
                bank_free(n)
                for k in range(KD):
                    last = mm(PA[n % 2], SL[s % NSL][:, k, (i % 2) * P:(i % 2) * P + P], UT[:, k, :], k == 0, k == KD - 1)
                last.then_inc(S_("proj_ps"), 1)

            conv_unit(0)
            for t in range(NT):
                pe.wait_ge(S_("qkn"), 3 * t + 3)
                if t:
                    pe.wait_ge(S_("kt_ready"), t)
                q = QNB[t % 2]
                for h in range(4):
                    pe.transpose(TA[:, h * P:(h + 1) * P], q[:, h * P:(h + 1) * P], ident[:, :])
                pe.transpose(TB[:, 0:P], q[:, 512:640], ident[:, :]).then_inc(S_("qk_ps"), 1)
            pe.wait_ge(S_("kt_ready"), NT)
            pe.wait_ge(S_("avs_in"), 16 * 6)
            for i in range(CHU + 2):
                if i < CHU:
                    if i:
                        conv_unit(i)
                    if i % 2:
                        pe.transpose(TB[:, 0:P], ident[:, :], ident[:, :]).then_inc(S_("slab_used"), 1)
                if 2 <= i < NCH + 2:
                    n = i - 2
                    pe.wait_ge(S_("pt_ready"), n + 1)
                    if n:
                        pe.wait_ge(S_("att_out"), n)
                    else:
                        pe.wait_ge(S_("dn_vec"), 4)
                    k = P if n else CH
                    v = AQ[0:k, (n - 1) // 2 if n else 0, 640:768] if n % 2 or n == 0 else AVS[:, n // 2 - 1, :]
                    for kv in range(KV):
                        last = mm(AO[64 * kv:64 * kv + 64, 0:256], v[:, 64 * kv:64 * kv + 64], PT[0:k, 256 * kv:256 * kv + 256], True, True)
                    last.then_inc(S_("pv_ps"), 1)
                if i < NCH:
                    if i == 1:
                        pe.wait_ge(S_("tri"), 2)
                        pe.wait_ge(S_("ones"), 1)
                        pe.wait_ge(S_("dn_vec"), 3)
                        mm(AO[:, 0:16], TRIU, GV, True, True)
                        mm(AO[:, 16:32], ONES, GV, True, True).then_inc(S_("g_ps"), 1)
                    if i:
                        pe.wait_ge(S_("shifted"), i)
                    k0, k1 = (i - 1) * CH if i else 0, (i + 1) * CH
                    for kv in range(KV):
                        rows = slice(64 * kv, 64 * kv + 64)
                        for hp in range(2):
                            last = mm(PSC[:, kv, hp * P:hp * P + k1 - k0],
                                      QNT[rows, i, 2 * hp:2 * hp + 2, :].rearrange("p h q -> p (h q)"), KNT[rows, k0:k1], True, True)
                    last.then_inc(S_("sc_ps"), 1)
                if 1 <= i <= NCH:
                    n = i - 1
                    pe.wait_ge(S_("pnorm"), n + 1)
                    if n:
                        pe.wait_ge(S_("pt_ready"), n)
                    k = P if n else CH
                    for g in range(4):
                        last = pe.transpose(TA[0:k, g * P:(g + 1) * P], PB[n % 2][:, g * P:g * P + k], ident[:, :])
                    last.then_inc(S_("pt_ps"), 1)
                if 2 <= i:
                    u = i - 2
                    pe.wait_ge(S_("silu"), u + 1)
                    if u:
                        pe.wait_ge(S_("tm_evac"), u)
                    else:
                        pe.wait_ge(S_("cw_evac"), 1)
                    for t in range(NT):
                        last = pe.transpose(XP[:, t * P:(t + 1) * P], ST[u % 2][:, t * P:(t + 1) * P], ident[:, :])
                    last.then_inc(S_("st_ps"), 1)
            def headwise(bank, sem, l, r):
                for h in range(HD):
                    hs = slice(h * P, (h + 1) * P)
                    last = mm(bank[:, hs], l[:, hs], r[:, hs], True, True)
                last.then_inc(S_(sem), 1)

            def dt(c, i, n, ready, count):
                m = 4 * c + i
                pe.wait_ge(S_(ready), count)
                if m >= 2:
                    pe.wait_ge(S_("dt_ready"), m - 1)
                for h in range(HD):
                    last = pe.transpose(PS[2 + m % 2][:, h * P:(h + 1) * P], B[c][n][:, h * P:(h + 1) * P], ident[:, :])
                last.then_inc(S_("dt_ps"), 1)

            def li(c):
                pe.wait_ge(S_("dt_ready"), 4 * c + 3)
                if c:
                    pe.wait_ge(S_("li"), 2 * c)
                headwise(PS[0], "li_ps", B[c]["KHT"], B[c]["KBT"])
                headwise(PS[1], "li_ps", B[c]["KHT"], B[c]["QNT"])

            pe.wait_ge(S_("att_out"), NCH)
            pe.wait_ge(S_("tm_evac"), CHU)
            for c in range(NT):
                if c:
                    pe.wait_ge(S_("dsub"), c)
                for h in range(HD):
                    last = mm(XP[:, h * P:(h + 1) * P], GV[:, 4 * c + h:4 * c + h + 1].to_broadcast([P, P]), TRIU, True, True)
                last.then_inc(S_("grow_ps"), 1)
                dt(c, 0, "KH", "kq_scaled", 3 * c + 1)
                dt(c, 1, "KB", "kq_scaled", 3 * c + 2)
                dt(c, 2, "QN", "kq_scaled", 3 * c + 3)
                if c:
                    li(c - 1)
                dt(c, 3, "QE", "scaled_pool", c + 1)
            li(NT - 1)
            for c in range(NT):
                pe.wait_ge(S_("u_init"), c + 1)
                if c >= 2:
                    pe.wait_ge(S_("t_ready"), c - 1)
                for h in range(HD):
                    hs = slice(h * P, (h + 1) * P)
                    last = pe.transpose(PS[4 + c % 2][:, hs], B[c]["U"][:, hs], ident[:, :])
                last.then_inc(S_("t0_ps"), 1)
            pe.wait_ge(S_("t_ready"), NT)
            pe.wait_ge(S_("li"), 2 * NT)
            for m in range(len(LEVELS) * NT + 1):
                if m < len(LEVELS) * NT:
                    b = B[m % NT]
                    pe.wait_ge(S_("ct"), m + 1)
                    if m >= NT:
                        pe.wait_ge(S_("t_upd"), m - NT + 1)
                    headwise(PS[4 + m % 2], "p1_ps", b["CT"], b["T"])
                if m:
                    n = m - 1
                    b = B[n % NT]
                    pe.wait_ge(S_("p1_ready"), n + 1)
                    if n >= 2:
                        pe.wait_ge(S_("u_upd"), n - 1)
                    if n < (len(LEVELS) - 1) * NT:
                        headwise(PS[6] if n % 2 == 0 else PS[0], "p2_ps", b["U"], b["P1"])
                    headwise(PS[7] if n % 2 == 0 else PS[1], "p2t_ps", b["P1"], b["U"])

            def uw(c):
                pe.wait_ge(S_("u_upd"), (len(LEVELS) - 1) * NT + c + 1)
                pe.wait_ge(S_("uw") if c else S_("dt_ready"), 2 * c if c else 4 * NT)
                headwise(PS[2], "uw_ps", B[c]["U"], B[c]["VB"])
                headwise(PS[3], "uw_ps", B[c]["KBEG"], B[c]["U"])

            def dcat(c):
                pe.wait_ge(S_("dn_out"), c + 1)
                if c >= 2:
                    pe.wait_ge(S_("dcat"), c - 1)
                for h in range(HD):
                    last = pe.transpose(PS[2 + c % 2][:, h * P:(h + 1) * P], OB[:, c, h * P:(h + 1) * P], ident[:, :])
                last.then_inc(S_("dcat_ps"), 1)

            uw(0)
            uw(1)
            pe.wait_ge(S_("u_upd"), len(LEVELS) * NT)
            for c in range(NT):
                b, state = B[c], STATES[c % 2]
                if c:
                    pe.wait_ge(S_("uw"), 2 * c + 2)
                    pe.wait_ge(S_("state"), c)
                    headwise(PS[7], "ws_ps", b["WT"], state)
                if c + 2 < NT:
                    uw(c + 2)
                pe.wait_ge(S_("vnew"), c + 1)
                if c < NT - 1:
                    headwise(PS[5], "kv_ps", b["KTE"], b["VN"])
                if c >= 2:
                    pe.wait_ge(S_("o_evac"), c - 1)
                for h in range(HD):
                    hs = slice(h * P, (h + 1) * P)
                    o = PS[6 - 2 * (c % 2)][:, hs]
                    if c:
                        mm(o, b["QET"][:, hs], state[:, hs], True, False)
                    last = mm(o, b["INT"][:, hs], b["VN"][:, hs], c == 0, True)
                last.then_inc(S_("o_ps"), 1)
            pe.wait_ge(S_("uw"), 2 * NT)
            dcat(0)
            pe.wait_ge(S_("wo_in"), 16 * 3)

            def hn_transposes(t):
                pe.wait_ge(S_("hn_ready"), t + 1)
                pe.wait_ge(S_("dcat"), NT)
                for half in range(2):
                    if t:
                        pe.wait_ge(S_("hnt_ready"), 2 * t - 1 + half)
                    for j in range(4):
                        k = 4 * half + j
                        last = pe.transpose(PS[2 + half][:, j * P:(j + 1) * P], HN[:, t, k * P:(k + 1) * P], ident[:, :])
                    last.then_inc(S_("hnt_ps"), 1)

            def logits(t):
                pe.wait_ge(S_("hnt_ready"), 2 * t + 2)
                if t:
                    pe.wait_ge(S_("logits"), t)
                for k in range(KD):
                    last = mm(PS[5][:, 0:NE], HNT[:, k, t * P:(t + 1) * P], RW[:, k, :], k == 0, k == KD - 1)
                last.then_inc(S_("lg_ps"), 1)

            for n in range(2 * NT):
                t, half = n // 2, n % 2
                if half == 0:
                    pe.wait_ge(S_("dcat"), t + 1)
                if n >= 2:
                    pe.wait_ge(S_("h_add"), n - 1)
                for k in range(KD):
                    w = WO0[:, k, :] if k < 4 else WO1[:, k - 4, :]
                    last = mm(PS[n % 2], CAT[:, k, t * P:(t + 1) * P], w[:, half * 512:half * 512 + 512], k == 0, k == KD - 1)
                last.then_inc(S_("outproj"), 1)
                if n < NT - 1:
                    dcat(n + 1)
                if half and t:
                    hn_transposes(t - 1)
                if half == 0 and t > 1:
                    if t == 2:
                        pe.wait_ge(S_("res_in"), 16 * (NT + 3))
                    logits(t - 2)
            logits(2)
            hn_transposes(3)
            logits(3)
            pe.wait_ge(S_("mask"), NT)
            pe.wait_ge(S_("consts"), 9)
            pe.wait_ge(S_("hnt_ready"), 2 * NT)
            for t in range(NT):
                for s in range(t):
                    mm(PS[2][:, t * NE:(t + 1) * NE], ONER, MASK[:, s, :], s == 0, False)
                mm(PS[2][:, t * NE:(t + 1) * NE], STRU, MASK[:, t, :], t == 0, True)
            for s in range(NT):
                last = mm(PS[3][:, 0:NE], ONER, MASK[:, s, :], s == 0, s == NT - 1)
            last.then_inc(S_("rank_ps"), 1)
            for i in range(4 * TOPK):
                pe.wait_ge(S_("onehots"), 2 * i + 2)
                last = mm(PS[4][:, 0:MAXB + 1], T1[i % 2], B1[i % 2], i == 0, i == 4 * TOPK - 1)
                last.then_inc(S_("list_ps"), 1)
            pe.wait_ge(S_("gathered"), 16)

            def x_transposes(i):
                for half in range(2):
                    last = pe.transpose(XPS[:, half * P:(half + 1) * P], XG[:, half * P:(half + 1) * P], ident[:, :])
                last.then_inc(S_("xt_ps"), 1)

            def gate_up(i, p, rnd, first_of_expert, first):
                pe.wait_ge(S_("xt_ready"), i + 1)
                if not first:
                    pe.wait_ge(S_("gu_evac"), i)
                for k in range(KD):
                    if first_of_expert and k % 2 == 0:
                        pe.wait_ge(S_(f"gu_in{p}{k // 2}"), rnd)
                    if k == 5:
                        pe.wait_ge(S_("gathered"), (i + 2) * 16)
                        x_transposes(i + 1)
                        if not first:
                            pe.wait_ge(S_("act_ready"), i)
                            act_transposes()
                    for j in range(4):
                        rhs = GUW[p][:, k, :].rearrange("p (g n) -> p g n", g=2)[:, :, j * QW:(j + 1) * QW]
                        last = pe.matmul(GPS[32 * j:32 * j + 32, :].rearrange("p (g n) -> p g n", g=2),
                                         XT[:, (k % 2) * P + (k // 2) * 32:(k % 2) * P + (k // 2) * 32 + 32], rhs,
                                         start=(k == 0), stop=(k == KD - 1), tile_position=(0, 32 * j), skip_group_check=True)
                    if k % 2:
                        last.then_inc(S_(f"gu_read{k // 2}" if k < KD - 1 else "gu_ps"), 1)

            def act_transposes():
                for half in range(2):
                    last = pe.transpose(ATPS[:, half * P:(half + 1) * P], GU[:, half * P:(half + 1) * P], ident[:, :])
                last.then_inc(S_("at_ps"), 1)

            def down(i, p, rnd):
                pe.wait_ge(S_("at_ready"), i + 1)
                pe.wait_ge(S_("y_ready"), i + 1)
                if rnd is not None:
                    pe.wait_ge(S_(f"dn_in{p}0"), rnd)
                    pe.wait_ge(S_(f"dn_in{p}1"), rnd)
                for k in range(KD):
                    for j in range(4):
                        last = pe.matmul(DPS[32 * j:32 * j + 32, :],
                                         AT[:, (k % 2) * P + (k // 2) * 32:(k % 2) * P + (k // 2) * 32 + 32],
                                         DNW[p][:, k, j * QW:(j + 1) * QW],
                                         start=(k == 0), stop=(k == KD - 1), tile_position=(0, 32 * j), skip_group_check=True)
                    if k == KD // 2 - 1:
                        last.then_inc(S_("dn_read"), 1)
                last.then_inc(S_("d_ps"), 1)

            def more_blocks(e, p, before, rnd):
                last = pe.value_load(LASTB[0:1, bass.ds(e, 1)], min_val=0, max_val=MAXB - 1)
                with pe.If(last > before + 1):
                    with pe.Fori(before + 2, last + 1) as i:
                        gate_up(i, p, rnd, False, False)
                        down(i - 1, p, rnd)
                return last

            def expert(e, p, before, rnd, prnd):
                gate_up(before + 1, p, rnd, True, False)
                down(before, 1 - p, prnd)
                return more_blocks(e, p, before, rnd)

            pe.transpose(RPS, ident[:, :], ident[:, :]).then_inc(S_("d_ps"), 1)
            x_transposes(0)
            gate_up(0, 0, 16, True, True)
            last = pe.value_load(LASTB[0:1, 0:1], min_val=0, max_val=MAXB - 1)
            with pe.If(last > 0):
                gate_up(1, 0, 16, False, False)
                down(0, 0, 16)
            with pe.If(last > 1):
                with pe.Fori(2, last + 1) as i:
                    gate_up(i, 0, 16, False, False)
                    down(i - 1, 0, 16)

            with pe.Fori(0, NE // 2 - 1) as r:
                last = pe.value_load(LASTB[0:1, bass.ds(2 * r, 1)], min_val=0, max_val=MAXB - 1)
                last = expert(2 * r + 1, 1, last, (r + 1) * 16, (r + 1) * 16)
                expert(2 * r + 2, 0, last, (r + 2) * 16, (r + 1) * 16)
            last = pe.value_load(LASTB[0:1, NE - 2:NE - 1], min_val=0, max_val=MAXB - 1)
            last = expert(NE - 1, 1, last, NE * 8, NE * 8)
            pe.wait_ge(S_("act_ready"), last + 1)
            act_transposes()
            down(last, 1, NE * 8)

        @block.vector
        def _(v):
            stt, tt, ts = v.scalar_tensor_tensor, v.tensor_tensor, v.tensor_scalar
            chain = [0]

            def link(ins):
                chain[0] += 1
                ins.then_inc(S_("v_chain"), 1)
                v.wait_ge(S_("v_chain"), chain[0])

            v.wait_ge(S_("ssx"), NT)
            ts(SSX, SSX, 1.0 / D, EPS, ALU.mult, ALU.add).then_inc(S_("meansq"), 1)
            v.wait_ge(S_("sqrt"), 1)
            link(v.reciprocal(RSX, RSX))
            v.wait_ge(S_("nw_in"), 16)
            for t in range(NT):
                stt(out=X[:, t, :], in0=X[:, t, :], scalar=RSX[:, t:t + 1], in1=NW, op0=ALU.mult, op1=ALU.mult).then_inc(S_("u_ready"), 1)
            v.wait_ge(S_("cw_ps"), 1)
            v.tensor_copy(CW, XP[:, 0:48]).then_inc(S_("cw_evac"), 1)
            v.wait_ge(S_("par_in"), 16 * 8)
            link(stt(out=KWT, in0=KWT, scalar=DH ** -0.5, in1=SIG[:, 0:64], op0=ALU.mult, op1=ALU.mult))
            for t in range(NT):
                v.wait_ge(S_("tok_evac"), 2 * NT + t + 1)
                link(tt(SQA, AQ[:, t, 0:640], AQ[:, t, 0:640], ALU.mult))
                link(v.tensor_reduce(SSA[:, 10 * t:10 * t + 10], SQA.rearrange("p (h n) -> p h n", h=10), AX.X, ALU.add))
            ts(SSA, SSA, 1.0 / DH, EPS, ALU.mult, ALU.add).then_inc(S_("meansq"), 1)
            v.wait_ge(S_("sqrt"), 2)
            link(v.reciprocal(RNA, RNA))
            for t in range(NT):
                if t >= 2:
                    v.wait_ge(S_("qk_ps"), t - 1)
                q = QNB[t % 2]
                tt(q[:, 0:512].rearrange("p (h g d) -> p g h d", h=4, g=2),
                   AQ[:, t, 0:512].rearrange("p (g h d) -> p g h d", g=2, h=4),
                   RNA[:, 10 * t:10 * t + 8].rearrange("p (g h o) -> p g h o", g=2, o=1).to_broadcast([P, 2, 4, 64]), ALU.mult).then_inc(S_("qkn"), 1)
                k = q[:, 512:640].rearrange("p (g d) -> p g d", g=2)
                tt(k, AQ[:, t, 512:640].rearrange("p (g d) -> p g d", g=2), bc(RNA[:, 10 * t + 8:10 * t + 10], 64), ALU.mult).then_inc(S_("qkn"), 1)
                v.wait_ge(S_("qkn"), 3 * t + 2)
                tt(k, k, bm(KWT, 2), ALU.mult).then_inc(S_("qkn"), 1)
            for t in range(NT):
                v.wait_ge(S_("z_sig"), t + 1)
                tt(DZ[:, t, 0:512], DZ[:, t, 0:512], SGZ, ALU.mult).then_inc(S_("z_done"), 1)
            v.wait_ge(S_("z_done"), NT)
            for t in range(NT):
                tt(h4(DZ[:, t, 0:512]), h4(DZ[:, t, 0:512]), bm(ZNW, HD), ALU.mult).then_inc(S_("zw"), 1)

            link(tt(SPT.rearrange("p (t h) -> p t h", t=NT), DZ[:, :, 516:520], bm(DTB, NT), ALU.add))
            link(ts(SPM, SPT, -1.0, None, ALU.mult))
            tt(SPM, SPM, SPT, ALU.min).then_inc(S_("dn_vec"), 1)
            v.wait_ge(S_("dn_vec"), 1)
            link(ts(SPT, SPT, 0.0, None, ALU.max))
            v.wait_ge(S_("dn_act"), 2)
            ts(SPM, SPM, 1.0, None, ALU.add).then_inc(S_("dn_vec"), 1)
            v.wait_ge(S_("dn_act"), 4)
            link(tt(SPT, SPT, SPM, ALU.add))
            v.wait_ge(S_("dn_act"), 3)
            link(ts(AL, AL, -1.0, None, ALU.mult))
            tt(GV.rearrange("p (t h) -> p t h", t=NT), SPT.rearrange("p (t h) -> p t h", t=NT), bm(AL, NT), ALU.mult).then_inc(S_("dn_vec"), 1)

            def taps(i):
                n = TOKU + i
                v.wait_ge(S_("proj_ps"), n + 1)
                if i >= 2:
                    v.wait_ge(S_("sig"), i - 1)
                    v.wait_ge(S_("silu"), i - 1)
                src, cv = PA[n % 2], CV[i % 2]
                ts(cv, src, CW[:, 36 + i:37 + i], None, ALU.mult).then_inc(S_("conv"), 1)
                for j in range(1, 4):
                    v.wait_ge(S_("conv"), 4 * i + j)
                    col = (3 - j) * 12 + i
                    stt(out=cv[:, j:S], in0=src[:, 0:S - j], scalar=CW[:, col:col + 1], in1=cv[:, j:S],
                        op0=ALU.mult, op1=ALU.add).then_inc(S_("conv"), 1)

            def silu(i):
                v.wait_ge(S_("sig"), i + 1)
                if i >= 2:
                    v.wait_ge(S_("st_ps"), i - 1)
                tt(ST[i % 2], CV[i % 2], SG[i % 2], ALU.mult).then_inc(S_("silu"), 1)

            def softmax_a(n):
                w = P if n else CH
                v.wait_ge(S_("sc_ps"), n + 1)
                if n >= 2:
                    v.wait_ge(S_("pt_ps"), n - 1)
                if n:
                    v.wait_ge(S_("shifted"), n)
                sc = PSC[:, :, 0:256].rearrange("p k (h n) -> p k h n", h=2)[:, :, :, 0:w]
                link(v.tensor_reduce(MXS.rearrange("p (k h) -> p k h", k=2), sc, AX.X, ALU.max))
                link(tt(MXS, MXS, SKT, ALU.max))
                link(tt(MNEG, SKT, MXS, ALU.subtract))
                pb = PB[n % 2].rearrange("p (k h n) -> p k h n", k=2, h=2)[:, :, :, 0:w]
                tt(pb, sc, MXS.rearrange("p (k h o) -> p k h o", k=2, o=1).to_broadcast([P, 2, 2, w]), ALU.subtract).then_inc(S_("shifted"), 1)

            def softmax_b(n):
                w = P if n else CH
                pb = PB[n % 2].rearrange("p (g n) -> p g n", g=4)[:, :, 0:w]
                v.wait_ge(S_("exps_done"), 2 * (n + 1) - 1)
                if n:
                    v.wait_ge(S_("pnorm"), n)
                link(v.tensor_reduce(DEN, pb, AX.X, ALU.add))
                v.wait_ge(S_("exps_done"), 2 * (n + 1) - 0)
                link(tt(DEN, DEN, ESK, ALU.add))
                link(v.reciprocal(RDEN, DEN))
                tt(pb, pb, bc(RDEN, w), ALU.mult).then_inc(S_("pnorm"), 1)

            for i in range(CHU + 1):
                if i < CHU:
                    taps(i)
                if i < NCH:
                    softmax_a(i)
                if i >= 1:
                    silu(i - 1)
                if i < NCH:
                    softmax_b(i)
                if i == 1:
                    v.wait_ge(S_("g_ps"), 1)
                    link(v.tensor_copy(GC, AO[:, 0:16]))
                    v.tensor_copy(GLC, AO[:, 16:32]).then_inc(S_("dn_vec"), 1)
                    v.wait_ge(S_("dn_vec"), 4)
                    tt(EGD, GLC, GC, ALU.subtract).then_inc(S_("dn_vec"), 1)
                for n in NORM_AT.get(i, ()):
                    at = 8 * (n % NT) + 4 * (n // NT)
                    v.wait_ge(S_("sq_done"), n + 1)
                    v.tensor_reduce(SSQ[:, at:at + 4], h4(SQD[n % 2]), AX.X, ALU.add).then_inc(S_("ssq"), 1)
                if i == CHU - 1:
                    v.wait_ge(S_("ssq"), 8)
                    ts(SSQ, SSQ, EPS, None, ALU.add).then_inc(S_("meansq"), 1)
            v.wait_ge(S_("sqrt"), 3)
            link(v.reciprocal(RSQ, RSQ))
            link(ts(RSQ.rearrange("p (c s h) -> p c s h", c=NT, s=2)[:, :, 0, :], RSQ.rearrange("p (c s h) -> p c s h", c=NT, s=2)[:, :, 0, :],
                    float(P) ** -0.5, None, ALU.mult))
            v.wait_ge(S_("dn_act"), 1)
            v.wait_ge(S_("att_out"), NCH)
            v.wait_ge(S_("tri"), 2)
            v.wait_ge(S_("p_b"), 28)
            v.wait_ge(S_("tm_evac"), CHU)

            def scaled(c):
                b = B[c]
                hs = slice(4 * c, 4 * c + 4)
                tt(h4(b["KH"]), KTM[:, c, :, :], bc(RSQ[:, 8 * c + 4:8 * c + 8], P), ALU.mult).then_inc(S_("kq_scaled"), 1)
                v.wait_ge(S_("kq_scaled"), 3 * c + 1)
                tt(h4(b["KB"]), h4(b["KH"]), bc(BETA[:, hs], P), ALU.mult).then_inc(S_("kq_scaled"), 1)
                tt(h4(b["QN"]), QTM[:, c, :, :], bc(RSQ[:, 8 * c:8 * c + 4], P), ALU.mult).then_inc(S_("kq_scaled"), 1)
                v.wait_ge(S_("grow_ps"), c + 1)
                link(tt(h4(b["DEC"]), h4(XP), bc(GC[:, hs], P), ALU.subtract))
                tt(h4(b["DEC"]), h4(b["DEC"]), bm(NEGM, HD), ALU.add).then_inc(S_("dsub"), 1)

            def decayed(c):
                b = B[c]
                v.wait_ge(S_("decay"), c + 1)
                v.wait_ge(S_("li_ps"), 2 * c + 1)
                tt(b["LT"], PS[0], b["DEC"], ALU.mult).then_inc(S_("li"), 1)
                v.wait_ge(S_("li_ps"), 2 * c + 2)
                v.wait_ge(S_("scaled_pool"), c + 1)
                tt(b["INT"], PS[1], b["DEC"], ALU.mult).then_inc(S_("li"), 1)
                v.wait_ge(S_("li"), 2 * c + 1)
                link(tt(h4(b["CT"]), h4(b["LT"]), bm(MSK[0], HD), ALU.mult))
                tt(h4(b["U"]), bm(ident[:, :], HD), h4(b["CT"]), ALU.subtract).then_inc(S_("u_init"), 1)
                v.wait_ge(S_("u_init"), c + 1)
                tt(h4(b["CT"]), h4(b["LT"]), bm(MSK[1], HD), ALU.mult).then_inc(S_("ct"), 1)

            for c in range(NT + 1):
                if c < NT:
                    scaled(c)
                if c:
                    decayed(c - 1)
            for m in range(len(LEVELS) * NT):
                b, lv = B[m % NT], m // NT
                if lv < len(LEVELS) - 1:
                    v.wait_ge(S_("p2_ps"), m + 1)
                    tt(b["T"], b["T"], PS[6] if m % 2 == 0 else PS[0], ALU.subtract).then_inc(S_("t_upd"), 1)
                v.wait_ge(S_("p2t_ps"), m + 1)
                tt(b["U"], b["U"], PS[7] if m % 2 == 0 else PS[1], ALU.subtract).then_inc(S_("u_upd"), 1)
                if lv < len(LEVELS) - 1:
                    tt(h4(b["CT"]), h4(b["LT"]), bm(MSK[lv + 2], HD), ALU.mult).then_inc(S_("ct"), 1)
            v.wait_ge(S_("dn_act"), 7)
            v.wait_ge(S_("zw"), NT)
            for i in range(NT + 2):
                if i < NT:
                    b, old, new = B[i], STATES[i % 2], STATES[(i + 1) % 2]
                    v.wait_ge(S_("uw"), 2 * i + 1)
                    if i:
                        v.wait_ge(S_("ws_ps"), i)
                        tt(b["VN"], b["USOL"], PS[7], ALU.subtract).then_inc(S_("vnew"), 1)
                    else:
                        v.tensor_copy(b["VN"], b["USOL"]).then_inc(S_("vnew"), 1)
                    if 0 < i < NT - 1:
                        v.wait_ge(S_("o_ps"), i)
                        v.wait_ge(S_("state"), i)
                        link(tt(h4(new), h4(old), bc(EGL[:, 4 * i:4 * i + 4], P), ALU.mult))
                        v.wait_ge(S_("kv_ps"), i + 1)
                        tt(new, new, PS[5], ALU.add).then_inc(S_("state"), 1)
                    if i == 0:
                        v.wait_ge(S_("kv_ps"), 1)
                        v.tensor_copy(new, PS[5]).then_inc(S_("state"), 1)
                if 1 <= i <= NT:
                    c = i - 1
                    v.wait_ge(S_("sq_done"), 8 + c + 1)
                    v.tensor_reduce(SSO[:, 4 * c:4 * c + 4], h4(B[c]["LT"]), AX.X, ALU.add).then_inc(S_("ssq"), 1)
                    v.wait_ge(S_("ssq"), 8 + c + 1)
                    ts(SSO[:, 4 * c:4 * c + 4], SSO[:, 4 * c:4 * c + 4], 1.0 / P, EPS, ALU.mult, ALU.add).then_inc(S_("meansq"), 1)
                if i >= 2:
                    c = i - 2
                    v.wait_ge(S_("sqrt"), 4 + c)
                    link(v.reciprocal(RSO[:, 4 * c:4 * c + 4], RSO[:, 4 * c:4 * c + 4]))
                    link(tt(h4(OB[:, c, :]), h4(OB[:, c, :]), bc(RSO[:, 4 * c:4 * c + 4], P), ALU.mult))
                    tt(OB[:, c, :], OB[:, c, :], DZ[:, c, 0:512], ALU.mult).then_inc(S_("dn_out"), 1)
            v.wait_ge(S_("res_in"), 16 * (NT + 3))

            def top4(t):
                v.wait_ge(S_("lg_ps"), t + 1)
                tt(LG[:, t, :], PS[5][:, 0:NE], RB, ALU.add).then_inc(S_("logits"), 1)
                v.wait_ge(S_("logits"), t + 1)
                link(v.max(MX8[:, t, :], LG[:, t, :]))
                link(v.max_index(MI8[:, t, :], MX8[:, t, :], LG[:, t, :]))
                link(v.tensor_copy(MIF[:, t, :], MI8[:, t, :]))

            for t in range(NT):
                for half in range(2):
                    v.wait_ge(S_("outproj"), 2 * t + half + 1)
                    hh = H[:, t, half * 512:half * 512 + 512]
                    tt(hh, hh, PS[half], ALU.add).then_inc(S_("h_add"), 1)
                v.wait_ge(S_("h_add"), 2 * t + 2)
                v.wait_ge(S_("ssh"), t + 1)
                ts(SSH[:, t:t + 1], SSH[:, t:t + 1], 1.0 / D, EPS, ALU.mult, ALU.add).then_inc(S_("meansq"), 1)
                v.wait_ge(S_("sqrt"), 8 + t)
                link(v.reciprocal(RSH[:, t:t + 1], RSH[:, t:t + 1]))
                stt(out=HN[:, t, :], in0=H[:, t, :], scalar=RSH[:, t:t + 1], in1=FW, op0=ALU.mult, op1=ALU.mult).then_inc(S_("hn_ready"), 1)
                if t >= 2:
                    top4(t - 2)
            for t in (2, 3):
                top4(t)
            for t in range(NT):
                ts(GATE[:, 4 * t:4 * t + 4], MX8[:, t, 0:4], MX8[:, t, 0:1], None, ALU.subtract).then_inc(S_("v_gate"), 1)
            v.wait_ge(S_("v_gate"), NT)
            v.wait_ge(S_("consts"), 9)
            for t in range(NT):
                for k in range(TOPK):
                    ts(OH[:, t, k, :], IO32, MIF[:, t, k:k + 1], None, ALU.is_equal).then_inc(S_("v_oh"), 1)
                v.wait_ge(S_("v_oh"), 4 * t + 4)
                v.tensor_reduce(MASK[:, t, :], OH[:, t, :, :].rearrange("p k e -> p e k"), AX.X, ALU.add).then_inc(S_("mask"), 1)
            v.wait_ge(S_("gexp"), 1)
            link(v.tensor_reduce(GSUM, GATE[:, :].rearrange("p (t k) -> p t k", t=NT), AX.X, ALU.add))
            link(v.reciprocal(GREC, GSUM))
            link(tt(GATE[:, :].rearrange("p (t k) -> p t k", t=NT), GATE[:, :].rearrange("p (t k) -> p t k", t=NT), bc(GREC, TOPK), ALU.mult))
            v.wait_ge(S_("rank_ps"), 1)
            link(ts(NBI, PS[3][:, 0:NE], float(BT - 1), None, ALU.add))
            link(ts(NBI, NBI, 5, None, ALU.logical_shift_right))
            link(ts(NBF, NBI, 1.0, None, ALU.max))
            link(v.tensor_tensor_scan(BEF, ONE32, NBF, 0.0, ALU.mult, ALU.add))
            link(ts(LASTB[:, :], BEF, -1.0, None, ALU.add))
            link(tt(BSF, BEF, NBF, ALU.subtract))
            v.wait_ge(S_("rank"), 1)
            for t in range(NT):
                link(tt(OHR[:, t, :, :], OH[:, t, :, :], bm(RANK[:, t, :], TOPK), ALU.mult))
            link(v.tensor_reduce(RK.rearrange("p (t k) -> p t k", t=NT), OHR, AX.X, ALU.add))
            for t in range(NT):
                link(tt(OHR[:, t, :, :], OH[:, t, :, :], bm(BSF, TOPK), ALU.mult))
            link(v.tensor_reduce(BSK.rearrange("p (t k) -> p t k", t=NT), OHR, AX.X, ALU.add))
            link(v.tensor_copy(RKI, RK))
            link(ts(RKI, RKI, 5, None, ALU.logical_shift_right))
            link(v.tensor_copy(RKB, RKI))
            link(stt(out=TPOS, in0=RKB, scalar=-float(BT), in1=RK, op0=ALU.mult, op1=ALU.add))
            link(tt(BLK, BSK, RKB, ALU.add))
            link(stt(out=SLOT[:, :], in0=BSK, scalar=float(BT), in1=RK, op0=ALU.mult, op1=ALU.add))
            for i in range(4 * TOPK):
                if i >= 2:
                    v.wait_ge(S_("list_ps"), i - 1)
                t = i // TOPK
                ts(T1[i % 2], IOM, TPOS[:, i:i + 1], TOK4[:, t:t + 1], ALU.is_equal, ALU.mult).then_inc(S_("onehots"), 1)
                ts(B1[i % 2], IOB, BLK[:, i:i + 1], None, ALU.is_equal).then_inc(S_("onehots"), 1)
            link(ts(PJI, PJI, 5, None, ALU.logical_shift_right))
            link(v.tensor_copy(PJ, PJI))
            v.wait_ge(S_("list_ps"), 4 * TOPK)
            ts(IDX[:, :], PS[4][:, 0:MAXB + 1], PJ, None, ALU.add).then_inc(S_("lists_done"), 1)
            v.wait_ge(S_("lists_done"), 1)

            def activate(i, p, first):
                v.wait_ge(S_("gu_ps"), i + 1)
                if not first:
                    v.wait_ge(S_("at_ps"), i)
                tt(GU[:, :], GPS, BGU[p][:, :], ALU.add).then_inc(S_("gu_evac"), 1)
                v.wait_ge(S_("gu_evac"), i + 1)
                ts(GU[:, 0:QW], GU[:, 0:QW], LIMIT, None, ALU.min).then_inc(S_("gate_ready"), 1)
                ts(GU[:, QW:2 * QW], GU[:, QW:2 * QW], LIMIT, -LIMIT, ALU.min, ALU.max)
                v.wait_ge(S_("sig_ready"), i + 1)
                tt(SIG[:, :], SIG[:, :], GU[:, 0:QW], ALU.mult).then_inc(S_("glu"), 1)
                v.wait_ge(S_("glu"), i + 1)
                stt(out=GU[:, 0:QW], in0=GU[:, QW:2 * QW], scalar=1.0, in1=SIG[:, :], op0=ALU.add, op1=ALU.mult).then_inc(S_("act_ready"), 1)

            def spread_biases(e, p, rnd):
                v.wait_ge(S_(f"bias_in{p}"), rnd)
                v.sem_inc(S_("bias_passed"), 1)
                v.stream_shuffle(BGU[p][:, :], BGU[p][:, :], [0] * 32).then_inc(S_("bias_spread"), 1)
                v.stream_shuffle(BDN[p][:, :], BDN[p][:, :], [0] * 32).then_inc(S_("bias_spread"), 1)
                v.wait_ge(S_("bias_spread"), 2 * (e + 1))

            def y_evac(i, p):
                v.wait_ge(S_("d_ps"), i + 2)
                v.wait_ge(S_("y_out"), (i + 1) * 16)
                tt(Y[:, :], DPS, BDN[p][:, :], ALU.add).then_inc(S_("y_ready"), 1)

            v.memset(IDXC[:, 1:2], 0).then_inc(S_("y_ready"), 1)
            spread_biases(0, 0, 32)
            activate(0, 0, True)
            last = v.value_load(LASTB[0:1, 0:1], min_val=0, max_val=MAXB - 1)
            with v.If(last > 0):
                activate(1, 0, False)
                y_evac(0, 0)
            with v.If(last > 1):
                with v.Fori(2, last + 1) as i:
                    activate(i, 0, False)
                    y_evac(i - 1, 0)

            def expert(e, p, before, brnd):
                spread_biases(e, p, brnd)
                activate(before + 1, p, False)
                y_evac(before, 1 - p)
                v.memset(IDXC[:, 1:2], 0).then_inc(S_("y_free"), 1)
                last = v.value_load(LASTB[0:1, bass.ds(e, 1)], min_val=0, max_val=MAXB - 1)
                with v.If(last > before + 1):
                    with v.Fori(before + 2, last + 1) as i:
                        activate(i, p, False)
                        y_evac(i - 1, p)
                return last

            with v.Fori(0, NE // 2 - 1) as r:
                last = v.value_load(LASTB[0:1, bass.ds(2 * r, 1)], min_val=0, max_val=MAXB - 1)
                last = expert(2 * r + 1, 1, last, (r + 1) * 32)
                expert(2 * r + 2, 0, last, (r + 2) * 32)
            last = v.value_load(LASTB[0:1, NE - 2:NE - 1], min_val=0, max_val=MAXB - 1)
            last = expert(NE - 1, 1, last, NE * 16)
            y_evac(last, 1)
            v.wait_ge(S_("hf_in"), 16 * NT)
            for k in range(4):
                v.wait_ge(S_(f"yg_in{k}"), 64)
            for t in range(NT):
                for k in range(TOPK):
                    i = TOPK * t + k
                    ins = stt(out=HF[:, t, :], in0=YG[:, i, :], scalar=GATE[:, i:i + 1], in1=HF[:, t, :], op0=ALU.mult, op1=ALU.add)
                    if k == TOPK - 1:
                        ins.then_inc(S_("summed"), 1)
                    else:
                        link(ins)


_INS = ["x", "norm_mix_w", "w_in", "attn_q_norm_w", "attn_k_norm_w", "attn_sinks", "dn_conv_w", "dn_a_log", "dn_dt_bias",
        "dn_out_norm_w", "w_out", "norm_ffn_w", "router_w", "router_b", "expert_w_gate_up", "expert_b_gate_up",
        "expert_w_down", "expert_b_down"]


def kernel(**inputs):
    import numpy as _np
    import concourse.bacc as _bacc
    from concourse import mybir as _mybir
    from concourse.bass_utils import run_bass_kernel_spmd as _run

    nc = _bacc.Bacc("TRN2", target_bir_lowering=False, num_devices=1)
    arrays, args = {}, []
    for name in _INS:
        a = _np.ascontiguousarray(inputs[name])[0]
        arrays[f"in_{name}"] = a
        args.append(nc.dram_tensor(f"in_{name}", a.shape, _mybir.dt.from_np(a.dtype), kind="ExternalInput").ap())
    out = nc.dram_tensor("out_0", (S, D), _mybir.dt.float32, kind="ExternalOutput").ap()
    hybrid_block(nc, *args, out)
    r = _run(nc, [arrays], core_ids=[0])
    return r.results[0]["out_0"].reshape(1, S, D)
```

```python
from contextlib import ExitStack

import numpy as np

import concourse.bass as bass
from concourse import mybir
from concourse.alu_op_type import AluOpType as ALU

ACT = mybir.ActivationFunctionType
AX = mybir.AxisListType
F32 = mybir.dt.float32
I32 = mybir.dt.int32
U32 = mybir.dt.uint32

P = 128
D = 1024
S = 512
NT = S // P
KD = D // P
HA, DH, KV = 8, 64, 2
HP = HA // KV
CH = 64
NCH = S // CH
HD = 4
NE, TOPK = 32, 4
EPS = 1e-6
BT = 32
MAXB = S * TOPK // BT + NE
Y_ROWS = (NE - 1) * BT + -(-(MAXB + 1 - (NE - 1)) * BT // P) * P
Y_ZERO = MAXB * BT
YL_ROWS = S + P
YL_ZERO = S
QW = 256
LIMIT, ALPHA = 7.0, 1.702

SLABS = [(0, 256), (256, 256), (512, 256), (2304, 260), (2564, 260)] + [(768 + 256 * i, 256) for i in range(6)]
SLABW = 260
NSL = 3
TOKU = 5 * NT
CHU = 12
LEVELS = [2, 4, 8, 16, 32, 64]


def hybrid_block(nc, x, norm_mix_w, w_in, qn_w, kn_w, sinks, conv_w, a_log, dt_bias, out_norm_w, w_out,
                 norm_ffn_w, router_w, router_b, w_gu, b_gu, w_dn, b_dn, out):
    ctx = ExitStack()
    with ctx:
        def sb(name, cols, dt=F32):
            return ctx.enter_context(nc.sbuf_tensor(name, [P, cols], dt))

        sems = {}

        def S_(name):
            if name not in sems:
                sems[name] = ctx.enter_context(nc.semaphore(name))
            return sems[name]

        h_d = nc.dram_tensor("h_scratch", (S, D), F32).ap()
        hn_d = nc.dram_tensor("hn_scratch", (S * 4, QW), F32).ap()
        y_d = nc.dram_tensor("y_scratch", (Y_ROWS, D), F32).ap()
        yl_d = nc.dram_tensor("y_last_scratch", (YL_ROWS, D), F32).ap()

        WE = [sb("W0", 24576), sb("W1", 24576)]
        W0, W1 = WE
        GUW = [w[:, 0:16384].rearrange("p (k n) -> p k n", k=KD) for w in WE]
        DNW = [w[:, 16384:24576].rearrange("p (k n) -> p k n", k=KD) for w in WE]

        ident = sb("ident", P)
        XG = sb("XG", QW)
        XT = sb("XT", 2 * P)
        GU = sb("GU", 2 * QW)
        SIG = sb("SIG", QW)
        AT = sb("AT", 2 * P)
        Y = sb("Y", QW)
        BGU = [sb("BGU0", 2 * QW), sb("BGU1", 2 * QW)]
        BDN = [sb("BDN0", QW), sb("BDN1", QW)]
        IDX = sb("IDX", MAXB + 1, U32)
        IDXC = sb("IDXC", 2, U32)
        LASTB = sb("LASTB", NE, I32)
        SLOT = sb("SLOT", 4 * TOPK, U32)
        SLOTL = sb("SLOTL", NT, U32)
        GATE = sb("GATE", 4 * TOPK)
        SM = sb("SM", 416)

        def small(at, n):
            return SM[:, at:at + n]

        SSX, RSX = small(0, 4), small(4, 4)
        SSA, RNA = small(8, 40), small(48, 40)
        MXS, MNEG, ESK, DEN, RDEN = [small(88 + 4 * i, 4) for i in range(5)]
        SKT = small(108, 4)
        KWT = small(112, 64)
        AL, DTB = small(176, 4), small(180, 4)
        GV, SPT, SPM = small(184, 16), small(200, 16), small(216, 16)
        BETA = small(232, 16)
        GC, GLC = small(248, 16), small(264, 16)
        EG, EGD, EGL = small(280, 16), small(296, 16), small(312, 16)
        SSQ, RSQ = small(328, 32), small(360, 32)
        SSO, RSO = small(392, 16), small(392, 16)
        SSH, RSH = small(408, 4), small(412, 4)

        X = W0[:, 0:4096].rearrange("p (t n) -> p t n", t=NT)
        CV = [W0[:, 512 * i:512 * i + 512] for i in range(2)]
        SG = [W0[:, 1024 + 512 * i:1536 + 512 * i] for i in range(2)]
        ST = [W0[:, 2048 + 512 * i:2560 + 512 * i] for i in range(2)]
        SGZ = [W0[:, 3072:3584], W0[:, 3584:4096]]
        UT = W0[:, 4096:8192].rearrange("p (k n) -> p k n", k=KD)
        SL = [W0[:, 8192 + i * KD * SLABW:8192 + (i + 1) * KD * SLABW].rearrange("p (k n) -> p k n", k=KD) for i in range(NSL)]
        AQ = W0[:, 14432:17504].rearrange("p (t n) -> p t n", t=NT)
        QNT = W0[:, 17504:19552].rearrange("p (c h q) -> p c h q", c=NCH, h=HP)
        KNT = W0[:, 19552:20064]
        AVS = W0[:, 20064:20448].rearrange("p (i n) -> p i n", i=3)
        MSK = [W0[:, 20480 + P * i:20608 + P * i] for i in range(7)]
        TRIU = W0[:, 21376:21504]
        ONES = W0[:, 21504:21632]
        NEGM = W0[:, 21632:21760]
        STATE = W0[:, 21760:22272]
        WO1 = W0[:, 16384:20480].rearrange("p (k n) -> p k n", k=4)
        QTM, KTM, VTM = [W1[:, 2048 * i:2048 * i + 2048].rearrange("p (t h n) -> p t h n", t=NT, h=HD)
                         for i in range(3)]
        OB = W1[:, 0:2048].rearrange("p (t n) -> p t n", t=NT)
        WO0 = W1[:, 2048:6144].rearrange("p (k n) -> p k n", k=4)
        DZ = W1[:, 6144:8224].rearrange("p (t n) -> p t n", t=NT)
        CAT = W1[:, 20480:24576].rearrange("p (k n) -> p k n", k=KD)

        def slot(i, c):
            if c >= 2:
                at = 512 * (2 * i + c - 2)
                return W0[:, at:at + 512]
            n = 2 * i + c
            return W1[:, 8224 + 512 * n:8736 + 512 * n] if n < 23 else W0[:, 22272 + 512 * (n - 23):22784 + 512 * (n - 23)]

        names = ["KH", "KB", "QN", "QE", "KBEG", "KTE", "VB", "KHT", "KBT", "QET", "QNT", "DEC", "LT"]
        B = [{n: slot(i, c) for i, n in enumerate(names)} for c in range(NT)]
        for b in B:
            b.update(INT=b["KH"], CT=b["KB"], P1=b["QN"], USOL=b["QE"], U=b["KHT"], T=b["KBT"], WT=b["QNT"], VN=b["DEC"])
        STATES = [STATE, B[0]["T"]]
        QNB = [W1[:, 8224 + 640 * i:8864 + 640 * i] for i in range(2)]
        PB = [W1[:, 9504 + 512 * i:10016 + 512 * i] for i in range(2)]
        PT = W1[:, 10528:11040]
        SQA = W1[:, 11040:11680]
        NW = W1[:, 11680:12704]
        CWR = W1[0:48, 12704:12832]
        CW = W0[:, 23808:23856]
        ZNW = W0[:, 23856:23984]
        SQD = SGZ
        HNT = [W1[:, D * i:D * i + D].rearrange("p (k n) -> p k n", k=KD) for i in range(2)]
        HN = [W1[:, 6144 + D * i:6144 + D * i + D] for i in range(2)]
        H = [W1[:, at:at + D] for at in (9216, 10240, 11264, 8192)]
        FW = W0[:, 22272:23296]
        RW = W0[:, 23296:23552].rearrange("p (k n) -> p k n", k=KD)
        RB = W0[:, 23552:23584]
        LG = W0[:, 23584:23712].rearrange("p (t n) -> p t n", t=NT)
        MX8 = W0[:, 23712:23744].rearrange("p (t n) -> p t n", t=NT)
        MI8 = W0[:, 23744:23776].bitcast(U32).rearrange("p (t n) -> p t n", t=NT)
        MIF = W0[:, 23776:23808].rearrange("p (t n) -> p t n", t=NT)
        RT = W0[:, 20480:22272]
        OH = RT[:, 0:512].rearrange("p (t k e) -> p t k e", t=NT, k=TOPK)
        MASK = RT[:, 512:640].rearrange("p (t e) -> p t e", t=NT)
        IO32 = RT[:, 640:672]
        IOM = RT[:, 672:800]
        IOB = RT[:, 800:800 + MAXB + 1]
        ONE32 = RT[:, 900:932]
        STRU = RT[:, 932:1060]
        ONER = RT[:, 1060:1188]
        TOK4 = RT[:, 1188:1192]
        PJ = RT[:, 1192:1193]
        PJI = RT[:, 1193:1194].bitcast(I32)
        RK, RKB, BSK, TPOS, BLK = [RT[:, 1196 + 16 * i:1212 + 16 * i] for i in range(5)]
        RKI = RT[:, 1276:1292].bitcast(I32)
        NBF, BEF, BSF = [RT[:, 1292 + 32 * i:1324 + 32 * i] for i in range(3)]
        NBI = RT[:, 1388:1420].bitcast(I32)
        GSUM, GREC = RT[:, 1420:1424], RT[:, 1424:1428]
        OHR = RT[:, 1428:1556].rearrange("p (k e) -> p k e", k=TOPK)
        LISTS = W1[:, 20480:24576]
        OHB = LISTS[:, 0:512].rearrange("p (i e) -> p i e", e=NE)
        T1 = LISTS[:, 512:2560].rearrange("p (t k m) -> p t k m", t=NT, k=TOPK)
        NB1 = 3
        B1 = LISTS[:, 2560:2560 + NB1 * TOPK * (MAXB + 1)].rearrange("p (i k b) -> p i k b", i=NB1, k=TOPK)
        HF = W0[:, 0:4096].rearrange("p (t n) -> p t n", t=NT)
        YG = W0[:, 4096:20480].rearrange("p (i n) -> p i n", i=4 * TOPK)
        YGL = W0[:, 20480:24576].rearrange("p (t n) -> p t n", t=NT)
        GATEL = small(0, NT)
        M31, SLF, SLT = small(8, 16), small(24, 16), small(40, 16)
        C31, SLS = small(56, 1), small(60, 4)

        PS = [ctx.enter_context(nc.psum_tensor(f"PS{i}", [P, 512], F32))[:, :] for i in range(4)]
        PSC = ctx.enter_context(nc.psum_tensor("PSC", [P, 2, 512], F32))
        PS += [PSC[:, 0, :], PSC[:, 1, :]]
        PS += [ctx.enter_context(nc.psum_tensor(f"PS{i}", [P, 512], F32))[:, :] for i in (6, 7)]
        PA = PS[0:2]
        TA, TB, AO, XP = PS[2], PS[3], PS[6], PS[7]

        RANKS = [PS[i][:, 0:NE] for i in (6, 7, 0, 1)]
        GPS, DPS, XPS, ATPS, RPS = PS[0], PS[1][:, 0:QW], PS[2][:, 0:QW], PS[3][:, 0:QW], PS[6][:, 0:P]

        def bc(v, n):
            a = v.shape[1]
            return v.rearrange("p (a o) -> p a o", o=1).to_broadcast([P, a, n])

        def bm(v, a):
            return v.rearrange("p (o n) -> p o n", o=1).to_broadcast([P, a, v.shape[1]])

        def h4(v):
            return v.rearrange("p (h n) -> p h n", h=HD)

        def even(v, lv):
            return v.rearrange("p (h b two s) -> p h b two s", h=HD, two=2, s=LEVELS[lv])[:, :, :, 0, :]

        def compact(v, lv):
            return v[:, 0:HD * P // 2].rearrange("p (h b s) -> p h b s", h=HD, s=LEVELS[lv])

        def within(i, most, why):
            return i if isinstance(i, int) else nc.s_assert_within(i, 0, most, skip_runtime_bounds_check_because=why)

        block = ctx.enter_context(nc.Block())

        def rep(v, n=P):
            return v.partition_broadcast(n)

        NORM_AT = {6: (0,), 7: (1,), 8: (2,), 9: (3, 4), 10: (5, 6, 7)}
        EARLY = 11

        @block.sync
        def _(sp):
            def biases(e, p):
                sp.dma_start(BGU[p][0:P:32, :].rearrange("p (g n) -> p g n", g=2),
                             b_gu[e].rearrange("(g j n) -> j g n", g=2, j=4)).then_inc(S_(f"bias_in{p}"), 16)
                sp.dma_start(BDN[p][0:P:32, :], b_dn[e].rearrange("(j n) -> j n", j=4)).then_inc(S_(f"bias_in{p}"), 16)

            def gu_part(e, p, parts, through=None):
                for q in parts:
                    if through is not None:
                        sp.wait_ge(S_(f"gu_read{q}" if q < 3 else "gu_ps"), through)
                    sp.dma_start(GUW[p][:, 2 * q:2 * q + 2, :],
                                 w_gu[e].rearrange("(k p) n -> p k n", p=P)[:, 2 * q:2 * q + 2, :]).then_inc(S_(f"gu_in{p}{q}"), 16)

            def dn_part(e, p, parts, through=None):
                for q in parts:
                    if through is not None:
                        sp.wait_ge(S_("dn_read"), through) if q == 0 else sp.wait_ge(S_("d_ps"), through + 1)
                    sp.dma_start(DNW[p][:, 4 * q:4 * q + 4, :],
                                 w_dn[e].rearrange("(k p) n -> p k n", p=P)[:, 4 * q:4 * q + 4, :]).then_inc(S_(f"dn_in{p}{q}"), 16)

            def small_parameters():
                sp.dma_start(KWT, rep(kn_w)).then_inc(S_("par_in"), 16)
                sp.dma_start(SIG[:, 0:64], rep(qn_w)).then_inc(S_("par_in"), 16)
                for half in range(2):
                    sp.dma_start(SKT[64 * half:64 * half + 64, :],
                                sinks.rearrange("(g two) -> two g", two=2)[half].partition_broadcast(64),
                                allow_slow_non_contiguous=True).then_inc(S_("par_in"), 16)
                sp.dma_start(AL, rep(a_log)).then_inc(S_("par_in"), 16)
                sp.dma_start(DTB, rep(dt_bias)).then_inc(S_("par_in"), 16)
                sp.dma_start(ZNW, rep(out_norm_w)).then_inc(S_("par_in"), 16)
                sp.dma_start(CWR, conv_w.rearrange("j (t c) -> (j t) c", c=P)).then_inc(S_("par_in"), 16)
                sp.wait_ge(S_("zeros"), 1)
                for rows, sem in ((y_d[(NE - 1) * BT:, :], "y_out"), (yl_d, "yl_zeroed")):
                    n = rows.shape[0] * D // P
                    sp.dma_start(rows.rearrange("(p r) n -> p (r n)", p=P).rearrange("p (a n) -> p a n", n=2 * P),
                                 AT[:, :].rearrange("p (o n) -> p o n", o=1).to_broadcast([P, n // (2 * P), 2 * P])).then_inc(S_(sem), 16)

            for t in range(NT):
                sp.dma_start(X[:, t, :], x[t * P:(t + 1) * P, :]).then_inc(S_(f"x_in{t}"), 16)
                if t == 0:
                    sp.dma_start(NW, rep(norm_mix_w)).then_inc(S_("nw_in"), 16)
            for n, (c0, w) in enumerate(SLABS):
                if n == NSL:
                    small_parameters()
                if n >= NSL:
                    sp.wait_ge(S_("slab_used"), n - NSL + 1)
                sp.dma_start(SL[n % NSL][:, :, 0:w],
                             w_in.rearrange("(k p) n -> p k n", p=P)[:, :, c0:c0 + w]).then_inc(S_(f"slab_in{n % NSL}"), 16)
                if n == 3:
                    sp.wait_ge(S_("tok_evac"), 3 * NT)
                    for i in range(3):
                        sp.dma_start(AVS[0:64, i, :], AQ[64:P, i, 640:768]).then_inc(S_("avs_in"), 16)
                        sp.dma_start(AVS[64:P, i, :], AQ[0:64, i + 1, 640:768]).then_inc(S_("avs_in"), 16)
            sp.wait_ge(S_("att_out"), NCH)
            wo_v = w_out[512:1024, :].rearrange("(k p) n -> p k n", p=P)
            sp.dma_start(WO1, wo_v).then_inc(S_("wo_in"), 16)
            sp.wait_ge(S_("kq_scaled"), 3 * NT)
            sp.wait_ge(S_("vb_ready"), NT)
            for kv in range(KV):
                sp.dma_start(WO0[kv * 64:kv * 64 + 64, :, :],
                             w_out[kv * 256:kv * 256 + 256, :].rearrange("(h d) n -> d h n", h=HP)).then_inc(S_("wo_in"), 16)
            sp.wait_ge(S_("kv_ps"), 2)
            sp.wait_ge(S_("o_ps"), 2)
            for t in range(NT - 1):
                sp.dma_start(H[t], x[t * P:(t + 1) * P, :]).then_inc(S_("res_in"), 16)
            sp.wait_ge(S_("dn_out"), 2)
            sp.dma_start(FW, rep(norm_ffn_w)).then_inc(S_("res_in"), 16)
            sp.dma_start(RW, router_w.rearrange("(k p) n -> p k n", p=P)).then_inc(S_("res_in"), 16)
            sp.dma_start(RB, rep(router_b)).then_inc(S_("res_in"), 16)
            sp.wait_ge(S_("dn_out"), NT)
            sp.dma_start(H[NT - 1], x[(NT - 1) * P:, :]).then_inc(S_("res_in"), 16)
            for q in range(4):
                sp.dma_start(GUW[0][:, 2 * q:2 * q + 2, :],
                             w_gu[0].rearrange("(k p) n -> p k n", p=P)[:, 2 * q:2 * q + 2, :]).then_inc(S_(f"gu_in0{q}"), 16)
            for t in range(NT):
                sp.wait_ge(S_("h_add"), 2 * t + 2)
                sp.dma_start(h_d[t * P:(t + 1) * P, :], H[t]).then_inc(S_("h_out"), 16)
                sp.wait_ge(S_("hn_ready"), t + 1)
                sp.dma_start(hn_d[t * 512:(t + 1) * 512, :].rearrange("(p j) n -> p (j n)", j=4), HN[t % 2]).then_inc(S_(f"hn_out{t % 2}"), 16)
                if t == 0:
                    gu_part(1, 1, [3])
                    dn_part(1, 1, [0])
            sp.wait_ge(S_("bias_zeros"), 4)
            biases(0, 0)
            sp.wait_ge(S_("outproj"), 2 * NT)
            dn_part(0, 0, [0])
            sp.wait_ge(S_("h_out"), 16 * NT)
            gu_part(1, 1, [2])
            sp.wait_ge(S_("hn_out0"), 16 * NT // 2)
            sp.wait_ge(S_("hn_out1"), 16 * NT // 2)
            sp.wait_ge(S_("hnt_ps"), 2 * NT)
            gu_part(1, 1, [1])
            sp.wait_ge(S_("lg_ps"), NT)
            gu_part(1, 1, [0])
            sp.wait_ge(S_("lists_done"), 2)
            sp.wait_ge(S_("gathered"), 16)
            dn_part(0, 0, [1])
            biases(1, 1)
            sp.wait_ge(S_("gathered"), 32)
            dn_part(1, 1, [1])

            def reload(e, p):
                through = sp.value_load(LASTB[0:1, bass.ds(e - 2, 1)], min_val=0, max_val=MAXB - 1) + 1
                gu_part(e, p, range(4), through)
                dn_part(e, p, range(2), through)
                sp.wait_ge(S_("y_free"), e - 1)
                biases(e, p)

            with sp.Fori(1, NE // 2) as r:
                reload(2 * r, 0)
                reload(2 * r + 1, 1)
            through = sp.value_load(LASTB[0:1, NE - 2:NE - 1], min_val=0, max_val=MAXB - 1) + 1
            sp.wait_ge(S_("gu_ps"), through)
            for t in range(NT):
                sp.dma_start(HF[:, t, :], h_d[t * P:(t + 1) * P, :]).then_inc(S_("hf_in"), 16)
            for t in range(NT):
                sp.wait_ge(S_("summed"), t + 1)
                sp.dma_start(out[t * P:(t + 1) * P, :], HF[:, t, :]).then_inc(S_("out_done"), 16)
            sp.wait_ge(S_("out_done"), 16 * NT)

        @block.gpsimd
        def _(g):
            g.memset(AT[:, :], 0.0).then_inc(S_("zeros"), 1)
            g.memset(ident[:, :], 0.0).then_inc(S_("p_a"), 1)
            g.memset(ONES, 1.0).then_inc(S_("ones"), 1)
            for b in BGU + BDN:
                g.memset(b[:, :], 0.0).then_inc(S_("bias_zeros"), 1)
            g.memset(TRIU, 1.0).then_inc(S_("p_a"), 1)
            g.memset(NEGM, 0.0).then_inc(S_("p_a"), 1)
            g.wait_ge(S_("p_a"), 3)
            g.affine_select(out=ident[:, :], in_=ident[:, :], compare_op=ALU.not_equal, fill=1.0, base=0,
                            pattern=[[-1, P]], channel_multiplier=1).then_inc(S_("ident"), 1)
            g.affine_select(out=TRIU, in_=TRIU, compare_op=ALU.is_ge, fill=0.0, base=0,
                            pattern=[[1, P]], channel_multiplier=-1).then_inc(S_("tri"), 1)
            g.affine_select(out=NEGM, in_=NEGM, compare_op=ALU.is_ge, fill=-1e30, base=0,
                            pattern=[[1, P]], channel_multiplier=-1).then_inc(S_("tri"), 1)
            for i, s in enumerate([1] + LEVELS):
                g.memset(MSK[i], 0.0).then_inc(S_("p_b"), 1)
                g.wait_ge(S_("p_b"), 4 * i + 1)
                odd = MSK[i].rearrange("p (b two s) -> p b two s", two=2, s=s)[:, :, 1, :]
                g.memset(odd, 1.0).then_inc(S_("p_b"), 1)
                g.wait_ge(S_("p_b"), 4 * i + 2)
                g.affine_select(out=odd, in_=odd, compare_op=ALU.is_ge, fill=0.0, base=0,
                                pattern=[[-2 * s, P // (2 * s)], [0, s]], channel_multiplier=1).then_inc(S_("p_b"), 1)
                g.wait_ge(S_("p_b"), 4 * i + 3)
                g.affine_select(out=odd, in_=odd, compare_op=ALU.is_ge, fill=0.0, base=s - 1,
                                pattern=[[2 * s, P // (2 * s)], [0, s]], channel_multiplier=-1).then_inc(S_("p_b"), 1)
            g.wait_ge(S_("att_out"), NCH)
            g.wait_ge(S_("dn_act"), 7)
            g.wait_ge(S_("dn_vec"), 5)
            for c in range(NT):
                b = B[c]
                hs = slice(4 * c, 4 * c + 4)
                if c == 2:
                    g.wait_ge(S_("tm_evac"), CHU)
                g.wait_ge(S_("kq_scaled"), 3 * c + 1)
                g.tensor_tensor(h4(b["KTE"]), h4(b["KH"]), bc(EGD[:, hs], P), ALU.mult).then_inc(S_("p_c"), 1)
                g.wait_ge(S_("kq_scaled"), 3 * c + 3)
                g.tensor_tensor(h4(b["QE"]), h4(b["QN"]), bc(EG[:, hs], P), ALU.mult).then_inc(S_("qe_ready"), 1)
                g.tensor_tensor(h4(b["KBEG"]), h4(b["KB"]), bc(EG[:, hs], P), ALU.mult).then_inc(S_("scaled_pool"), 1)
            for c in range(NT):
                g.tensor_tensor(h4(B[c]["VB"]), VTM[:, c, :, :], bc(BETA[:, 4 * c:4 * c + 4], P), ALU.mult).then_inc(S_("vb_ready"), 1)
            g.wait_ge(S_("dn_out"), NT)
            g.iota(PJI, pattern=[[0, 1]], base=0, channel_multiplier=1).then_inc(S_("consts"), 1)
            g.iota(TOK4, pattern=[[512, 4]], base=0, channel_multiplier=4, allow_small_or_imprecise_dtypes=True).then_inc(S_("consts"), 1)
            g.iota(IO32, pattern=[[1, 32]], base=0, channel_multiplier=0, allow_small_or_imprecise_dtypes=True).then_inc(S_("consts"), 1)
            g.iota(IOM.rearrange("p (a b) -> p a b", a=4), pattern=[[0, 4], [1, 32]], base=0, channel_multiplier=0, allow_small_or_imprecise_dtypes=True).then_inc(S_("consts"), 1)
            g.iota(IOB, pattern=[[1, MAXB + 1]], base=0, channel_multiplier=0, allow_small_or_imprecise_dtypes=True).then_inc(S_("consts"), 1)
            g.memset(ONE32, 1.0).then_inc(S_("consts"), 1)
            g.memset(ONER, 1.0).then_inc(S_("consts"), 1)
            g.memset(STRU, 1.0).then_inc(S_("consts"), 1)
            g.wait_ge(S_("consts"), 8)
            g.affine_select(out=STRU, in_=STRU, compare_op=ALU.is_gt, fill=0.0, base=0,
                            pattern=[[1, P]], channel_multiplier=-1).then_inc(S_("consts"), 1)
            g.wait_ge(S_("outproj"), 2 * NT)
            for t in range(NT):
                g.wait_ge(S_("tpos"), t + 1)
                for k in range(TOPK):
                    g.tensor_scalar(T1[:, t, k, :], IOM, TPOS[:, 4 * t + k:4 * t + k + 1], TOK4[:, t:t + 1], ALU.is_equal, ALU.mult).then_inc(S_("t1_ready"), 1)
            g.wait_ge(S_("lists_done"), 1)
            g.wait_ge(S_("hn_out0"), 16 * NT // 2)
            g.wait_ge(S_("hn_out1"), 16 * NT // 2)
            nb = g.value_load(LASTB[0:1, NE - 1:NE], min_val=NE - 1, max_val=MAXB - 1) + 1

            def gather(i):
                at = within(i, MAXB, "no routing gives more than MAXB blocks, and one is gathered behind them")
                g.tensor_copy(IDXC[:, 0:1], IDX[:, bass.ds(at, 1)]).then_inc(S_("idx_cur"), 1)
                g.wait_ge(S_("idx_cur"), i + 1)
                g.sem_inc(S_("pool_passed"), 1)
                g.indirect_dma_start(out=XG[:, :], out_offset=None, in_=hn_d,
                                     in_offset=bass.IndirectOffsetOnAxis(ap=IDXC[:, 0:1], axis=0)).then_inc(S_("gathered"), 16)

            gather(0)
            def next_gather(i):
                g.wait_ge(S_("xt_ps"), i)
                g.wait_ge(S_("gathered"), i * 16)
                gather(i)

            def y_gathers(t):
                for i in range(TOPK * t, TOPK * t + TOPK):
                    g.indirect_dma_start(out=YG[:, i, :], out_offset=None, in_=y_d,
                                         in_offset=bass.IndirectOffsetOnAxis(ap=SLOT[:, i:i + 1], axis=0)).then_inc(S_(f"yg_in{t}"), 16)

            f = g.value_load(LASTB[0:1, NE - 2:NE - 1], min_val=NE - 2, max_val=MAXB - 1) + 1
            with g.Fori(1, f + 1) as i:
                next_gather(i)
            next_gather(f + 1)
            for t in range(NT):
                if t < NT - 1:
                    with g.If(nb > f + t + 1):
                        next_gather(f + t + 2)
                else:
                    with g.If(nb > f + t + 1):
                        with g.Fori(f + t + 2, nb + 1) as i:
                            next_gather(i)
                if t == 0:
                    g.wait_ge(S_("y_out"), (f + 1) * 16)
                    g.sem_inc(S_("pool_passed"), 1)
                y_gathers(t)
            g.wait_ge(S_("y_out"), (nb + 1) * 16)
            g.sem_inc(S_("pool_passed"), 1)
            for t in range(NT):
                g.wait_ge(S_(f"yg_in{t}"), 16 * TOPK)
                g.indirect_dma_start(out=YGL[:, t, :], out_offset=None, in_=yl_d,
                                     in_offset=bass.IndirectOffsetOnAxis(ap=SLOTL[:, t:t + 1], axis=0)).then_inc(S_(f"yg_in{t}"), 16)

        @block.scalar
        def _(a):
            def ut_copies(t):
                for half in range(2):
                    n = 2 * t + half
                    a.wait_ge(S_("ut_ps"), n + 1)
                    a.activation(UT[:, 4 * half:4 * half + 4, t * P:(t + 1) * P], h4(PS[2 + half]), ACT.Copy).then_inc(S_("ut_ready"), 1)

            def tok_unit(n):
                s, t = n // NT, n % NT
                w = SLABS[s][1]
                dst = AQ[:, t, 256 * s:256 * s + 256] if s < 3 else DZ[:, t, 260 * (s - 3):260 * (s - 3) + 260]
                a.wait_ge(S_("proj_ps"), n + 1)
                a.activation(dst, PA[n % 2][:, 0:w], ACT.Copy).then_inc(S_("tok_evac"), 1)

            for t in range(NT):
                a.wait_ge(S_(f"x_in{t}"), 16)
                if t:
                    a.wait_ge(S_("ssx"), t)
                a.activation(W1[:, 0:D], X[:, t, :], ACT.Square, accum_out=SSX[:, t:t + 1]).then_inc(S_("ssx"), 1)
                a.wait_ge(S_("meansq"), t + 1)
                a.activation(RSX[:, t:t + 1], SSX[:, t:t + 1], ACT.Sqrt).then_inc(S_("sqrt"), 1)
                if t:
                    ut_copies(t - 1)
                if t >= 2:
                    tok_unit(t - 2)
            ut_copies(NT - 1)
            for n in range(2, 12):
                tok_unit(n)
            a.wait_ge(S_("meansq"), NT + 1)
            a.activation(RNA, SSA, ACT.Sqrt).then_inc(S_("sqrt"), 1)
            for n in range(12, TOKU):
                tok_unit(n)
            a.wait_ge(S_("tok_evac"), TOKU)
            a.activation(BETA.rearrange("p (t h) -> p t h", t=NT), DZ[:, :, 512:516], ACT.Sigmoid).then_inc(S_("dn_act"), 1)
            for t in range(NT):
                if t >= 2:
                    a.wait_ge(S_("z_done"), t - 1)
                a.activation(SGZ[t % 2], DZ[:, t, 0:512], ACT.Sigmoid).then_inc(S_("z_sig"), 1)
            a.wait_ge(S_("dn_vec"), 1)
            a.activation(SPM, SPM, ACT.Exp).then_inc(S_("dn_act"), 1)
            a.activation(AL, AL, ACT.Exp).then_inc(S_("dn_act"), 1)
            a.wait_ge(S_("dn_vec"), 2)
            a.activation(SPM, SPM, ACT.Ln).then_inc(S_("dn_act"), 1)
            def qk_copies(t):
                a.wait_ge(S_("qk_ps"), t + 1)
                a.activation(QNT[:, 2 * t:2 * t + 2, :, :].rearrange("p c h q -> p h c q"),
                             TA.rearrange("p (h c q) -> p h c q", h=4, c=2), ACT.Copy)
                a.activation(KNT[:, t * P:(t + 1) * P], TB[:, 0:P], ACT.Copy).then_inc(S_("kt_ready"), 1)

            qk_copies(0)
            qk_copies(1)

            def square(n):
                a.wait_ge(S_("tm_evac"), 4 * (n // NT + 1))
                a.wait_ge(S_("z_done"), NT)
                if n >= 2:
                    a.wait_ge(S_("ssq"), n - 1)
                a.activation(h4(SQD[n % 2]), [QTM, KTM][n // NT][:, n % NT, :, :], ACT.Square).then_inc(S_("sq_done"), 1)

            def prepare(c):
                b = B[c]
                a.wait_ge(S_("dsub"), c + 1)
                a.activation(b["DEC"], b["DEC"], ACT.Exp).then_inc(S_("decay"), 1)
                for i, n in enumerate(("KHT", "KBT", "QNT", "QET")):
                    a.wait_ge(S_("dt_ps"), 4 * c + i + 1)
                    a.activation(b[n], PS[4 + i % 2], ACT.Copy).then_inc(S_("dt_ready"), 1)

            for i in range(CHU + 2):
                if i in (1, 2):
                    qk_copies(i + 1)
                if i == 2:
                    a.wait_ge(S_("dn_vec"), 5)
                    a.activation(EG, GC, ACT.Exp).then_inc(S_("dn_act"), 1)
                    a.activation(EGD, EGD, ACT.Exp).then_inc(S_("dn_act"), 1)
                    a.activation(EGL, GLC, ACT.Exp).then_inc(S_("dn_act"), 1)
                if i == CHU - 1:
                    a.wait_ge(S_("meansq"), NT + 2)
                    a.activation(RSQ, SSQ, ACT.Sqrt).then_inc(S_("sqrt"), 1)
                if i < CHU:
                    a.wait_ge(S_("conv"), 4 * i + 4)
                    if i >= 2:
                        a.wait_ge(S_("silu"), i - 1)
                    a.activation(SG[i % 2], CV[i % 2], ACT.Sigmoid).then_inc(S_("sig"), 1)
                if i < NCH:
                    a.wait_ge(S_("shifted"), i + 1)
                    w = P if i else CH
                    pv = PB[i % 2].rearrange("p (g n) -> p g n", g=4)[:, :, 0:w]
                    a.activation(pv, pv, ACT.Exp).then_inc(S_("exps_done"), 1)
                    a.activation(ESK, MNEG, ACT.Exp).then_inc(S_("exps_done"), 1)
                if 1 <= i <= NCH:
                    n = i - 1
                    k = P if n else CH
                    a.wait_ge(S_("pt_ps"), n + 1)
                    if n:
                        a.wait_ge(S_("pv_ps"), n)
                    a.activation(PT[0:k, :], TA[0:k, :], ACT.Copy).then_inc(S_("pt_ready"), 1)
                if 2 <= i:
                    u = i - 2
                    sub, hd = u // 4, u % 4
                    a.wait_ge(S_("st_ps"), u + 1)
                    dst = [QTM, KTM, VTM][sub][:, :, hd, :]
                    a.activation(dst, h4(XP), ACT.Copy).then_inc(S_("tm_evac"), 1)
                if 2 <= i < NCH + 2:
                    n = i - 2
                    a.wait_ge(S_("pv_ps"), n + 1)
                    a.activation(CAT[:, 0:4, n * CH:(n + 1) * CH], AO[:, 0:256].rearrange("p (h q) -> p h q", h=4), ACT.Copy).then_inc(S_("att_out"), 1)
                for n in NORM_AT.get(i, ()):
                    square(n)
                if i > EARLY:
                    prepare(i - EARLY - 1)
            for c in range(2, NT):
                prepare(c)
            def t0_copy(c):
                a.wait_ge(S_("t0_ps"), c + 1)
                a.activation(B[c]["T"], PS[c % 2], ACT.Copy).then_inc(S_("t_ready"), 1)

            t0_copy(0)
            t0_copy(1)
            for m in range(len(LEVELS) * NT + 2):
                if m < len(LEVELS) * NT:
                    a.wait_ge(S_("p1_ps"), m + 1)
                    a.activation(B[m % NT]["P1"][:, 0:HD * 64], PS[4 + m % 2][:, 0:HD * 64], ACT.Copy).then_inc(S_("p1_ready"), 1)
                if m < 2:
                    t0_copy(m + 2)
                if m >= 2:
                    a.wait_ge(S_("tt_ps"), m - 1)
                    a.activation(B[(m - 2) % NT]["U"], PS[7 - 6 * (m % 2)], ACT.Copy).then_inc(S_("u_upd"), 1)

            def uw_copies(c):
                a.wait_ge(S_("uw_ps"), 2 * c + 1)
                a.activation(B[c]["USOL"], PS[2], ACT.Copy).then_inc(S_("uw"), 1)
                a.wait_ge(S_("uw_ps"), 2 * c + 2)
                a.activation(B[c]["WT"], PS[3], ACT.Copy).then_inc(S_("uw"), 1)

            def dcat_copy(c):
                a.wait_ge(S_("dcat_ps"), c + 1)
                a.activation(CAT[:, 4:8, c * P:(c + 1) * P], h4(PS[2 + c % 2]), ACT.Copy).then_inc(S_("dcat"), 1)

            uw_copies(0)
            uw_copies(1)
            for i in range(NT + 1):
                if i < NT:
                    a.wait_ge(S_("o_ps"), i + 1)
                    a.activation(OB[:, i, :], PS[6 - 2 * (i % 2)], ACT.Copy).then_inc(S_("o_evac"), 1)
                    a.wait_ge(S_("o_evac"), i + 1)
                    if i + 2 < NT:
                        uw_copies(i + 2)
                    a.activation(B[i]["LT"], OB[:, i, :], ACT.Square).then_inc(S_("sq_done"), 1)
                else:
                    dcat_copy(0)
                if i:
                    cs = slice(4 * (i - 1), 4 * i)
                    a.wait_ge(S_("meansq"), NT + 2 + i)
                    a.activation(RSO[:, cs], SSO[:, cs], ACT.Sqrt).then_inc(S_("sqrt"), 1)
            for c in range(1, NT):
                dcat_copy(c)
            for t in range(NT):
                a.wait_ge(S_("h_add"), 2 * t + 2)
                if t >= 2:
                    a.wait_ge(S_(f"hn_out{t % 2}"), 16)
                    a.wait_ge(S_("hnt_ps"), 2 * (t - 1))
                a.activation(HN[t % 2], H[t], ACT.Square, accum_out=SSH[:, t:t + 1]).then_inc(S_("ssh"), 1)
                a.wait_ge(S_("meansq"), 2 * NT + 3 + t)
                a.activation(RSH[:, t:t + 1], SSH[:, t:t + 1], ACT.Sqrt).then_inc(S_("sqrt"), 1)
                for half in range(2):
                    a.wait_ge(S_("hnt_ps"), 2 * t + half + 1)
                    if t >= 2:
                        a.wait_ge(S_("lg_ps"), t - 1)
                    a.activation(HNT[t % 2][:, 4 * half:4 * half + 4, :], h4(PS[2 + half]), ACT.Copy).then_inc(S_("hnt_ready"), 1)
            a.wait_ge(S_("v_gate"), NT)
            a.activation(GATE[:, :], GATE[:, :], ACT.Exp).then_inc(S_("gexp"), 1)
            a.wait_ge(S_("lists_done"), 1)
            last = a.value_load(LASTB[0:1, NE - 1:NE], min_val=NE - 1, max_val=MAXB - 1)
            nb = last + 1

            def xt_copy(i):
                a.activation(XT[:, :], XPS, ACT.Copy).then_inc(S_("xt_ready"), 1)

            def sigmoid(i):
                a.wait_ge(S_("gate_ready"), i + 1)
                if not (isinstance(i, int) and i == 0):
                    a.wait_ge(S_("act_ready"), i)
                a.activation(SIG[:, :], GU[:, 0:QW], ACT.Sigmoid, scale=ALPHA).then_inc(S_("sig_ready"), 1)

            def at_copy(i):
                a.wait_ge(S_("at_ps"), i + 1)
                a.wait_ge(S_("d_ps"), i + 1)
                a.activation(AT[:, :], ATPS, ACT.Copy).then_inc(S_("at_ready"), 1)

            def y_store(i, dst, row):
                a.wait_ge(S_("y_ready"), i + 2)
                if dst is yl_d:
                    row = within(row, S - BT, "a token is routed to an expert once at most, so its blocks are S / BT at most")
                a.dma_start(dst[bass.ds(row, BT), :].rearrange("t (j n) -> j t n", j=4), Y[:, :]).then_inc(S_("y_out"), 16)

            f = a.value_load(LASTB[0:1, NE - 2:NE - 1], min_val=NE - 2, max_val=MAXB - 1) + 1
            a.wait_ge(S_("xt_ps"), 1)
            xt_copy(0)
            a.wait_ge(S_("xt_ps"), 2)
            a.wait_ge(S_("gu_ps"), 1)
            xt_copy(1)
            sigmoid(0)
            a.wait_ge(S_("y_out"), 16)
            a.wait_ge(S_("yl_zeroed"), 16)

            def block_step(i, dst, row):
                at_copy(i - 1)
                a.wait_ge(S_("xt_ps"), i + 2)
                a.wait_ge(S_("gu_ps"), i + 1)
                xt_copy(i + 1)
                sigmoid(i)
                y_store(i - 1, dst, row)

            with a.Fori(1, f + 1) as i:
                block_step(i, y_d, (i - 1) * BT)
            with a.If(last > f):
                with a.Fori(0, last - f) as j:
                    block_step(f + 1 + j, yl_d, j * BT)
            at_copy(last)
            y_store(last, yl_d, (last - f) * BT)

        @block.tensor
        def _(pe):
            def mm(o, l, r, st, sp_):
                return pe.matmul(o, l, r, start=st, stop=sp_)

            pe.wait_ge(S_("ident"), 1)
            def u_transposes(t):
                pe.wait_ge(S_("u_ready"), t + 1)
                for half in range(2):
                    n = 2 * t + half
                    if n >= 2:
                        pe.wait_ge(S_("ut_ready"), n - 1)
                    for j in range(4):
                        k = 4 * half + j
                        last = pe.transpose(PS[2 + half][:, j * P:(j + 1) * P], X[:, t, k * P:(k + 1) * P], ident[:, :])
                    last.then_inc(S_("ut_ps"), 1)

            def bank_free(n):
                m = n - 2
                if m < 0:
                    return
                if m < TOKU:
                    pe.wait_ge(S_("tok_evac"), m + 1)
                else:
                    pe.wait_ge(S_("conv"), 4 * (m - TOKU) + 4)

            def tok_unit(n):
                s, t = n // NT, n % NT
                w = SLABS[s][1]
                if t == 0:
                    pe.wait_ge(S_(f"slab_in{s % NSL}"), 16 * (s // NSL + 1))
                if s == 0:
                    pe.wait_ge(S_("ut_ready"), 2 * t + 2)
                bank_free(n)
                for k in range(KD):
                    last = mm(PA[n % 2][:, 0:w], UT[:, k, t * P:(t + 1) * P], SL[s % NSL][:, k, 0:w], k == 0, k == KD - 1)
                last.then_inc(S_("proj_ps"), 1)
                if t == NT - 1:
                    pe.transpose(TB[:, 0:P], ident[:, :], ident[:, :]).then_inc(S_("slab_used"), 1)

            u_transposes(0)
            for n in range(TOKU):
                if n < NT - 1:
                    u_transposes(n + 1)
                tok_unit(n)

            def conv_unit(i):
                n, s = TOKU + i, 5 + i // 2
                if i % 2 == 0:
                    pe.wait_ge(S_(f"slab_in{s % NSL}"), 16 * (s // NSL + 1))
                bank_free(n)
                for k in range(KD):
                    last = mm(PA[n % 2], SL[s % NSL][:, k, (i % 2) * P:(i % 2) * P + P], UT[:, k, :], k == 0, k == KD - 1)
                last.then_inc(S_("proj_ps"), 1)

            pe.wait_ge(S_("par_in"), 16 * 8)
            pe.transpose(XP[:, 0:48], CWR, ident[0:48, 0:48]).then_inc(S_("cw_ps"), 1)
            conv_unit(0)

            def qk_transposes(t):
                pe.wait_ge(S_("qkn"), 3 * t + 3)
                if t:
                    pe.wait_ge(S_("kt_ready"), t)
                q = QNB[t % 2]
                for h in range(4):
                    pe.transpose(TA[:, h * P:(h + 1) * P], q[:, h * P:(h + 1) * P], ident[:, :])
                pe.transpose(TB[:, 0:P], q[:, 512:640], ident[:, :]).then_inc(S_("qk_ps"), 1)
            qk_transposes(0)
            qk_transposes(1)
            pe.wait_ge(S_("kt_ready"), 2)
            pe.wait_ge(S_("avs_in"), 16 * 6)

            def headwise(bank, sem, l, r):
                for h in range(HD):
                    hs = slice(h * P, (h + 1) * P)
                    last = mm(bank[:, hs], l[:, hs], r[:, hs], True, True)
                last.then_inc(S_(sem), 1)

            def dt(c, i, n, ready, count):
                m = 4 * c + i
                pe.wait_ge(S_(ready), count)
                if m >= 2:
                    pe.wait_ge(S_("dt_ready"), m - 1)
                for h in range(HD):
                    last = pe.transpose(PS[4 + m % 2][:, h * P:(h + 1) * P], B[c][n][:, h * P:(h + 1) * P], ident[:, :])
                last.then_inc(S_("dt_ps"), 1)

            def li(c):
                pe.wait_ge(S_("dt_ready"), 4 * c + 3)
                if c:
                    pe.wait_ge(S_("li"), 2 * c)
                headwise(PS[2], "li_ps", B[c]["KHT"], B[c]["KBT"])
                headwise(PS[3], "li_ps", B[c]["KHT"], B[c]["QNT"])

            def prepare(c):
                if c:
                    pe.wait_ge(S_("dsub"), c)
                for h in range(HD):
                    last = mm(AO[:, h * P:(h + 1) * P], GV[:, 4 * c + h:4 * c + h + 1].to_broadcast([P, P]), TRIU, True, True)
                last.then_inc(S_("grow_ps"), 1)
                dt(c, 0, "KH", "kq_scaled", 3 * c + 1)
                dt(c, 1, "KB", "kq_scaled", 3 * c + 2)
                dt(c, 2, "QN", "kq_scaled", 3 * c + 3)
                if c:
                    li(c - 1)
                dt(c, 3, "QE", "qe_ready", c + 1)

            for i in range(CHU + 2):
                if i < CHU:
                    if i:
                        conv_unit(i)
                    if i % 2:
                        pe.transpose(TB[:, 0:P], ident[:, :], ident[:, :]).then_inc(S_("slab_used"), 1)
                if 2 <= i < NCH + 2:
                    n = i - 2
                    pe.wait_ge(S_("pt_ready"), n + 1)
                    if n:
                        pe.wait_ge(S_("att_out"), n)
                    else:
                        pe.wait_ge(S_("dn_vec"), 4)
                    k = P if n else CH
                    v = AQ[0:k, (n - 1) // 2 if n else 0, 640:768] if n % 2 or n == 0 else AVS[:, n // 2 - 1, :]
                    for kv in range(KV):
                        last = mm(AO[64 * kv:64 * kv + 64, 0:256], v[:, 64 * kv:64 * kv + 64], PT[0:k, 256 * kv:256 * kv + 256], True, True)
                    last.then_inc(S_("pv_ps"), 1)
                if i in (1, 2):
                    if i == 2:
                        pe.wait_ge(S_("pt_ready"), 1)
                    qk_transposes(i + 1)
                if i < NCH:
                    if i == 1:
                        pe.wait_ge(S_("tri"), 2)
                        pe.wait_ge(S_("ones"), 1)
                        pe.wait_ge(S_("dn_vec"), 3)
                        mm(AO[:, 0:16], TRIU, GV, True, True)
                        mm(AO[:, 16:32], ONES, GV, True, True).then_inc(S_("g_ps"), 1)
                    if i:
                        pe.wait_ge(S_("shifted"), i)
                    k0, k1 = (i - 1) * CH if i else 0, (i + 1) * CH
                    for kv in range(KV):
                        rows = slice(64 * kv, 64 * kv + 64)
                        for hp in range(2):
                            last = mm(PSC[:, kv, hp * P:hp * P + k1 - k0],
                                      QNT[rows, i, 2 * hp:2 * hp + 2, :].rearrange("p h q -> p (h q)"), KNT[rows, k0:k1], True, True)
                    last.then_inc(S_("sc_ps"), 1)
                if 1 <= i <= NCH:
                    n = i - 1
                    pe.wait_ge(S_("pnorm"), n + 1)
                    if n:
                        pe.wait_ge(S_("pt_ready"), n)
                    k = P if n else CH
                    if i in (1, 2):
                        pe.wait_ge(S_("kt_ready"), i + 2)
                    for g in range(4):
                        last = pe.transpose(TA[0:k, g * P:(g + 1) * P], PB[n % 2][:, g * P:g * P + k], ident[:, :])
                    last.then_inc(S_("pt_ps"), 1)
                if 2 <= i:
                    u = i - 2
                    pe.wait_ge(S_("silu"), u + 1)
                    if u:
                        pe.wait_ge(S_("tm_evac"), u)
                    else:
                        pe.wait_ge(S_("cw_evac"), 1)
                    for t in range(NT):
                        last = pe.transpose(XP[:, t * P:(t + 1) * P], ST[u % 2][:, t * P:(t + 1) * P], ident[:, :])
                    last.then_inc(S_("st_ps"), 1)
                if i == EARLY + 1:
                    pe.wait_ge(S_("att_out"), NCH)
                    prepare(0)
                if i == EARLY + 2:
                    prepare(1)
            for c in range(2, NT):
                prepare(c)
            li(NT - 1)
            def t0(c):
                pe.wait_ge(S_("u_init"), c + 1)
                if c >= 2:
                    pe.wait_ge(S_("t_ready"), c - 1)
                for h in range(HD):
                    hs = slice(h * P, (h + 1) * P)
                    last = pe.transpose(PS[c % 2][:, hs], B[c]["U"][:, hs], ident[:, :])
                last.then_inc(S_("t0_ps"), 1)

            t0(0)
            t0(1)
            pe.wait_ge(S_("dt_ready"), 4 * NT)
            pe.wait_ge(S_("dsub"), NT)
            STEPS = len(LEVELS) * NT
            for m in range(STEPS + 2):
                if m < STEPS:
                    b = B[m % NT]
                    pe.wait_ge(S_("ct"), m + 1)
                    if m >= NT:
                        pe.wait_ge(S_("t_upd"), m - NT + 1)
                    else:
                        pe.wait_ge(S_("t_ready"), m + 1)
                    for h in range(HD):
                        last = mm(compact(PS[4 + m % 2], m // NT)[:, h], b["CT"][:, h * P:(h + 1) * P], even(b["T"], m // NT)[:, h], True, True)
                    last.then_inc(S_("p1_ps"), 1)
                if 1 <= m <= STEPS:
                    n = m - 1
                    b = B[n % NT]
                    pe.wait_ge(S_("p1_ready"), n + 1)
                    if n >= NT:
                        pe.wait_ge(S_("u_upd"), n - NT + 1)
                    if n == 1:
                        pe.wait_ge(S_("t_ready"), 3)
                    for h in range(HD):
                        last = mm(PS[6 - 6 * (n % 2)][:, h * 64:h * 64 + 64], b["U"][:, h * P:(h + 1) * P], b["P1"][:, h * 64:h * 64 + 64], True, True)
                    last.then_inc(S_("p2_ps"), 1)
                if m < 2:
                    t0(m + 2)
                if m >= 2:
                    n = m - 2
                    pe.wait_ge(S_("t_upd"), n + 1)
                    if n >= 2:
                        pe.wait_ge(S_("u_upd"), n - 1)
                    if n == 1:
                        pe.wait_ge(S_("t_ready"), NT)
                    for h in range(HD):
                        hs = slice(h * P, (h + 1) * P)
                        last = pe.transpose(PS[7 - 6 * (n % 2)][:, hs], B[n % NT]["T"][:, hs], ident[:, :])
                    last.then_inc(S_("tt_ps"), 1)

            def uw(c):
                pe.wait_ge(S_("u_upd"), (len(LEVELS) - 1) * NT + c + 1)
                pe.wait_ge(S_("uw") if c else S_("li"), 2 * c if c else 2 * NT)
                pe.wait_ge(S_("vb_ready"), c + 1)
                headwise(PS[2], "uw_ps", B[c]["U"], B[c]["VB"])
                headwise(PS[3], "uw_ps", B[c]["KBEG"], B[c]["U"])

            def dcat(c):
                pe.wait_ge(S_("dn_out"), c + 1)
                if c >= 2:
                    pe.wait_ge(S_("dcat"), c - 1)
                for h in range(HD):
                    last = pe.transpose(PS[2 + c % 2][:, h * P:(h + 1) * P], OB[:, c, h * P:(h + 1) * P], ident[:, :])
                last.then_inc(S_("dcat_ps"), 1)

            early = [(half, k) for half in range(2) for k in range(4)]

            def early_outproj(count):
                for _ in range(count):
                    half, k = early.pop(0)
                    mm(PS[half], CAT[:, k, 0:P], WO0[:, k, half * 512:half * 512 + 512], k == 0, False)

            pe.wait_ge(S_("wo_in"), 16 * 3)
            uw(0)
            uw(1)
            pe.wait_ge(S_("u_upd"), len(LEVELS) * NT)
            for c in range(NT):
                b, state = B[c], STATES[c % 2]
                if c:
                    pe.wait_ge(S_("uw"), 2 * c + 2)
                    pe.wait_ge(S_("state"), c)
                    headwise(PS[7], "ws_ps", b["WT"], state)
                early_outproj(2 if c == 0 else 1)
                pe.wait_ge(S_("vnew"), c + 1)
                if c < NT - 1:
                    headwise(PS[5], "kv_ps", b["KTE"], b["VN"])
                if c >= 2:
                    pe.wait_ge(S_("o_evac"), c - 1)
                for h in range(HD):
                    hs = slice(h * P, (h + 1) * P)
                    o = PS[6 - 2 * (c % 2)][:, hs]
                    if c:
                        mm(o, b["QET"][:, hs], state[:, hs], True, False)
                    last = mm(o, b["INT"][:, hs], b["VN"][:, hs], c == 0, True)
                last.then_inc(S_("o_ps"), 1)
                if c + 2 < NT:
                    uw(c + 2)
            early_outproj(len(early))
            pe.wait_ge(S_("uw"), 2 * NT)
            dcat(0)

            def hn_transposes(t):
                pe.wait_ge(S_("hn_ready"), t + 1)
                pe.wait_ge(S_("dcat"), NT)
                for half in range(2):
                    if t:
                        pe.wait_ge(S_("hnt_ready"), 2 * t - 1 + half)
                    for j in range(4):
                        k = 4 * half + j
                        last = pe.transpose(PS[2 + half][:, j * P:(j + 1) * P], HN[t % 2][:, k * P:(k + 1) * P], ident[:, :])
                    last.then_inc(S_("hnt_ps"), 1)

            def logits(t):
                pe.wait_ge(S_("hnt_ready"), 2 * t + 2)
                if t:
                    pe.wait_ge(S_("logits"), t)
                for k in range(KD):
                    last = mm(PS[5][:, 0:NE], HNT[t % 2][:, k, :], RW[:, k, :], k == 0, k == KD - 1)
                last.then_inc(S_("lg_ps"), 1)

            def ranks(t):
                pe.wait_ge(S_("mask"), t + 1)
                pe.wait_ge(S_("consts"), 9)
                o = RANKS[t]
                for u in range(t):
                    mm(o, ONER, MASK[:, u, :], u == 0, False)
                mm(o, STRU, MASK[:, t, :], t == 0, True).then_inc(S_("rank_ps"), 1)

            for n in range(2 * NT):
                t, half = n // 2, n % 2
                if half == 0:
                    pe.wait_ge(S_("dcat"), t + 1)
                if n >= 2:
                    pe.wait_ge(S_("h_add"), n - 1)
                for k in range(0 if t else 4, KD):
                    w = WO0[:, k, :] if k < 4 else WO1[:, k - 4, :]
                    last = mm(PS[n % 2], CAT[:, k, t * P:(t + 1) * P], w[:, half * 512:half * 512 + 512], k == 0, k == KD - 1)
                last.then_inc(S_("outproj"), 1)
                if n < NT - 1:
                    dcat(n + 1)
                if half and t:
                    hn_transposes(t - 1)
                if half == 0 and t > 1:
                    if t == 2:
                        pe.wait_ge(S_("res_in"), 16 * (NT + 3))
                    logits(t - 2)
            logits(2)
            hn_transposes(3)
            ranks(0)
            ranks(1)
            pe.wait_ge(S_("h_add"), 2 * NT)
            ranks(2)
            pe.wait_ge(S_("hnt_ready"), 2 * NT)
            for o in (RANKS[NT - 1], PS[2][:, 0:NE]):
                for u in range(NT - 1):
                    mm(o, ONER, MASK[:, u, :], u == 0, False)
            logits(NT - 1)
            pe.wait_ge(S_("mask"), NT)
            mm(PS[2][:, 0:NE], ONER, MASK[:, NT - 1, :], False, True).then_inc(S_("count_ps"), 1)
            mm(RANKS[NT - 1], STRU, MASK[:, NT - 1, :], False, True).then_inc(S_("rank_ps"), 1)
            for i in range(4 * TOPK):
                t, k = i // TOPK, i % TOPK
                pe.wait_ge(S_("t1_ready"), i + 1)
                pe.wait_ge(S_("b1_ready"), t + 1)
                last = mm(PS[4][:, 0:MAXB + 1], T1[:, t, k, :], B1[:, t % NB1, k, :], i == 0, i == 4 * TOPK - 1)
                last.then_inc(S_("list_ps"), 1)
            pe.wait_ge(S_("gathered"), 16)

            def x_transposes(i):
                for half in range(2):
                    last = pe.transpose(XPS[:, half * P:(half + 1) * P], XG[:, half * P:(half + 1) * P], ident[:, :])
                last.then_inc(S_("xt_ps"), 1)

            def gate_up(i, p, rnd, first_of_expert, first):
                pe.wait_ge(S_("xt_ready"), i + 1)
                if not first:
                    pe.wait_ge(S_("gu_evac"), i)
                for k in range(KD):
                    if first_of_expert and k % 2 == 0:
                        pe.wait_ge(S_(f"gu_in{p}{k // 2}"), rnd)
                    if k == 5:
                        pe.wait_ge(S_("gathered"), (i + 2) * 16)
                        x_transposes(i + 1)
                        if not first:
                            pe.wait_ge(S_("act_ready"), i)
                            act_transposes()
                    for j in range(4):
                        rhs = GUW[p][:, k, :].rearrange("p (g n) -> p g n", g=2)[:, :, j * QW:(j + 1) * QW]
                        last = pe.matmul(GPS[32 * j:32 * j + 32, :].rearrange("p (g n) -> p g n", g=2),
                                         XT[:, (k % 2) * P + (k // 2) * 32:(k % 2) * P + (k // 2) * 32 + 32], rhs,
                                         start=(k == 0), stop=(k == KD - 1), tile_position=(0, 32 * j), skip_group_check=True)
                    if k % 2:
                        last.then_inc(S_(f"gu_read{k // 2}" if k < KD - 1 else "gu_ps"), 1)

            def act_transposes():
                for half in range(2):
                    last = pe.transpose(ATPS[:, half * P:(half + 1) * P], GU[:, half * P:(half + 1) * P], ident[:, :])
                last.then_inc(S_("at_ps"), 1)

            def down(i, p, rnd):
                pe.wait_ge(S_("at_ready"), i + 1)
                pe.wait_ge(S_("y_ready"), i + 1)
                if rnd is not None:
                    pe.wait_ge(S_(f"dn_in{p}0"), rnd)
                    pe.wait_ge(S_(f"dn_in{p}1"), rnd)
                for k in range(KD):
                    for j in range(4):
                        last = pe.matmul(DPS[32 * j:32 * j + 32, :],
                                         AT[:, (k % 2) * P + (k // 2) * 32:(k % 2) * P + (k // 2) * 32 + 32],
                                         DNW[p][:, k, j * QW:(j + 1) * QW],
                                         start=(k == 0), stop=(k == KD - 1), tile_position=(0, 32 * j), skip_group_check=True)
                    if k == KD // 2 - 1:
                        last.then_inc(S_("dn_read"), 1)
                last.then_inc(S_("d_ps"), 1)

            def more_blocks(e, p, before, rnd):
                last = pe.value_load(LASTB[0:1, bass.ds(e, 1)], min_val=0, max_val=MAXB - 1)
                with pe.If(last > before + 1):
                    with pe.Fori(before + 2, last + 1) as i:
                        gate_up(i, p, rnd, False, False)
                        down(i - 1, p, rnd)
                return last

            def expert(e, p, before, rnd, prnd):
                gate_up(before + 1, p, rnd, True, False)
                down(before, 1 - p, prnd)
                return more_blocks(e, p, before, rnd)

            pe.transpose(RPS, ident[:, :], ident[:, :]).then_inc(S_("d_ps"), 1)
            x_transposes(0)
            gate_up(0, 0, 16, True, True)
            last = pe.value_load(LASTB[0:1, 0:1], min_val=0, max_val=MAXB - 1)
            with pe.If(last > 0):
                gate_up(1, 0, 16, False, False)
                down(0, 0, 16)
            with pe.If(last > 1):
                with pe.Fori(2, last + 1) as i:
                    gate_up(i, 0, 16, False, False)
                    down(i - 1, 0, 16)

            with pe.Fori(0, NE // 2 - 1) as r:
                last = pe.value_load(LASTB[0:1, bass.ds(2 * r, 1)], min_val=0, max_val=MAXB - 1)
                last = expert(2 * r + 1, 1, last, (r + 1) * 16, (r + 1) * 16)
                expert(2 * r + 2, 0, last, (r + 2) * 16, (r + 1) * 16)
            last = pe.value_load(LASTB[0:1, NE - 2:NE - 1], min_val=0, max_val=MAXB - 1)
            last = expert(NE - 1, 1, last, NE * 8, NE * 8)
            pe.wait_ge(S_("act_ready"), last + 1)
            act_transposes()
            down(last, 1, NE * 8)

        @block.vector
        def _(v):
            stt, tt, ts = v.scalar_tensor_tensor, v.tensor_tensor, v.tensor_scalar
            chain = [0]

            def link(ins):
                chain[0] += 1
                ins.then_inc(S_("v_chain"), 1)
                v.wait_ge(S_("v_chain"), chain[0])

            v.wait_ge(S_("nw_in"), 16)
            for t in range(NT):
                r = RSX[:, t:t + 1]
                v.wait_ge(S_("ssx"), t + 1)
                ts(SSX[:, t:t + 1], SSX[:, t:t + 1], 1.0 / D, EPS, ALU.mult, ALU.add).then_inc(S_("meansq"), 1)
                v.wait_ge(S_("sqrt"), t + 1)
                link(v.reciprocal(r, r))
                stt(out=X[:, t, :], in0=X[:, t, :], scalar=RSX[:, t:t + 1], in1=NW, op0=ALU.mult, op1=ALU.mult).then_inc(S_("u_ready"), 1)
            v.wait_ge(S_("par_in"), 16 * 8)
            link(stt(out=KWT, in0=KWT, scalar=DH ** -0.5, in1=SIG[:, 0:64], op0=ALU.mult, op1=ALU.mult))
            for t in range(NT):
                v.wait_ge(S_("tok_evac"), 2 * NT + t + 1)
                link(tt(SQA, AQ[:, t, 0:640], AQ[:, t, 0:640], ALU.mult))
                link(v.tensor_reduce(SSA[:, 10 * t:10 * t + 10], SQA.rearrange("p (h n) -> p h n", h=10), AX.X, ALU.add))
            ts(SSA, SSA, 1.0 / DH, EPS, ALU.mult, ALU.add).then_inc(S_("meansq"), 1)
            v.wait_ge(S_("sqrt"), NT + 1)
            link(v.reciprocal(RNA, RNA))

            def qk_normed(t):
                if t >= 2:
                    v.wait_ge(S_("qk_ps"), t - 1)
                q = QNB[t % 2]
                tt(q[:, 0:512].rearrange("p (h g d) -> p g h d", h=4, g=2),
                   AQ[:, t, 0:512].rearrange("p (g h d) -> p g h d", g=2, h=4),
                   RNA[:, 10 * t:10 * t + 8].rearrange("p (g h o) -> p g h o", g=2, o=1).to_broadcast([P, 2, 4, 64]), ALU.mult).then_inc(S_("qkn"), 1)
                k = q[:, 512:640].rearrange("p (g d) -> p g d", g=2)
                tt(k, AQ[:, t, 512:640].rearrange("p (g d) -> p g d", g=2), bc(RNA[:, 10 * t + 8:10 * t + 10], 64), ALU.mult).then_inc(S_("qkn"), 1)
                v.wait_ge(S_("qkn"), 3 * t + 2)
                tt(k, k, bm(KWT, 2), ALU.mult).then_inc(S_("qkn"), 1)

            qk_normed(0)
            qk_normed(1)
            for t in range(NT):
                v.wait_ge(S_("z_sig"), t + 1)
                tt(DZ[:, t, 0:512], DZ[:, t, 0:512], SGZ[t % 2], ALU.mult).then_inc(S_("z_done"), 1)
            v.wait_ge(S_("z_done"), NT)
            for t in range(NT):
                tt(h4(DZ[:, t, 0:512]), h4(DZ[:, t, 0:512]), bm(ZNW, HD), ALU.mult).then_inc(S_("zw"), 1)

            link(tt(SPT.rearrange("p (t h) -> p t h", t=NT), DZ[:, :, 516:520], bm(DTB, NT), ALU.add))
            link(ts(SPM, SPT, -1.0, None, ALU.mult))
            tt(SPM, SPM, SPT, ALU.min).then_inc(S_("dn_vec"), 1)
            v.wait_ge(S_("dn_vec"), 1)
            link(ts(SPT, SPT, 0.0, None, ALU.max))
            v.wait_ge(S_("dn_act"), 2)
            ts(SPM, SPM, 1.0, None, ALU.add).then_inc(S_("dn_vec"), 1)
            v.wait_ge(S_("dn_act"), 4)
            link(tt(SPT, SPT, SPM, ALU.add))
            v.wait_ge(S_("dn_act"), 3)
            link(ts(AL, AL, -1.0, None, ALU.mult))
            tt(GV.rearrange("p (t h) -> p t h", t=NT), SPT.rearrange("p (t h) -> p t h", t=NT), bm(AL, NT), ALU.mult).then_inc(S_("dn_vec"), 1)
            v.wait_ge(S_("cw_ps"), 1)
            v.tensor_copy(CW, XP[:, 0:48]).then_inc(S_("cw_evac"), 1)
            v.wait_ge(S_("cw_evac"), 1)
            qk_normed(2)
            qk_normed(3)

            def taps(i):
                n = TOKU + i
                v.wait_ge(S_("proj_ps"), n + 1)
                if i >= 2:
                    v.wait_ge(S_("sig"), i - 1)
                    v.wait_ge(S_("silu"), i - 1)
                src, cv = PA[n % 2], CV[i % 2]
                ts(cv, src, CW[:, 36 + i:37 + i], None, ALU.mult).then_inc(S_("conv"), 1)
                for j in range(1, 4):
                    v.wait_ge(S_("conv"), 4 * i + j)
                    col = (3 - j) * 12 + i
                    stt(out=cv[:, j:S], in0=src[:, 0:S - j], scalar=CW[:, col:col + 1], in1=cv[:, j:S],
                        op0=ALU.mult, op1=ALU.add).then_inc(S_("conv"), 1)

            def silu(i):
                v.wait_ge(S_("sig"), i + 1)
                if i >= 2:
                    v.wait_ge(S_("st_ps"), i - 1)
                tt(ST[i % 2], CV[i % 2], SG[i % 2], ALU.mult).then_inc(S_("silu"), 1)

            def softmax_a(n):
                w = P if n else CH
                v.wait_ge(S_("sc_ps"), n + 1)
                if n >= 2:
                    v.wait_ge(S_("pt_ps"), n - 1)
                if n:
                    v.wait_ge(S_("shifted"), n)
                sc = PSC[:, :, 0:256].rearrange("p k (h n) -> p k h n", h=2)[:, :, :, 0:w]
                link(v.tensor_reduce(MXS.rearrange("p (k h) -> p k h", k=2), sc, AX.X, ALU.max))
                link(tt(MXS, MXS, SKT, ALU.max))
                link(tt(MNEG, SKT, MXS, ALU.subtract))
                pb = PB[n % 2].rearrange("p (k h n) -> p k h n", k=2, h=2)[:, :, :, 0:w]
                tt(pb, sc, MXS.rearrange("p (k h o) -> p k h o", k=2, o=1).to_broadcast([P, 2, 2, w]), ALU.subtract).then_inc(S_("shifted"), 1)

            def softmax_b(n):
                w = P if n else CH
                pb = PB[n % 2].rearrange("p (g n) -> p g n", g=4)[:, :, 0:w]
                v.wait_ge(S_("exps_done"), 2 * n + 1)
                if n:
                    v.wait_ge(S_("pnorm"), n)
                link(v.tensor_reduce(DEN, pb, AX.X, ALU.add))
                v.wait_ge(S_("exps_done"), 2 * (n + 1))
                link(tt(DEN, DEN, ESK, ALU.add))
                link(v.reciprocal(RDEN, DEN))
                tt(pb, pb, bc(RDEN, w), ALU.mult).then_inc(S_("pnorm"), 1)

            def scaled(c):
                b = B[c]
                hs = slice(4 * c, 4 * c + 4)
                tt(h4(b["KH"]), KTM[:, c, :, :], bc(RSQ[:, 8 * c + 4:8 * c + 8], P), ALU.mult).then_inc(S_("kq_scaled"), 1)
                v.wait_ge(S_("kq_scaled"), 3 * c + 1)
                tt(h4(b["KB"]), h4(b["KH"]), bc(BETA[:, hs], P), ALU.mult).then_inc(S_("kq_scaled"), 1)
                tt(h4(b["QN"]), QTM[:, c, :, :], bc(RSQ[:, 8 * c:8 * c + 4], P), ALU.mult).then_inc(S_("kq_scaled"), 1)
                v.wait_ge(S_("grow_ps"), c + 1)
                link(tt(h4(b["DEC"]), h4(AO), bc(GC[:, hs], P), ALU.subtract))
                tt(h4(b["DEC"]), h4(b["DEC"]), bm(NEGM, HD), ALU.add).then_inc(S_("dsub"), 1)

            def decayed(c):
                b = B[c]
                v.wait_ge(S_("decay"), c + 1)
                v.wait_ge(S_("li_ps"), 2 * c + 1)
                tt(b["LT"], PS[2], b["DEC"], ALU.mult).then_inc(S_("li"), 1)
                v.wait_ge(S_("li_ps"), 2 * c + 2)
                v.wait_ge(S_("scaled_pool"), c + 1)
                tt(b["INT"], PS[3], b["DEC"], ALU.mult).then_inc(S_("li"), 1)
                v.wait_ge(S_("li"), 2 * c + 1)
                link(tt(h4(b["CT"]), h4(b["LT"]), bm(MSK[0], HD), ALU.mult))
                tt(h4(b["U"]), bm(ident[:, :], HD), h4(b["CT"]), ALU.subtract).then_inc(S_("u_init"), 1)
                v.wait_ge(S_("u_init"), c + 1)
                tt(h4(b["CT"]), h4(b["LT"]), bm(MSK[1], HD), ALU.mult).then_inc(S_("ct"), 1)

            for i in range(CHU + 1):
                if i < CHU:
                    taps(i)
                if i < NCH:
                    softmax_a(i)
                if i >= 1:
                    silu(i - 1)
                if i < NCH:
                    softmax_b(i)
                if i == 1:
                    v.wait_ge(S_("g_ps"), 1)
                    link(v.tensor_copy(GC, AO[:, 0:16]))
                    v.tensor_copy(GLC, AO[:, 16:32]).then_inc(S_("dn_vec"), 1)
                    v.wait_ge(S_("dn_vec"), 4)
                    tt(EGD, GLC, GC, ALU.subtract).then_inc(S_("dn_vec"), 1)
                for n in NORM_AT.get(i, ()):
                    at = 8 * (n % NT) + 4 * (n // NT)
                    v.wait_ge(S_("sq_done"), n + 1)
                    v.tensor_reduce(SSQ[:, at:at + 4], h4(SQD[n % 2]), AX.X, ALU.add).then_inc(S_("ssq"), 1)
                if i == EARLY - 1:
                    v.wait_ge(S_("ssq"), 8)
                    ts(SSQ, SSQ, EPS, None, ALU.add).then_inc(S_("meansq"), 1)
                if i == EARLY:
                    v.wait_ge(S_("sqrt"), NT + 2)
                    link(v.reciprocal(RSQ, RSQ))
                    link(ts(RSQ.rearrange("p (c s h) -> p c s h", c=NT, s=2)[:, :, 0, :], RSQ.rearrange("p (c s h) -> p c s h", c=NT, s=2)[:, :, 0, :],
                            float(P) ** -0.5, None, ALU.mult))
                    v.wait_ge(S_("dn_act"), 1)
                    v.wait_ge(S_("att_out"), NCH)
                    v.wait_ge(S_("tri"), 2)
                    v.wait_ge(S_("p_b"), 28)
                    scaled(0)
                if i == EARLY + 1:
                    scaled(1)
            v.wait_ge(S_("tm_evac"), CHU)

            scaled(2)
            decayed(0)
            scaled(3)
            for c in range(1, NT):
                decayed(c)
            for m in range(len(LEVELS) * NT):
                b, lv = B[m % NT], m // NT
                v.wait_ge(S_("p2_ps"), m + 1)
                tt(even(b["T"], lv), even(b["T"], lv), compact(PS[6 - 6 * (m % 2)], lv), ALU.subtract).then_inc(S_("t_upd"), 1)
                if lv < len(LEVELS) - 1:
                    tt(h4(b["CT"]), h4(b["LT"]), bm(MSK[lv + 2], HD), ALU.mult).then_inc(S_("ct"), 1)
            v.wait_ge(S_("dn_act"), 7)
            v.wait_ge(S_("zw"), NT)
            for i in range(NT + 2):
                if i < NT:
                    b, old, new = B[i], STATES[i % 2], STATES[(i + 1) % 2]
                    v.wait_ge(S_("uw"), 2 * i + 1)
                    if i:
                        v.wait_ge(S_("ws_ps"), i)
                        tt(b["VN"], b["USOL"], PS[7], ALU.subtract).then_inc(S_("vnew"), 1)
                    else:
                        v.tensor_copy(b["VN"], b["USOL"]).then_inc(S_("vnew"), 1)
                    if 0 < i < NT - 1:
                        v.wait_ge(S_("o_ps"), i)
                        v.wait_ge(S_("state"), i)
                        link(tt(h4(new), h4(old), bc(EGL[:, 4 * i:4 * i + 4], P), ALU.mult))
                        v.wait_ge(S_("kv_ps"), i + 1)
                        tt(new, new, PS[5], ALU.add).then_inc(S_("state"), 1)
                    if i == 0:
                        v.wait_ge(S_("kv_ps"), 1)
                        v.tensor_copy(new, PS[5]).then_inc(S_("state"), 1)
                if 1 <= i <= NT:
                    c = i - 1
                    v.wait_ge(S_("sq_done"), 8 + c + 1)
                    v.tensor_reduce(SSO[:, 4 * c:4 * c + 4], h4(B[c]["LT"]), AX.X, ALU.add).then_inc(S_("ssq"), 1)
                    v.wait_ge(S_("ssq"), 8 + c + 1)
                    ts(SSO[:, 4 * c:4 * c + 4], SSO[:, 4 * c:4 * c + 4], 1.0 / P, EPS, ALU.mult, ALU.add).then_inc(S_("meansq"), 1)
                if i >= 2:
                    c = i - 2
                    v.wait_ge(S_("sqrt"), NT + 3 + c)
                    link(v.reciprocal(RSO[:, 4 * c:4 * c + 4], RSO[:, 4 * c:4 * c + 4]))
                    link(tt(h4(OB[:, c, :]), h4(OB[:, c, :]), bc(RSO[:, 4 * c:4 * c + 4], P), ALU.mult))
                    tt(OB[:, c, :], OB[:, c, :], DZ[:, c, 0:512], ALU.mult).then_inc(S_("dn_out"), 1)
            v.wait_ge(S_("res_in"), 16 * (NT + 3))

            def top4(t):
                v.wait_ge(S_("lg_ps"), t + 1)
                tt(LG[:, t, :], PS[5][:, 0:NE], RB, ALU.add).then_inc(S_("logits"), 1)
                v.wait_ge(S_("logits"), t + 1)
                link(v.max(MX8[:, t, :], LG[:, t, :]))
                link(v.max_index(MI8[:, t, :], MX8[:, t, :], LG[:, t, :]))
                link(v.tensor_copy(MIF[:, t, :], MI8[:, t, :]))
                ts(GATE[:, 4 * t:4 * t + 4], MX8[:, t, 0:4], MX8[:, t, 0:1], None, ALU.subtract).then_inc(S_("v_gate"), 1)
                v.wait_ge(S_("consts"), 9)
                link(tt(OH[:, t], bm(IO32, TOPK), bc(MIF[:, t, 0:TOPK], NE), ALU.is_equal))
                v.tensor_reduce(MASK[:, t, :], OH[:, t].rearrange("p k e -> p e k"), AX.X, ALU.add).then_inc(S_("mask"), 1)

            def positions(t):
                r = slice(4 * t, 4 * t + 4)
                v.wait_ge(S_("rank_ps"), t + 1)
                v.wait_ge(S_("mask"), t + 1)
                link(tt(OHR, OH[:, t], bm(RANKS[t], TOPK), ALU.mult))
                link(v.tensor_reduce(RK[:, r], OHR, AX.X, ALU.add))
                link(v.tensor_copy(RKI[:, r], RK[:, r]))
                link(ts(RKI[:, r], RKI[:, r], 5, None, ALU.logical_shift_right))
                link(v.tensor_copy(RKB[:, r], RKI[:, r]))
                stt(out=TPOS[:, r], in0=RKB[:, r], scalar=-float(BT), in1=RK[:, r], op0=ALU.mult, op1=ALU.add).then_inc(S_("tpos"), 1)

            for t in range(NT):
                for half in range(2):
                    v.wait_ge(S_("outproj"), 2 * t + half + 1)
                    hh = H[t][:, half * 512:half * 512 + 512]
                    tt(hh, hh, PS[half], ALU.add).then_inc(S_("h_add"), 1)
                v.wait_ge(S_("h_add"), 2 * t + 2)
                v.wait_ge(S_("ssh"), t + 1)
                ts(SSH[:, t:t + 1], SSH[:, t:t + 1], 1.0 / D, EPS, ALU.mult, ALU.add).then_inc(S_("meansq"), 1)
                v.wait_ge(S_("sqrt"), 2 * NT + 3 + t)
                link(v.reciprocal(RSH[:, t:t + 1], RSH[:, t:t + 1]))
                stt(out=HN[t % 2], in0=H[t], scalar=RSH[:, t:t + 1], in1=FW, op0=ALU.mult, op1=ALU.mult).then_inc(S_("hn_ready"), 1)
                if t >= 2:
                    top4(t - 2)
            top4(2)
            positions(0)
            positions(1)
            v.wait_ge(S_("consts"), 9)
            link(ts(PJI, PJI, 5, None, ALU.logical_shift_right))
            link(v.tensor_copy(PJ, PJI))
            positions(2)
            top4(3)
            v.wait_ge(S_("count_ps"), 1)
            link(ts(NBI, PS[2][:, 0:NE], float(BT - 1), None, ALU.add))
            link(ts(NBI, NBI, 5, None, ALU.logical_shift_right))
            link(ts(NBF, NBI, 1.0, None, ALU.max))
            link(v.tensor_tensor_scan(BEF, ONE32, NBF, 0.0, ALU.mult, ALU.add))
            link(tt(BSF, BEF, NBF, ALU.subtract))
            positions(3)
            link(tt(OHB, OH.rearrange("p t k e -> p (t k) e"), bm(BSF, 4 * TOPK), ALU.mult))
            link(v.tensor_reduce(BSK, OHB, AX.X, ALU.add))
            link(tt(BLK, BSK, RKB, ALU.add))
            for t in range(NT):
                if t >= NB1:
                    v.wait_ge(S_("list_ps"), TOPK * (t - NB1 + 1))
                tt(B1[:, t % NB1], bm(IOB, TOPK), bc(BLK[:, 4 * t:4 * t + 4], MAXB + 1), ALU.is_equal).then_inc(S_("b1_ready"), 1)
            v.wait_ge(S_("tpos"), NT)
            link(ts(LASTB[:, :], BEF, -1.0, None, ALU.add))
            v.wait_ge(S_("list_ps"), 4 * TOPK)
            ts(IDX[:, :], PS[4][:, 0:MAXB + 1], PJ, None, ALU.add).then_inc(S_("lists_done"), 1)
            v.wait_ge(S_("gexp"), 1)
            link(v.tensor_reduce(GSUM, GATE[:, :].rearrange("p (t k) -> p t k", t=NT), AX.X, ALU.add))
            link(v.reciprocal(GREC, GSUM))
            link(tt(GATE[:, :].rearrange("p (t k) -> p t k", t=NT), GATE[:, :].rearrange("p (t k) -> p t k", t=NT), bc(GREC, TOPK), ALU.mult))
            tk = lambda w: w.rearrange("p (t k) -> p t k", t=NT)
            link(ts(tk(M31), MIF[:, :, 0:TOPK], float(NE - 1), None, ALU.is_equal))
            link(stt(out=SLF, in0=BSK, scalar=float(BT), in1=RK, op0=ALU.mult, op1=ALU.add))
            link(ts(SLT, SLF, -1.0, float(Y_ZERO), ALU.mult, ALU.add))
            link(tt(SLT, SLT, M31, ALU.mult))
            link(tt(SLOT[:, :], SLF, SLT, ALU.add))
            link(ts(C31, BSF[:, NE - 1:NE], -float(BT), -float(YL_ZERO), ALU.mult, ALU.add))
            link(ts(SLF, SLF, C31, None, ALU.add))
            link(tt(SLF, SLF, M31, ALU.mult))
            link(v.tensor_reduce(SLS, tk(SLF), AX.X, ALU.add))
            link(ts(SLOTL[:, :], SLS, float(YL_ZERO), None, ALU.add))
            link(tt(SLT, GATE[:, :], M31, ALU.mult))
            v.tensor_reduce(GATEL, tk(SLT), AX.X, ALU.add).then_inc(S_("lists_done"), 1)
            v.wait_ge(S_("lists_done"), 1)

            def activate(i, p, first):
                v.wait_ge(S_("gu_ps"), i + 1)
                if not first:
                    v.wait_ge(S_("at_ps"), i)
                tt(GU[:, :], GPS, BGU[p][:, :], ALU.add).then_inc(S_("gu_evac"), 1)
                v.wait_ge(S_("gu_evac"), i + 1)
                ts(GU[:, 0:QW], GU[:, 0:QW], LIMIT, None, ALU.min).then_inc(S_("gate_ready"), 1)
                ts(GU[:, QW:2 * QW], GU[:, QW:2 * QW], LIMIT, -LIMIT, ALU.min, ALU.max)
                v.wait_ge(S_("sig_ready"), i + 1)
                tt(SIG[:, :], SIG[:, :], GU[:, 0:QW], ALU.mult).then_inc(S_("glu"), 1)
                v.wait_ge(S_("glu"), i + 1)
                stt(out=GU[:, 0:QW], in0=GU[:, QW:2 * QW], scalar=1.0, in1=SIG[:, :], op0=ALU.add, op1=ALU.mult).then_inc(S_("act_ready"), 1)

            def spread_biases(e, p, rnd):
                v.wait_ge(S_(f"bias_in{p}"), rnd)
                v.sem_inc(S_("bias_passed"), 1)
                v.stream_shuffle(BGU[p][:, :], BGU[p][:, :], [0] * 32).then_inc(S_("bias_spread"), 1)
                v.stream_shuffle(BDN[p][:, :], BDN[p][:, :], [0] * 32).then_inc(S_("bias_spread"), 1)
                v.wait_ge(S_("bias_spread"), 2 * (e + 1))

            def y_evac(i, p):
                v.wait_ge(S_("d_ps"), i + 2)
                v.wait_ge(S_("y_out"), (i + 1) * 16)
                tt(Y[:, :], DPS, BDN[p][:, :], ALU.add).then_inc(S_("y_ready"), 1)

            v.memset(IDXC[:, 1:2], 0).then_inc(S_("y_ready"), 1)
            spread_biases(0, 0, 32)
            activate(0, 0, True)
            last = v.value_load(LASTB[0:1, 0:1], min_val=0, max_val=MAXB - 1)
            with v.If(last > 0):
                activate(1, 0, False)
                y_evac(0, 0)
            with v.If(last > 1):
                with v.Fori(2, last + 1) as i:
                    activate(i, 0, False)
                    y_evac(i - 1, 0)

            def expert(e, p, before, brnd):
                spread_biases(e, p, brnd)
                activate(before + 1, p, False)
                y_evac(before, 1 - p)
                v.memset(IDXC[:, 1:2], 0).then_inc(S_("y_free"), 1)
                last = v.value_load(LASTB[0:1, bass.ds(e, 1)], min_val=0, max_val=MAXB - 1)
                with v.If(last > before + 1):
                    with v.Fori(before + 2, last + 1) as i:
                        activate(i, p, False)
                        y_evac(i - 1, p)
                return last

            with v.Fori(0, NE // 2 - 1) as r:
                last = v.value_load(LASTB[0:1, bass.ds(2 * r, 1)], min_val=0, max_val=MAXB - 1)
                last = expert(2 * r + 1, 1, last, (r + 1) * 32)
                expert(2 * r + 2, 0, last, (r + 2) * 32)

            def sum_others(t):
                v.wait_ge(S_("hf_in"), 16 * NT)
                v.wait_ge(S_(f"yg_in{t}"), 16 * TOPK)
                for k in range(TOPK):
                    i = TOPK * t + k
                    if i:
                        v.wait_ge(S_("partial"), i)
                    stt(out=HF[:, t, :], in0=YG[:, i, :], scalar=GATE[:, i:i + 1], in1=HF[:, t, :],
                        op0=ALU.mult, op1=ALU.add).then_inc(S_("partial"), 1)

            f = v.value_load(LASTB[0:1, NE - 2:NE - 1], min_val=0, max_val=MAXB - 1) + 1
            last = v.value_load(LASTB[0:1, NE - 1:NE], min_val=0, max_val=MAXB - 1)
            spread_biases(NE - 1, 1, NE * 16)
            activate(f, 1, False)
            y_evac(f - 1, 0)
            for t in range(NT):
                with v.If(last > f + t):
                    activate(f + t + 1, 1, False)
                if t == 0:
                    y_evac(f, 1)
                else:
                    with v.If(last > f + t - 1):
                        y_evac(f + t, 1)
                if t == NT - 1:
                    with v.If(last > f + NT):
                        with v.Fori(f + NT + 1, last + 1) as i:
                            activate(i, 1, False)
                            y_evac(i - 1, 1)
                    with v.If(last > f + NT - 1):
                        y_evac(last, 1)
                sum_others(t)
            for t in range(NT):
                v.wait_ge(S_(f"yg_in{t}"), 16 * TOPK + 16)
                v.wait_ge(S_("partial"), 4 * TOPK)
                stt(out=HF[:, t, :], in0=YGL[:, t, :], scalar=GATEL[:, t:t + 1], in1=HF[:, t, :], op0=ALU.mult, op1=ALU.add).then_inc(S_("summed"), 1)


_INS = ["x", "norm_mix_w", "w_in", "attn_q_norm_w", "attn_k_norm_w", "attn_sinks", "dn_conv_w", "dn_a_log", "dn_dt_bias",
        "dn_out_norm_w", "w_out", "norm_ffn_w", "router_w", "router_b", "expert_w_gate_up", "expert_b_gate_up",
        "expert_w_down", "expert_b_down"]


def kernel(**inputs):
    import numpy as _np
    import concourse.bacc as _bacc
    from concourse import mybir as _mybir
    from concourse.bass_utils import run_bass_kernel_spmd as _run

    nc = _bacc.Bacc("TRN2", target_bir_lowering=False, num_devices=1)
    arrays, args = {}, []
    for name in _INS:
        a = _np.ascontiguousarray(inputs[name])[0]
        arrays[f"in_{name}"] = a
        args.append(nc.dram_tensor(f"in_{name}", a.shape, _mybir.dt.from_np(a.dtype), kind="ExternalInput").ap())
    out = nc.dram_tensor("out_0", (S, D), _mybir.dt.float32, kind="ExternalOutput").ap()
    hybrid_block(nc, *args, out)
    r = _run(nc, [arrays], core_ids=[0])
    return r.results[0]["out_0"].reshape(1, S, D)
```
